# Optimizing a Trainium2 kernel written in Bass

```python
import math
import jax
import jax.numpy as jnp
from jax import lax
import numpy as np

D_MODEL = 1024
BATCH = 1
SEQ = 256
DEPTH = 2

GRID_W = 64
CTX_LEN = 256
EPS = 1e-6
A_WIDTH = 512
A_CONV = 3
B_HEADS = 4
B_DK = 128
B_DV = 128
B_CONV = 3
B_CHUNK = 64
B_QK = B_HEADS * B_DK
B_VW = B_HEADS * B_DV
IN_EVEN = 3 * A_WIDTH + 2 * B_QK + 2 * B_VW + 4 * B_HEADS
MIX_EVEN = A_WIDTH + B_VW
C_HEADS = 8
C_Q_LORA = 384
C_KV_LORA = 256
C_NOPE = 128
C_ROPE = 64
C_VDIM = 128
C_QBLOCK = 128
IN_ODD = C_Q_LORA + C_KV_LORA + C_ROPE
MIX_ODD = C_HEADS * C_VDIM
ROPE_BASE = 10000.0
P_HEADS = 8
P_NKEYS = 128
P_NEXP = P_NKEYS * P_NKEYS
P_DKEY = 128
P_TOPK = 16
P_BLOCK = 128
N_EVEN = (DEPTH + 1) // 2
N_ODD = DEPTH // 2

kernel_name = 'hybrid_conv_deltanet_mla_peer_dit'

def rms_norm(x, gain):
    xf = x.astype(jnp.float32)
    y = xf * lax.rsqrt(jnp.mean(xf * xf, axis=-1, keepdims=True) + EPS)
    return (y * gain.astype(jnp.float32)).astype(x.dtype)

def modulate(h, shift, scale):
    return h * (1 + scale[..., None, :]) + shift[..., None, :]

def dwconv_centred(x, w):
    p = w.shape[0] // 2
    return lax.conv_general_dilated(x, w[:, None, :].astype(x.dtype), window_strides=(1,), padding=[(p, p)],
                                    dimension_numbers=('NWC', 'WIO', 'NWC'), feature_group_count=x.shape[-1])

def l2_normalize(t):
    return t * lax.rsqrt(jnp.sum(t * t, axis=-1, keepdims=True) + EPS)

def gdn_chunked(q, k, v, g, beta, s0):
    Bn, H, L, dk = q.shape
    dv = v.shape[-1]
    n = L // B_CHUNK
    q = q * (dk ** -0.5)
    rs = lambda t: t.reshape((Bn, H, n, B_CHUNK) + t.shape[3:])
    q, k, v, g, beta = rs(q), rs(k), rs(v), rs(g), rs(beta)
    decay = jnp.cumsum(g, axis=-1)
    tri = jnp.tril(jnp.ones((B_CHUNK, B_CHUNK), bool))
    strict = jnp.tril(jnp.ones((B_CHUNK, B_CHUNK), bool), -1)
    gamma = jnp.exp(jnp.where(tri, decay[..., :, None] - decay[..., None, :], -jnp.inf))
    kb = k * beta[..., None]
    a = jnp.where(strict, jnp.einsum('bhncd,bhnmd->bhncm', kb, k) * gamma, 0.0)
    eye = jnp.eye(B_CHUNK, dtype=jnp.float32)
    rhs = jnp.concatenate([v * beta[..., None], kb * jnp.exp(decay)[..., None]], axis=-1)
    sol = lax.linalg.triangular_solve(eye + a, rhs, left_side=True, lower=True)
    u, w = sol[..., :dv], sol[..., dv:]
    intra = jnp.where(tri, jnp.einsum('bhncd,bhnmd->bhncm', q, k) * gamma, 0.0)
    q_dec = q * jnp.exp(decay)[..., None]
    k_dec = k * jnp.exp(decay[..., -1:] - decay)[..., None]
    last = jnp.exp(decay[..., -1])

    def step(s, inp):
        u_c, w_c, qd_c, kd_c, intra_c, last_c = inp
        v_new = u_c - jnp.einsum('bhck,bhkv->bhcv', w_c, s)
        o = jnp.einsum('bhck,bhkv->bhcv', qd_c, s) + jnp.einsum('bhcm,bhmv->bhcv', intra_c, v_new)
        s = s * last_c[..., None, None] + jnp.einsum('bhck,bhcv->bhkv', kd_c, v_new)
        return s, o

    xs = tuple(jnp.moveaxis(t, 2, 0) for t in (u, w, q_dec, k_dec, intra, last))
    s_fin, o = lax.scan(step, s0, xs)
    o = jnp.moveaxis(o, 0, 2).reshape(Bn, H, L, dv)
    return o, s_fin

def even_mixer(h, w_in, a_conv, qkv_conv, a_log, dt_bias, o_norm, w_out, s0_f, s0_b):
    Bn, L, _ = h.shape
    proj = h @ w_in
    bg, cg, xa, qkv, z, ab = jnp.split(
        proj, [A_WIDTH, 2 * A_WIDTH, 3 * A_WIDTH, 3 * A_WIDTH + 2 * B_QK + B_VW, 3 * A_WIDTH + 2 * B_QK + 2 * B_VW], axis=-1)
    y_a = bg * dwconv_centred(cg * xa, a_conv)
    qkv = jax.nn.silu(dwconv_centred(qkv, qkv_conv)).astype(jnp.float32)
    q, k, v = jnp.split(qkv, [B_QK, 2 * B_QK], axis=-1)
    heads = lambda t, d: t.reshape(Bn, L, B_HEADS, d).transpose(0, 2, 1, 3)
    q = l2_normalize(heads(q, B_DK))
    k = l2_normalize(heads(k, B_DK))
    v = heads(v, B_DV)
    ab4 = ab.reshape(Bn, L, 4, B_HEADS).transpose(2, 0, 3, 1).astype(jnp.float32)
    a_log = a_log.astype(jnp.float32)
    dt_bias = dt_bias.astype(jnp.float32)
    g_f = -jnp.exp(a_log[0])[None, :, None] * jax.nn.softplus(ab4[0] + dt_bias[0][None, :, None])
    g_b = -jnp.exp(a_log[1])[None, :, None] * jax.nn.softplus(ab4[1] + dt_bias[1][None, :, None])
    beta_f = jax.nn.sigmoid(ab4[2])
    beta_b = jax.nn.sigmoid(ab4[3])
    o_f, s_f = gdn_chunked(q, k, v, g_f, beta_f, s0_f)
    flip = lambda t: jnp.flip(t, axis=2)
    o_b, s_b = gdn_chunked(flip(q), flip(k), flip(v), flip(g_b), flip(beta_b), s0_b)
    o = (o_f + flip(o_b)).transpose(0, 2, 1, 3).astype(h.dtype)
    y_b = (rms_norm(o, o_norm) * jax.nn.silu(z.reshape(Bn, L, B_HEADS, B_DV))).reshape(Bn, L, B_VW)
    y = jnp.concatenate([y_a, y_b], axis=-1) @ w_out
    return y, s_f, s_b

def axial_rope(x, rows, cols):
    half = x.shape[-1] // 2

    def rot(seg, pos):
        n = seg.shape[-1] // 2
        freqs = ROPE_BASE ** (-jnp.arange(n, dtype=jnp.float32) / n)
        ang = pos.astype(jnp.float32)[:, None] * freqs[None, :]
        cos = jnp.cos(ang)[None, :, None, :]
        sin = jnp.sin(ang)[None, :, None, :]
        s1 = seg[..., :n].astype(jnp.float32)
        s2 = seg[..., n:].astype(jnp.float32)
        return jnp.concatenate([s1 * cos - s2 * sin, s2 * cos + s1 * sin], axis=-1)

    return jnp.concatenate([rot(x[..., :half], rows), rot(x[..., half:], cols)], axis=-1).astype(x.dtype)

def mla_project(h, w_in, q_norm, kv_norm, w_uq, w_ukv, rows, cols):
    Bn, L, _ = h.shape
    proj = h @ w_in
    cq, ckv, k_rope = jnp.split(proj, [C_Q_LORA, C_Q_LORA + C_KV_LORA], axis=-1)
    q = (rms_norm(cq, q_norm) @ w_uq).reshape(Bn, L, C_HEADS, C_NOPE + C_ROPE)
    kv = (rms_norm(ckv, kv_norm) @ w_ukv).reshape(Bn, L, C_HEADS, C_NOPE + C_VDIM)
    q_nope, q_rope = q[..., :C_NOPE], q[..., C_NOPE:]
    k_nope, v = kv[..., :C_NOPE], kv[..., C_NOPE:]
    k_rope = k_rope[:, :, None, :]
    if rows is not None:
        q_rope = axial_rope(q_rope, rows, cols)
        k_rope = axial_rope(k_rope, rows, cols)
    q = jnp.concatenate([q_nope, q_rope], axis=-1)
    k = jnp.concatenate([k_nope, jnp.broadcast_to(k_rope, (Bn, L, C_HEADS, C_ROPE))], axis=-1)
    return q, k, v

def block_attention(q, k, v):
    Bn, Lq, H, dq = q.shape
    nb = Lq // C_QBLOCK
    qb = q.reshape(Bn, nb, C_QBLOCK, H, dq).transpose(1, 0, 2, 3, 4)
    scale = dq ** -0.5

    def one(qblk):
        s = jnp.einsum('bqhd,bkhd->bhqk', qblk, k).astype(jnp.float32) * scale
        p = jax.nn.softmax(s, axis=-1).astype(v.dtype)
        return jnp.einsum('bhqk,bkhd->bqhd', p, v)

    o = lax.map(one, qb)
    return o.transpose(1, 0, 2, 3, 4).reshape(Bn, Lq, H, v.shape[-1])

def attn_out(o, w_out):
    Bn, L, H, dv = o.shape
    return o.reshape(Bn, L, H * dv) @ w_out

def peer(h, w_q, sub_keys, u_tab, v_tab):
    Bn, L, D = h.shape
    tok = h.reshape(-1, P_BLOCK, D)

    def one(hb):
        q = (hb @ w_q).reshape(P_BLOCK, P_HEADS, 2, P_DKEY // 2)
        s = jnp.einsum('thpk,hpnk->thpn', q, sub_keys).astype(jnp.float32)
        s1, i1 = lax.top_k(s[:, :, 0], P_TOPK)
        s2, i2 = lax.top_k(s[:, :, 1], P_TOPK)
        cand = (s1[..., :, None] + s2[..., None, :]).reshape(P_BLOCK, P_HEADS, P_TOPK * P_TOPK)
        sc, pos = lax.top_k(cand, P_TOPK)
        idx = (jnp.take_along_axis(i1, pos // P_TOPK, axis=-1) * P_NKEYS
               + jnp.take_along_axis(i2, pos % P_TOPK, axis=-1))
        gate = jax.nn.softmax(sc, axis=-1).astype(hb.dtype)
        act = jax.nn.gelu(jnp.einsum('td,thkd->thk', hb, u_tab[idx]), approximate=False)
        return jnp.einsum('thk,thkd->td', gate * act, v_tab[idx])

    return lax.map(one, tok).reshape(Bn, L, D)

def setup_inputs(seed: int = 0) -> dict:
    key = jax.random.key(seed)
    ks = iter(jax.random.split(key, 40))
    D = D_MODEL
    nrm = lambda shape, s: jax.random.normal(next(ks), shape, jnp.float32) * s
    gain = lambda shape: 1.0 + 0.02 * jax.random.normal(next(ks), shape, jnp.float32)
    x = nrm((BATCH, SEQ, D), 1.0)
    c = nrm((BATCH, D), 1.0)
    ctx = nrm((BATCH, CTX_LEN, D), 1.0)
    c_ctx = nrm((D,), 1.0)
    w_mod = nrm((DEPTH, D, 6 * D), 0.5 * D ** -0.5)
    b_mod = nrm((DEPTH, 6 * D), 0.02)
    norm1 = gain((DEPTH, D))
    norm2 = gain((DEPTH, D))
    ev_w_in = nrm((N_EVEN, D, IN_EVEN), D ** -0.5)
    ev_a_conv = nrm((N_EVEN, A_CONV, A_WIDTH), A_CONV ** -0.5)
    ev_qkv_conv = nrm((N_EVEN, B_CONV, 2 * B_QK + B_VW), B_CONV ** -0.5)
    ev_a_log = jnp.log(jax.random.uniform(next(ks), (N_EVEN, 2, B_HEADS), jnp.float32, 1.0, 16.0))
    dt = jnp.exp(jax.random.uniform(next(ks), (N_EVEN, 2, B_HEADS), jnp.float32, math.log(1e-3), math.log(1e-1)))
    ev_dt_bias = dt + jnp.log(-jnp.expm1(-dt))
    ev_o_norm = gain((N_EVEN, B_DV))
    ev_w_out = nrm((N_EVEN, MIX_EVEN, D), MIX_EVEN ** -0.5)
    od_w_in = nrm((N_ODD, D, IN_ODD), D ** -0.5)
    od_q_norm = gain((N_ODD, C_Q_LORA))
    od_kv_norm = gain((N_ODD, C_KV_LORA))
    od_w_uq = nrm((N_ODD, C_Q_LORA, C_HEADS * (C_NOPE + C_ROPE)), C_Q_LORA ** -0.5)
    od_w_ukv = nrm((N_ODD, C_KV_LORA, C_HEADS * (C_NOPE + C_VDIM)), C_KV_LORA ** -0.5)
    od_w_out = nrm((N_ODD, MIX_ODD, D), MIX_ODD ** -0.5)
    p_w_q = nrm((DEPTH, D, P_HEADS * P_DKEY), D ** -0.5)
    p_keys = nrm((DEPTH, P_HEADS, 2, P_NKEYS, P_DKEY // 2), (P_DKEY // 2) ** -0.5)
    p_u = nrm((DEPTH, P_NEXP, D), D ** -0.5)
    p_v = nrm((DEPTH, P_NEXP, D), 0.5)
    norm_f = gain((D,))
    return {'x': x, 'c': c, 'ctx': ctx, 'c_ctx': c_ctx, 'w_mod': w_mod, 'b_mod': b_mod,
            'norm1': norm1, 'norm2': norm2, 'ev_w_in': ev_w_in, 'ev_a_conv': ev_a_conv,
            'ev_qkv_conv': ev_qkv_conv, 'ev_a_log': ev_a_log, 'ev_dt_bias': ev_dt_bias,
            'ev_o_norm': ev_o_norm, 'ev_w_out': ev_w_out, 'od_w_in': od_w_in, 'od_q_norm': od_q_norm,
            'od_kv_norm': od_kv_norm, 'od_w_uq': od_w_uq, 'od_w_ukv': od_w_ukv, 'od_w_out': od_w_out,
            'p_w_q': p_w_q, 'p_keys': p_keys, 'p_u': p_u, 'p_v': p_v, 'norm_f': norm_f}

def reference(x, c, ctx, c_ctx, w_mod, b_mod, norm1, norm2, ev_w_in, ev_a_conv, ev_qkv_conv, ev_a_log,
              ev_dt_bias, ev_o_norm, ev_w_out, od_w_in, od_q_norm, od_kv_norm, od_w_uq, od_w_ukv, od_w_out,
              p_w_q, p_keys, p_u, p_v, norm_f):
    Bn, S, _ = x.shape
    n_rows = S // GRID_W
    rows = jnp.repeat(jnp.arange(n_rows, dtype=jnp.int32), GRID_W)
    cols = jnp.tile(jnp.arange(GRID_W, dtype=jnp.int32), n_rows)
    for i in range(DEPTH):
        last = i == DEPTH - 1
        j = i // 2
        mod_x = jnp.split(jax.nn.silu(c) @ w_mod[i] + b_mod[i], 6, axis=-1)
        mod_c = jnp.split(jax.nn.silu(c_ctx) @ w_mod[i] + b_mod[i], 6, axis=-1)
        hx = modulate(rms_norm(x, norm1[i]), mod_x[0], mod_x[1])
        hc = modulate(rms_norm(ctx, norm1[i]), mod_c[0], mod_c[1])
        if i % 2 == 0:
            zero = jnp.zeros((Bn, B_HEADS, B_DK, B_DV), jnp.float32)
            yc, s_f, s_b = even_mixer(hc, ev_w_in[j], ev_a_conv[j], ev_qkv_conv[j], ev_a_log[j], ev_dt_bias[j],
                                      ev_o_norm[j], ev_w_out[j], zero, zero)
            yx, _, _ = even_mixer(hx, ev_w_in[j], ev_a_conv[j], ev_qkv_conv[j], ev_a_log[j], ev_dt_bias[j],
                                  ev_o_norm[j], ev_w_out[j], s_f, s_b)
        else:
            qc, kc, vc = mla_project(hc, od_w_in[j], od_q_norm[j], od_kv_norm[j], od_w_uq[j], od_w_ukv[j], None, None)
            qx, kx, vx = mla_project(hx, od_w_in[j], od_q_norm[j], od_kv_norm[j], od_w_uq[j], od_w_ukv[j], rows, cols)
            yx = attn_out(block_attention(qx, jnp.concatenate([kx, kc], axis=1), jnp.concatenate([vx, vc], axis=1)),
                          od_w_out[j])
            yc = None if last else attn_out(block_attention(qc, kc, vc), od_w_out[j])
        x = x + mod_x[2][:, None, :] * yx
        hx2 = modulate(rms_norm(x, norm2[i]), mod_x[3], mod_x[4])
        x = x + mod_x[5][:, None, :] * peer(hx2, p_w_q[i], p_keys[i], p_u[i], p_v[i])
        if not last:
            ctx = ctx + mod_c[2] * yc
            hc2 = modulate(rms_norm(ctx, norm2[i]), mod_c[3], mod_c[4])
            ctx = ctx + mod_c[5] * peer(hc2, p_w_q[i], p_keys[i], p_u[i], p_v[i])
    return rms_norm(x, norm_f)


_drawn_inputs = setup_inputs


def setup_inputs(seed=0):
    import zlib

    import numpy as np

    out = dict(_drawn_inputs(seed))
    spreads = {}
    factors = {'norm1': 3.434,
     'norm2': 22.384,
     'ev_o_norm': 21.792,
     'od_q_norm': 8.0,
     'od_kv_norm': 8.0,
     'norm_f': 7.658}
    for name, (base, spread) in spreads.items():
        noise = np.random.default_rng([zlib.crc32(name.encode()), seed]).standard_normal(out[name].shape)
        drawn = base * np.exp(spread * noise) if base else spread * noise
        out[name] = jnp.asarray(drawn.astype(out[name].dtype))
    for name, factor in factors.items():
        out[name] = (out[name] * factor).astype(out[name].dtype)
    return out
```

```python
from contextlib import ExitStack

import numpy as np
import concourse.bass as bass
from concourse import mybir

F32 = mybir.dt.float32
U32 = mybir.dt.uint32
ALU = mybir.AluOpType
ACT = mybir.ActivationFunctionType
AX = mybir.AxisListType.X

P = 128
D = 1024
KT = D // P
NTOK = 4
EPS = 1e-6
HB = 4
DK = 128
HC = 8
NOPE, ROPE, VD = 128, 64, 128
QL, KVL = 384, 256
PH = 8
NKEY = 128
TOPK = 16
GRID_W = 64
LEVELS = [1, 2, 4, 8, 16, 32, 64]

IDENT, ONES, LE, GT, GE, LT, ZERO = range(7)
LOWER = {s: 7 + i for i, s in enumerate(LEVELS)}
UPPER = {s: 14 + i for i, s in enumerate(LEVELS)}
NCONST = 21

RING = 8
GRP = 4
SLOTS = PH * TOPK
PAIR = 2 * TOPK
PAIRS = SLOTS // PAIR


class Order:

    def __init__(self, sem, events):
        self.sem = sem
        self.events = list(events)
        self.at = {e: i + 1 for i, e in enumerate(self.events)}
        assert len(self.at) == len(self.events)
        self.done = 0

    def count(self, event):
        return self.at[event]

    def mark(self, ins, event):
        assert self.events[self.done] == event, (self.events[self.done], event)
        self.done += 1
        ins.then_inc(self.sem, 1)


class Steps:

    def __init__(self, eng, sem, waited):
        self.eng, self.sem, self.waited, self.base, self.n = eng, sem, waited, 0, 0

    def start(self, base):
        self.base, self.n = base, 0

    def __call__(self, *instructions, apart=False):
        for ins in instructions:
            ins.then_inc(self.sem, 1)
            self.n += 1
        self.eng.wait_ge(self.sem, self.base + self.n)
        if apart:
            self.wait_apart()

    def wait_apart(self):
        self.eng.sem_inc(self.waited, 1)


def group_names():
    first = [("mod", i, c) for i in range(2) for c in range(12)]
    first += [("ht", "m0", t, h) for t in range(NTOK) for h in range(2)]
    first += [("proj", b) for b in range(24)]
    first += [("z", t) for t in range(NTOK)] + [("ab",), ("cum",)]
    first += [("sumsq", b) for b in range(8)]
    first += [(n, t) for t in range(NTOK) for n in ("ktok", "vtok")]
    for q in range(4):
        first += [(n, q, d) for n in ("D", "KK", "QK") for d in range(2)]
        first += [(n, q, d) for d in range(2) for n in ("AT", "intraT")]
        for s in LEVELS[1:]:
            first += [("P1", q, d, s) for d in range(2)]
            for d in range(2):
                first += [("XBX", q, d, s)] + ([("YBY", q, d, s)] if s != LEVELS[-1] else [])
        for n in ("KS", "QS", "vnew", "intraV", "dS"):
            first += [(n, q, d) for d in range(2)]
    first += [("ybT", t) for t in range(NTOK)]
    first += [("out0", t, h) for t in range(NTOK) for h in range(2)]
    first += [("ht", "p0", t, h) for t in range(NTOK) for h in range(2)]
    first += [("q0", h) for h in range(PH)] + [("s0", t, j) for t in range(NTOK) for j in range(4)]
    second = [("ht", "m1", t, h) for t in range(NTOK) for h in range(2)]
    second += [(n, t) for t in range(NTOK) for n in (("lkv", "lq") if t >= 2 else ("lkv",))]
    second += [(n, t) for t in range(NTOK) for n in (("ckvT", "cqT") if t >= 2 else ("ckvT",))]
    second += [("qn", h) for h in range(HC)] + [("qr", t) for t in (2, 3)]
    second += [("qrT", t, g) for t in (2, 3) for g in range(2)]
    second += [("kn", h) for h in range(HC)] + [("v", t, h) for t in range(NTOK) for h in range(2)]
    for u in range(2 * HC):
        second += [("sc", u)]
        if u:
            second += [("pT", u - 1), ("oT", u - 1)]
    second += [("pT", 2 * HC - 1), ("oT", 2 * HC - 1)]
    second += [("out1", t, h) for t in (2, 3) for h in range(2)]
    second += [("ht", "p1", t, h) for t in (2, 3) for h in range(2)]
    second += [("q1", h) for h in range(PH)] + [("s1", t, j) for t in (2, 3) for j in range(4)]
    return first + second


def weight_loads():
    loads = [(("mod", i, c), ("mod", i, c)) for i in range(2) for c in range(12)]
    loads += [(("w_in", c), ("proj", 4 * c + 3)) for c in range(6)]
    loads += [(("w_in", 6), ("z", 3)), (("w_ab",), ("ab",))]
    loads += [(("w_out0", c), ("out0", 3, c)) for c in range(2)]
    loads += [(("w_q0", c), ("q0", 4 * c + 3)) for c in range(2)]
    loads += [(("w_kv1",), ("lkv", 3)), (("w_q_1",), ("lq", 3))]
    loads += [(("w_uq_n",), ("qn", 7)), (("w_uq_r",), ("qr", 3)), (("w_ukv",), ("v", 3, 1))]
    loads += [(("w_out1", c), ("out1", 3, c)) for c in range(2)]
    loads += [(("w_q1", c), ("q1", 4 * c + 3)) for c in range(2)]
    return loads


def build(nc, T, out):
    with ExitStack() as ctx:
        def sb(name, shape, dt=F32):
            return ctx.enter_context(nc.sbuf_tensor(name, shape, dt))

        def sem(name):
            return ctx.enter_context(nc.semaphore(name))

        consts = sb("consts", [P, NCONST * P])
        x = sb("x", [P, NTOK, D])
        wring = sb("wring", [P, 3, 4096])
        arena = sb("arena", [P, 28672])
        small = sb("small", [P, 1024])
        conv_w = sb("conv_w", [P, 16, 3])
        hx_cur = sb("hx_cur", [P, D])
        score_cur = sb("score_cur", [P, 2 * NKEY])
        score_left = sb("score_left", [P, 2 * NKEY])
        cand = sb("cand", [P, TOPK * TOPK])
        cand_left = sb("cand_left", [P, TOPK * TOPK])
        onehot = sb("onehot", [P, TOPK * TOPK])
        iota16 = sb("iota16", [P, TOPK])
        top_val = sb("top_val", [P, 2, TOPK])
        top_idx = sb("top_idx", [P, 2, TOPK], U32)
        top_idx_f = sb("top_idx_f", [P, 2, TOPK])
        best = sb("best", [P, TOPK])
        best_pos = sb("best_pos", [P, TOPK], U32)
        pos_ab = sb("pos_ab", [P, 2, TOPK], U32)
        pos_ab_f = sb("pos_ab_f", [P, 2, TOPK])
        sel_ab = sb("sel_ab", [P, 2, TOPK])
        best_all = sb("best_all", [P, PH, TOPK])
        expert_all = sb("expert_all", [P, PH, TOPK], U32)
        gate_all = sb("gate_all", [P, PH, TOPK])
        gate_tmp = sb("gate_tmp", [P, PH, TOPK])
        gate_sum = sb("gate_sum", [P, 2, PH])
        expert_cur = sb("expert_cur", [P, 2, TOPK], U32)
        gate_cur = sb("gate_cur", [P, PAIR])
        dots = sb("dots", [P, PAIR])
        acts = sb("acts", [P, PAIR])
        coef = sb("coef", [P, PAIR])
        diag = sb("diag", [P, RING, P])
        ps = ctx.enter_context(nc.psum_tensor("ps", [P, 8, 512], F32))
        mods = nc.dram_tensor("mods", (2, 2, 6, D), F32, kind="Internal").ap()

        def const(i):
            return consts[:, i * P:(i + 1) * P]

        def area(at, *shape):
            n = int(np.prod(shape))
            assert at + n <= 28672
            a = arena[:, at:at + n]
            if len(shape) == 1:
                return a
            names = "abcd"[:len(shape)]
            return a.rearrange(f"p ({' '.join(names)}) -> p {' '.join(names)}",
                               **{k: s for k, s in zip(names[:-1], shape)})

        mod_rows = [area(6144 * i, 6, D)[0:2] for i in range(2)]
        norm_rows = area(12288, 2, 2, D)[0:2]
        hT = area(0, KT, 512)
        bgcg = area(4096, 8, 512)
        qkvT = area(8192, 12, 512)
        yT = area(14336, KT, 512)
        zs = area(18432, NTOK, 512)
        ktok = area(20480, NTOK, 512)
        vtok = area(22528, NTOK, 512)
        modbc0 = [area(24576, 2, D), area(20480, 2, D)]
        hbuf0 = area(26624, 2, D)
        lg = area(0, 2, 512)
        A = area(1024, 2, 512)
        gam = area(2048, 2, 512)
        intra = area(3072, 2, 512)
        intraT = area(4096, 2, 512)
        X = area(5120, 2, 512)
        Y = area(6144, 2, 512)
        Bm = area(7168, 2, 512)
        P1s = area(24576, 2, 512)
        S = area(25600, 2, 512)
        oacc = area(26624, NTOK, 512)
        R, vn, tmp, kdK = gam, lg, intra, Bm
        rtmp0 = area(22528, 2, 512)
        gate0 = area(20480, 2, D)
        qT = area(4096, PH, 512)
        keysB = area(8192, PH, 256)
        modbcp = [area(10240, 2, D), area(12288, 2, D)]
        score = area(16384, NTOK, PH, 256)
        hx2 = area(24576, NTOK, D)
        ring = area(0, RING, 2 * D)
        peer_gate = area(0, 2, D)
        hbuf1 = area(4096, 2, D)
        modbc1 = [area(6144, 2, D), area(8192, 2, D)]
        lat = area(10240, NTOK, 704)
        cqT = area(13056, 3, 256)
        ckvT = area(13824, 2, 512)
        krT = area(14848, 512)
        lat_gain = area(15360, 640)
        rope_cs = area(16000, 2, 2, 2, 16)
        knT = area(16384, HC, 512)
        vatt = area(20480, NTOK, D)
        qnT = area(24576, HC, 256)
        qrope = area(26624, 2, 512)
        rtmp = area(27648, 4, 256)
        qrT = area(0, HC, 256)
        prob = area(2048, 2, 512)
        probT = area(3072, 2, 512)
        oT = area(4096, HC, 256)
        gate1 = area(6144, D)
        kdup = area(7168, 128)
        hfin = area(2048, 2, D)
        gain_f = area(4096, D)

        sT = small[:, 0:16]
        ab = small[:, 16:80].rearrange("p (t c) -> p t c", t=NTOK)
        ssq = small[:, 80:104]
        rstd = small[:, 104:128]
        alog = small[:, 128:136]
        dtb = small[:, 136:144]
        nexpa = small[:, 144:152]
        gdec = small[:, 152:184].rearrange("p (t c) -> p t c", t=NTOK)
        g1 = small[:, 184:216].rearrange("p (t c) -> p t c", t=NTOK)
        g2 = small[:, 216:248].rearrange("p (t c) -> p t c", t=NTOK)
        beta = small[:, 248:280].rearrange("p (t c) -> p t c", t=NTOK)
        expo = small[:, 280:376]
        edec = expo[:, 0:32].rearrange("p (d t h) -> p d t h", d=2, t=NTOK)
        erest = expo[:, 32:64].rearrange("p (d t h) -> p d t h", d=2, t=NTOK)
        eall = expo[:, 64:96].rearrange("p (t d h) -> p t d h", t=NTOK, d=2)
        ossq = small[:, 376:392]
        orst = small[:, 392:408]
        lssq = small[:, 408:416]
        lrst = small[:, 416:424]
        smax = small[:, 424:440]
        nsmax = small[:, 440:456]
        ssum = small[:, 456:472]
        srec = small[:, 472:488]
        sTin = small[:, 488:504]
        eps_col = small[:, 504:505]
        ogain = small[:, 512:640]

        GROUPS = group_names()
        product = Order(sem("product_done"), GROUPS)
        bank_free = [sem(f"bank_free{b}") for b in range(8)]
        w_landed = [sem(f"w_landed{i}") for i in range(3)]
        x_landed = sem("x_landed")
        consts_landed = sem("consts_landed")
        row_landed = [sem(f"mod_bias_landed{i}") for i in range(2)]
        rows_stored = sem("mod_rows_stored")
        bc_names = [("m0", 0), ("m0", 1), ("g0",), ("p0", 0), ("p0", 1), ("keys0",),
                    ("m1", 0), ("m1", 1), ("lat",), ("g1",), ("p1",), ("keys1",), ("pg0",), ("pg1",), ("nf",)]
        bc_landed = {n: sem("landed_" + "_".join(map(str, n))) for n in bc_names}
        act_steps = sem("act_steps")
        dve_steps = sem("dve_steps")
        pool_steps = sem("pool_steps")
        norm_events = ([("m0", t) for t in range(NTOK)] + [("p0", t) for t in range(NTOK)]
                       + [("m1", t) for t in range(NTOK)] + [("p1", t) for t in (2, 3)]
                       + [("f", t) for t in (2, 3)])
        ssq_ready = Order(sem("ssq_ready"), norm_events)
        h_ready = Order(sem("h_ready"), norm_events)
        silu_c = sem("silu_c_ready")
        rows_ready = sem("mod_rows_ready")
        xa_conv = Order(sem("xa_scaled"), [("xa", b) for b in range(4)])
        u_ready = Order(sem("gated_input_ready"), [("u", b) for b in range(4)])
        conv_ready = Order(sem("conv_ready"), [("conv", b) for b in range(12)])
        centre_ready = Order(sem("centre_tap_ready"), list(range(12)))
        eps_ready = sem("eps_ready")
        silu_ready = Order(sem("qkv_silu_ready"), [("silu", b) for b in range(12)])
        square_ready = Order(sem("qk_square_ready"), [("sq", b) for b in range(8)])
        qk_ready = Order(sem("qk_normed"), [("qk", b) for b in range(8)])
        ya_ready = sem("y_a_ready")
        sp_act = sem("softplus_act")
        sp_dve = sem("softplus_dve")
        pq = [(q, d) for q in range(4) for d in range(2)]
        lg_ready = Order(sem("lg_ready"), pq)
        ai_ready = Order(sem("a_intra_ready"), [(n, q, d) for q in range(4) for d in range(2) for n in "AI"])
        xy_ready = Order(sem("xy_ready"), [(n, q, d, s) for q in range(4) for s in LEVELS for d in range(2)
                                           for n in ("XY" if s != LEVELS[-1] else "X")])
        bm_ready = Order(sem("level_ready"), [(q, d, s) for q in range(4) for s in LEVELS[1:] for d in range(2)])
        kd_ready = Order(sem("kd_ready"), pq)
        r_ready = Order(sem("r_ready"), pq)
        s_ready = Order(sem("state_ready"), ["zero"] + pq)
        osq_ready = Order(sem("o_square_ready"), list(range(NTOK)))
        yb_ready = Order(sem("y_b_ready"), list(range(NTOK)))
        x_ready = Order(sem("x_ready"), [("m0", t) for t in range(NTOK)] + [("p0", t) for t in range(NTOK)]
                        + [("m1", t) for t in (2, 3)] + [("p1", t) for t in (2, 3)])
        lsq_ready = sem("latent_square_ready")
        lat_ready = Order(sem("latent_ready"), list(range(NTOK)))
        qr_ready = Order(sem("q_rope_ready"), [2, 3])
        nmax_ready = Order(sem("row_max_ready"), list(range(2 * HC)))
        pexp_ready = Order(sem("exp_ready"), list(range(2 * HC)))
        prob_ready = Order(sem("prob_ready"), list(range(2 * HC)))
        stored = sem("stored")
        slot_landed = [sem(f"slot_landed{k}") for k in range(RING)]
        slot_free = sem("slot_free")
        dots_ready = sem("dots_ready")
        coef_ready = sem("coef_ready")
        diag_ready = sem("diag_ready")
        ranked = sem("head_ranked")
        sub_ready = sem("gate_sub_ready")
        gexp_ready = sem("gate_exp_ready")
        gates_ready = sem("gates_ready")
        gates_taken = sem("gates_taken")
        peer_taken = sem("peer_tile_taken")

        def bank_of(name):
            return (product.count(name) - 1) % 8

        def out_bank(pe, name):
            n = product.count(name) - 1
            if n >= 8:
                pe.wait_ge(bank_free[n % 8], n // 8)
            return ps[:, n % 8, :]

        def in_bank(eng, name):
            eng.wait_ge(product.sem, product.count(name))
            return ps[:, bank_of(name), :]

        def free_bank(ins, name):
            ins.then_inc(bank_free[bank_of(name)], 1)

        def taken(eng, name):
            n = product.count(name) - 1
            eng.wait_ge(bank_free[n % 8], n // 8 + 1)

        LOADS = weight_loads()
        load_at = {name: i for i, (name, _) in enumerate(LOADS)}

        def weights(eng, name):
            i = load_at[name]
            eng.wait_ge(w_landed[i % 3], 16 * (i // 3 + 1))
            return wring[:, i % 3, :]

        def load_weight(sp, name, src):
            i = load_at[name]
            if i >= 3:
                sp.wait_ge(product.sem, product.count(LOADS[i - 3][1]))
            k, n = src.shape[1], src.shape[2]
            dst = wring[:, i % 3, 0:k * n].rearrange("p (k n) -> p k n", k=k)
            sp.dma_start(dst, src).then_inc(w_landed[i % 3], 16)

        def ktiles(w, lo, hi):
            return w.rearrange("(k p) n -> p k n", p=P)[:, :, lo:hi]

        def heads(ap):
            return ap.rearrange("p (h c) -> p h c", h=HB)

        def over_heads(matrix):
            return matrix.unsqueeze(1).broadcast_to((P, HB, P))

        def per_head(col):
            return col.unsqueeze(2).broadcast_to((P, HB, P))

        def tok(t):
            return slice(t * P, (t + 1) * P)

        def unit(q, d):
            s, k = q // 2, q % 2
            return 2 * s + (k if d == 0 else 1 - k)

        INCL = (GE, LE)
        SUM_TO = (LE, GE)
        SUM_REST = (GT, LT)
        MASK = (LOWER, UPPER)

        def norm_act(act, stage, t, dst, first):
            e = ssq_ready.count((stage, t)) - 1
            act.wait_ge(*first)
            act_step(nc.scalar.activation(dst, x[:, t, :], ACT.Square, accum_out=ssq[:, e:e + 1]))
            ssq_ready.mark(nc.scalar.activation(rstd[:, e:e + 1], ssq[:, e:e + 1], ACT.Sqrt, bias=eps_col,
                                                scale=1.0 / D), (stage, t))

        def norm_dve(dve, step, stage, t, dst, gain, shift):
            e = ssq_ready.count((stage, t)) - 1
            dve.wait_ge(ssq_ready.sem, e + 1)
            step(nc.vector.reciprocal(rstd[:, e:e + 1], rstd[:, e:e + 1]))
            last = nc.vector.scalar_tensor_tensor(out=dst, in0=x[:, t, :], scalar=rstd[:, e:e + 1], in1=gain,
                                                  op0=ALU.mult, op1=ALU.mult)
            if shift is not None:
                step(last)
                last = nc.vector.tensor_tensor(dst, dst, shift, ALU.add)
            h_ready.mark(last, (stage, t))

        def norm_pe(pe, stage, t, src):
            pe.wait_ge(h_ready.sem, h_ready.count((stage, t)))
            for half in range(2):
                name = ("ht", stage, t, half)
                bank = out_bank(pe, name)
                for j in range(4):
                    c = 4 * half + j
                    last = nc.tensor.transpose(bank[:, j * P:(j + 1) * P], src[:, c * P:(c + 1) * P], const(IDENT))
                product.mark(last, name)

        def norm_take(eng, copy, stage, t, half, slot):
            bank = in_bank(eng, ("ht", stage, t, half))
            free_bank(copy(hT[:, 4 * half:4 * half + 4, tok(slot)], bank.rearrange("p (k t) -> p k t", k=4)),
                      ("ht", stage, t, half))

        def residual(dve, step, product_name, stage, tiles, gate_of, gate_landed, rows):
            dve.wait_ge(gate_landed, 16)
            for t in tiles:
                for c in range(2):
                    cols = slice(512 * c, 512 * c + 512)
                    bank = in_bank(dve, (product_name, t, c))
                    free_bank(nc.vector.tensor_tensor(rows[:, c, :], bank, gate_of(t)[:, cols], ALU.mult),
                              (product_name, t, c))
                    taken(dve, (product_name, t, c))
                    last = nc.vector.tensor_tensor(x[:, t, cols], x[:, t, cols], rows[:, c, :], ALU.add)
                    if c:
                        x_ready.mark(last, (stage, t))

        def peer_scores_pe(pe, layer, tiles, keys_landed):
            n = P * len(tiles)
            for t in tiles:
                for half in range(2):
                    taken(pe, ("ht", "p" + layer, t, half))
            for h in range(PH):
                w = weights(pe, ("w_q" + layer, h // 4)).rearrange("p (k n) -> p k n", k=KT)
                c = (h % 4) * P
                bank = out_bank(pe, ("q" + layer, h))
                for k in range(KT):
                    last = nc.tensor.matmul(bank[:, 0:n], w[:, k, c:c + P], hT[:, k, 0:n],
                                            start=(k == 0), stop=(k == KT - 1))
                product.mark(last, ("q" + layer, h))
            pe.wait_ge(keys_landed, 16)
            for i, t in enumerate(tiles):
                for j in range(4):
                    bank = out_bank(pe, ("s" + layer, t, j))
                    for k in range(2):
                        h = 2 * j + k
                        taken(pe, ("q" + layer, h))
                        last = nc.tensor.matmul(bank[:, 256 * k:256 * k + 256], qT[:, h, tok(i)], keysB[:, h, :],
                                                start=True, stop=True)
                    product.mark(last, ("s" + layer, t, j))

        pool_step, act_step, dve_step = (Steps(e, s, sem("waited_" + n)) for e, s, n in (
            (nc.gpsimd, pool_steps, "pool"), (nc.scalar, act_steps, "act"), (nc.vector, dve_steps, "dve")))

        def first_block(block):
            @block.sync
            def _(sp):
                sp.dma_start(x[:, 0:2, :], T["ctx"].rearrange("(t p) d -> p t d", p=P)).then_inc(x_landed, 16)
                sp.dma_start(x[:, 2:4, :], T["x"].rearrange("(t p) d -> p t d", p=P)).then_inc(x_landed, 16)
                for i in range(2):
                    for c in range(12):
                        load_weight(sp, ("mod", i, c), ktiles(T["w_mod"][i], c * 512, (c + 1) * 512))
                for c in range(7):
                    load_weight(sp, ("w_in", c), ktiles(T["ev_w_in"], c * 512, (c + 1) * 512))
                load_weight(sp, ("w_ab",), ktiles(T["ev_w_in"], 3584, 3600))
                for c in range(2):
                    load_weight(sp, ("w_out0", c), ktiles(T["ev_w_out"], c * 512, (c + 1) * 512))
                for c in range(2):
                    load_weight(sp, ("w_q0", c), ktiles(T["p_w_q"][0], c * 512, (c + 1) * 512))

            @block.gpsimd
            def _(pool):
                step = pool_step
                nc.gpsimd.memset(eps_col, EPS).then_inc(eps_ready, 1)
                pool.dma_start(sTin, T["c_cols"]).then_inc(consts_landed, 16)
                pool.dma_start(consts[:, :], T["consts"]).then_inc(consts_landed, 16)
                pool.dma_start(iota16[:, :], T["iota16"]).then_inc(consts_landed, 16)
                pool.dma_start(conv_w[:, :, :], T["conv_w"]).then_inc(consts_landed, 16)
                pool.dma_start(alog, T["a_log"].partition_broadcast(P)).then_inc(consts_landed, 16)
                pool.dma_start(dtb, T["dt_bias"].partition_broadcast(P)).then_inc(consts_landed, 16)
                pool.dma_start(ogain, T["o_norm"].partition_broadcast(P)).then_inc(consts_landed, 16)
                for i in range(2):
                    for s in range(2):
                        pool.dma_start(mod_rows[i][s:s + 1], T["b_mod"][i:i + 1]).then_inc(row_landed[i], 16)
                for s in range(2):
                    pool.dma_start(norm_rows[s:s + 1], T["norms"]).then_inc(row_landed[0], 16)
                pool.wait_ge(rows_ready, 1)
                pool.dma_start(mods[0], mod_rows[0]).then_inc(rows_stored, 16)
                pool.wait_ge(rows_ready, 2)
                pool.dma_start(mods[1], mod_rows[1]).then_inc(rows_stored, 16)
                pool.wait_ge(rows_stored, 32)
                for s in range(2):
                    pool.dma_start(modbc0[s], mods[0, s, 0:2].partition_broadcast(P)).then_inc(bc_landed["m0", s], 16)
                for q in range(4):
                    for s in LEVELS[1:]:
                        for d in range(2):
                            if s == 2:
                                pool.wait_ge(ai_ready.sem, ai_ready.count(("A", q, d)))
                                if q:
                                    pool.wait_ge(product.sem, product.count(("dS", q - 1, d)))
                            else:
                                pool.wait_ge(product.sem, product.count(("P1", q, d, s // 2)))
                            bm_ready.mark(nc.gpsimd.tensor_tensor(heads(Bm[:, d, :]), heads(A[:, d, :]),
                                                                  over_heads(const(MASK[d][s])), ALU.mult), (q, d, s))
                    for d in range(2):
                        t = unit(q, d)
                        pool.wait_ge(product.sem, product.count(("P1", q, d, LEVELS[-1])))
                        if q == 0 and d == 0:
                            for tt in range(NTOK):
                                taken(pool, ("ktok", tt))
                            pool.wait_ge(sp_act, 5)
                        kd_ready.mark(nc.gpsimd.tensor_tensor(heads(kdK[:, d, :]), heads(ktok[:, t, :]),
                                                              per_head(erest[:, d, t, :]), ALU.mult), (q, d))
                pool.wait_ge(product.sem, product.count(("dS", 3, 1)))
                pool.wait_ge(kd_ready.sem, kd_ready.count((3, 1)))
                pool.wait_ge(r_ready.sem, r_ready.count((3, 1)))
                pool.dma_start(gate0[:, :, :], mods[0][:, 2].partition_broadcast(P)).then_inc(bc_landed["g0",], 16)
                for s in range(2):
                    pool.dma_start(modbcp[s], mods[0, s, 3:5].partition_broadcast(P)).then_inc(bc_landed["p0", s], 16)
                pool.dma_start(keysB[:, :, :], T["keys"][0]).then_inc(bc_landed["keys0",], 16)

            @block.scalar
            def _(act):
                step = act_step
                A_ = nc.scalar.activation
                act.wait_ge(consts_landed, 7 * 16)
                A_(sT, sTin, ACT.Silu).then_inc(silu_c, 1)
                act.wait_ge(x_landed, 32)
                act.wait_ge(eps_ready, 1)
                for t in range(NTOK):
                    first = (x_landed, 32) if t < 2 else (product.sem, product.count(("ht", "m0", t - 2, 1)))
                    norm_act(act, "m0", t, hbuf0[:, t % 2, :], first)
                    if t:
                        norm_take(act, nc.scalar.copy, "m0", t - 1, 0, t - 1)
                norm_take(act, nc.scalar.copy, "m0", 3, 0, 3)
                for b in range(8):
                    bank = in_bank(act, ("proj", b))
                    free_bank(nc.scalar.copy(bgcg[:, b, :], bank), ("proj", b))
                for b in range(4):
                    act.wait_ge(u_ready.sem, u_ready.count(("u", b)))
                    xa_conv.mark(A_(yT[:, b, :], yT[:, 4 + b, :], ACT.Copy, scale=conv_w[:, b, 1:2]), ("xa", b))
                for b in range(12):
                    bank = in_bank(act, ("proj", 12 + b))
                    centre_ready.mark(A_(qkvT[:, b, :], bank, ACT.Copy, scale=conv_w[:, 4 + b, 1:2]), b)
                    act.wait_ge(conv_ready.sem, conv_ready.count(("conv", b)))
                    silu_ready.mark(A_(qkvT[:, b, :], qkvT[:, b, :], ACT.Silu), ("silu", b))
                for t in range(NTOK):
                    bank = in_bank(act, ("z", t))
                    free_bank(A_(zs[:, t, :], bank, ACT.Silu), ("z", t))
                act.wait_ge(sp_dve, 1)
                A_(beta, ab[:, :, 8:16], ACT.Sigmoid).then_inc(sp_act, 1)
                A_(g2, g2, ACT.Exp).then_inc(sp_act, 1)
                A_(nexpa, alog, ACT.Exp).then_inc(sp_act, 1)
                act.wait_ge(sp_act, 3)
                A_(g2, g2, ACT.Ln, bias=1.0).then_inc(sp_act, 1)
                cum = in_bank(act, ("cum",))
                free_bank(A_(expo, cum[:, 0:96], ACT.Exp), ("cum",))
                taken(act, ("cum",))
                act.sem_inc(sp_act, 1)
                for b in range(8):
                    act.wait_ge(silu_ready.sem, silu_ready.count(("silu", b)))
                    square_ready.mark(A_(hT[:, b, :], qkvT[:, b, :], ACT.Square), ("sq", b))
                for b in range(8):
                    bank = in_bank(act, ("sumsq", b))
                    free_bank(A_(hT[:, b, :], bank, ACT.Sqrt, bias=eps_col), ("sumsq", b))
                for t in range(NTOK):
                    free_bank(nc.scalar.copy(vtok[:, t, :], in_bank(act, ("vtok", t))), ("vtok", t))
                for q in range(4):
                    for d in range(2):
                        bank = in_bank(act, ("D", q, d))
                        free_bank(A_(gam[:, d, :], bank, ACT.Exp), ("D", q, d))
                    for d in range(2):
                        bank = in_bank(act, ("intraT", q, d))
                        free_bank(nc.scalar.copy(intraT[:, d, :], bank), ("intraT", q, d))
                    for s in LEVELS[1:]:
                        for d in range(2):
                            bank = in_bank(act, ("P1", q, d, s))
                            free_bank(nc.scalar.copy(P1s[:, d, :], bank), ("P1", q, d, s))
                    for d in range(2):
                        bank = in_bank(act, ("vnew", q, d))
                        free_bank(nc.scalar.copy(vn[:, d, :], bank), ("vnew", q, d))
                for t in range(NTOK):
                    act.wait_ge(s_ready.sem, s_ready.count((3, 1)))
                    act.wait_ge(product.sem, product.count(("dS", 3, 1)))
                    act_step(*[A_(arena[:, 512 * t + h * P:512 * t + (h + 1) * P], oacc[:, t, h * P:(h + 1) * P],
                                  ACT.Square, accum_out=ossq[:, 4 * t + h:4 * t + h + 1]) for h in range(HB)])
                    osq_ready.mark(A_(orst[:, 4 * t:4 * t + 4], ossq[:, 4 * t:4 * t + 4], ACT.Sqrt, bias=eps_col,
                                      scale=1.0 / DK), t)
                for t in range(NTOK):
                    bank = in_bank(act, ("ybT", t))
                    free_bank(nc.scalar.copy(yT[:, 4:8, tok(t)], heads(bank)), ("ybT", t))
                for t in range(NTOK):
                    norm_act(act, "p0", t, hx2[:, t, :], (x_ready.sem, x_ready.count(("m0", t))))
                    if t:
                        norm_take(act, nc.scalar.copy, "p0", t - 1, 0, t - 1)
                norm_take(act, nc.scalar.copy, "p0", 3, 0, 3)
                for h in range(PH):
                    bank = in_bank(act, ("q0", h))
                    free_bank(nc.scalar.copy(qT[:, h, :], bank), ("q0", h))
                for t in range(NTOK):
                    for j in range(0, 4, 2):
                        bank = in_bank(act, ("s0", t, j))
                        free_bank(nc.scalar.copy(score[:, t, 2 * j:2 * j + 2, :],
                                                 bank.rearrange("p (h n) -> p h n", h=2)), ("s0", t, j))

            @block.vector
            def _(dve):
                step = dve_step
                V = nc.vector
                for i in range(2):
                    dve.wait_ge(row_landed[i], 64 if i == 0 else 32)
                    for c in range(12):
                        bank = in_bank(dve, ("mod", i, c))
                        row = mod_rows[i][:, c // 2, (c % 2) * 512:(c % 2) * 512 + 512]
                        free_bank(V.tensor_tensor(row, bank[0:2, :], row, ALU.add), ("mod", i, c))
                    for c in range(12):
                        taken(dve, ("mod", i, c))
                    step(*[V.scalar_tensor_tensor(out=mod_rows[i][:, 1 + 3 * n, :], in0=mod_rows[i][:, 1 + 3 * n, :],
                                                  scalar=1.0, in1=norm_rows[:, i, n, :], op0=ALU.add, op1=ALU.mult)
                           for n in range(2)])
                    dve.sem_inc(rows_ready, 1)
                for t in range(NTOK):
                    if t % 2 == 0:
                        dve.wait_ge(bc_landed["m0", t // 2], 16)
                    bc = modbc0[t // 2]
                    norm_dve(dve, step, "m0", t, hbuf0[:, t % 2, :], bc[:, 1, :], bc[:, 0, :])
                    if t:
                        norm_take(dve, V.tensor_copy, "m0", t - 1, 1, t - 1)
                norm_take(dve, V.tensor_copy, "m0", 3, 1, 3)

                def other_taps(acc, u, w):
                    a3, u3 = (v.rearrange("p (s t) -> p s t", s=2) for v in (acc, u))
                    step(V.scalar_tensor_tensor(out=a3[:, :, 1:256], in0=u3[:, :, 0:255], scalar=w[:, 0:1],
                                                in1=a3[:, :, 1:256], op0=ALU.mult, op1=ALU.add))
                    return V.scalar_tensor_tensor(out=a3[:, :, 0:255], in0=u3[:, :, 1:256], scalar=w[:, 2:3],
                                                  in1=a3[:, :, 0:255], op0=ALU.mult, op1=ALU.add)

                for b in range(4):
                    bank = in_bank(dve, ("proj", 8 + b))
                    taken(dve, ("proj", 4 + b))
                    free_bank(V.tensor_tensor(yT[:, 4 + b, :], bank, bgcg[:, 4 + b, :], ALU.mult), ("proj", 8 + b))
                    taken(dve, ("proj", 8 + b))
                    dve.sem_inc(u_ready.sem, 1)
                    u_ready.done += 1
                    dve.wait_ge(xa_conv.sem, xa_conv.count(("xa", b)))
                    step(other_taps(yT[:, b, :], yT[:, 4 + b, :], conv_w[:, b, :]))
                    taken(dve, ("proj", b))
                    last = V.tensor_tensor(yT[:, b, :], yT[:, b, :], bgcg[:, b, :], ALU.mult)
                    last.then_inc(ya_ready, 1)
                for b in range(12):
                    bank = in_bank(dve, ("proj", 12 + b))
                    dve.wait_ge(centre_ready.sem, centre_ready.count(b))
                    free_bank(other_taps(qkvT[:, b, :], bank, conv_w[:, 4 + b, :]), ("proj", 12 + b))
                    taken(dve, ("proj", 12 + b))
                    dve.sem_inc(conv_ready.sem, 1)
                    conv_ready.done += 1
                bank = in_bank(dve, ("ab",))
                free_bank(V.tensor_copy(small[:, 16:80], bank[:, 0:64]), ("ab",))
                taken(dve, ("ab",))
                step(V.tensor_tensor(g1, ab[:, :, 0:8], dtb.unsqueeze(1).broadcast_to((P, NTOK, 8)), ALU.add))
                step(V.scalar_tensor_tensor(out=g2, in0=g1, scalar=-1.0, in1=g1, op0=ALU.mult, op1=ALU.min))
                dve.sem_inc(sp_dve, 1)
                step(V.tensor_scalar(g1, g1, 0.0, None, ALU.max))
                dve.wait_ge(sp_act, 4)
                step(V.tensor_tensor(g1, g1, g2, ALU.add))
                step(V.scalar_tensor_tensor(out=gdec, in0=g1, scalar=-1.0,
                                            in1=nexpa.unsqueeze(1).broadcast_to((P, NTOK, 8)),
                                            op0=ALU.mult, op1=ALU.mult))
                dve.sem_inc(sp_dve, 1)
                for b in range(8):
                    r = hT[:, b, :]
                    taken(dve, ("sumsq", b))
                    step(V.reciprocal(r, r))
                    step(V.scalar_tensor_tensor(out=qkvT[:, b, :], in0=qkvT[:, b, :],
                                                scalar=float(DK) ** -0.5 if b < 4 else 1.0, in1=r,
                                                op0=ALU.mult, op1=ALU.mult))
                    dve.sem_inc(qk_ready.sem, 1)
                qk_ready.done = 8
                for t in range(NTOK):
                    free_bank(V.tensor_copy(ktok[:, t, :], in_bank(dve, ("ktok", t))), ("ktok", t))
                dve.sem_inc(slot_free, RING)
                dve.sem_inc(gates_taken, 1)
                dve.sem_inc(peer_taken, 1)
                dve.wait_ge(sp_act, 5)
                step(V.memset(S[:, :, :], 0.0))
                dve.sem_inc(s_ready.sem, 1)
                s_ready.done += 1
                for q in range(4):
                    for d in range(2):
                        t = unit(q, d)
                        if q:
                            dve.wait_ge(product.sem, product.count(("dS", q - 1, d)))
                        last = [V.tensor_scalar(lg[:, d, h * P:(h + 1) * P], const(SUM_TO[d]),
                                                gdec[:, t, 4 * d + h:4 * d + h + 1], None, ALU.mult)
                                for h in range(HB)][-1]
                        lg_ready.mark(last, (q, d))
                    for d in range(2):
                        t = unit(q, d)
                        kk, qk = in_bank(dve, ("KK", q, d)), in_bank(dve, ("QK", q, d))
                        taken(dve, ("D", q, d))
                        free_bank(V.tensor_tensor(A[:, d, :], kk, gam[:, d, :], ALU.mult), ("KK", q, d))
                        free_bank(V.tensor_tensor(intra[:, d, :], qk, gam[:, d, :], ALU.mult), ("QK", q, d))
                        taken(dve, ("KK", q, d))
                        ai_ready.mark(V.tensor_tensor(heads(A[:, d, :]), heads(A[:, d, :]),
                                                      per_head(beta[:, t, 4 * d:4 * d + 4]), ALU.mult), ("A", q, d))
                        taken(dve, ("QK", q, d))
                        ai_ready.mark(V.tensor_tensor(heads(intra[:, d, :]), heads(intra[:, d, :]),
                                                      over_heads(const(INCL[d])), ALU.mult), ("I", q, d))
                    for d in range(2):
                        dve.wait_ge(ai_ready.sem, ai_ready.count(("A", q, d)))
                        step(V.tensor_tensor(heads(Y[:, d, :]), heads(A[:, d, :]), over_heads(const(MASK[d][1])), ALU.mult))
                        bank = in_bank(dve, ("AT", q, d))
                        free_bank(V.tensor_tensor(heads(X[:, d, :]), heads(bank), over_heads(const(MASK[1 - d][1])),
                                                  ALU.mult), ("AT", q, d))
                        taken(dve, ("AT", q, d))
                        for n, m in (("X", X), ("Y", Y)):
                            xy_ready.mark(V.tensor_tensor(heads(m[:, d, :]), over_heads(const(IDENT)), heads(m[:, d, :]),
                                                          ALU.subtract), (n, q, d, 1))
                    for s in LEVELS[1:]:
                        for d in range(2):
                            for n, m in (("X", X), ("Y", Y)):
                                if n == "Y" and s == LEVELS[-1]:
                                    continue
                                name = (n + "B" + n, q, d, s)
                                bank = in_bank(dve, name)
                                dve.wait_ge(xy_ready.sem, xy_ready.count((n, q, d, s // 2)))
                                ins = V.tensor_tensor(m[:, d, :], m[:, d, :], bank, ALU.subtract)
                                free_bank(ins, name)
                                taken(dve, name)
                                dve.sem_inc(xy_ready.sem, 1)
                                xy_ready.done += 1
                    for d in range(2):
                        t = unit(q, d)
                        bank = in_bank(dve, ("KS", q, d))
                        free_bank(V.tensor_tensor(heads(R[:, d, :]), heads(bank), per_head(edec[:, d, t, :]), ALU.mult),
                                  ("KS", q, d))
                        if q == 0 and d == 0:
                            for tt in range(NTOK):
                                taken(dve, ("vtok", tt))
                        taken(dve, ("KS", q, d))
                        step(V.tensor_tensor(R[:, d, :], vtok[:, t, :], R[:, d, :], ALU.subtract))
                        r_ready.mark(V.tensor_tensor(heads(R[:, d, :]), heads(R[:, d, :]),
                                                     per_head(beta[:, t, 4 * d:4 * d + 4]), ALU.mult), (q, d))
                    for d in range(2):
                        t = unit(q, d)
                        bank = in_bank(dve, ("QS", q, d))
                        dve.wait_ge(product.sem, product.count(("intraT", q, d)))
                        free_bank(V.tensor_tensor(heads(tmp[:, d, :]), heads(bank), per_head(edec[:, d, t, :]), ALU.mult),
                                  ("QS", q, d))
                        taken(dve, ("QS", q, d))
                        bank = in_bank(dve, ("intraV", q, d))
                        if q % 2 == 0:
                            free_bank(V.tensor_tensor(oacc[:, t, :], tmp[:, d, :], bank, ALU.add), ("intraV", q, d))
                            taken(dve, ("intraV", q, d))
                        else:
                            free_bank(V.tensor_tensor(tmp[:, d, :], tmp[:, d, :], bank, ALU.add), ("intraV", q, d))
                            taken(dve, ("intraV", q, d))
                            step(V.tensor_tensor(oacc[:, t, :], oacc[:, t, :], tmp[:, d, :], ALU.add))
                        bank = in_bank(dve, ("dS", q, d))
                        step(V.tensor_tensor(heads(S[:, d, :]), heads(S[:, d, :]), per_head(eall[:, t, d, :]), ALU.mult))
                        free_bank(V.tensor_tensor(S[:, d, :], S[:, d, :], bank, ALU.add), ("dS", q, d))
                        taken(dve, ("dS", q, d))
                        dve.sem_inc(s_ready.sem, 1)
                        s_ready.done += 1
                for t in range(NTOK):
                    dve.wait_ge(osq_ready.sem, osq_ready.count(t))
                    r4 = orst[:, 4 * t:4 * t + 4]
                    step(V.reciprocal(r4, r4))
                    step(V.tensor_tensor(heads(oacc[:, t, :]), heads(oacc[:, t, :]), per_head(r4), ALU.mult))
                    step(V.tensor_tensor(heads(oacc[:, t, :]), heads(oacc[:, t, :]), over_heads(ogain), ALU.mult))
                    if t == 0:
                        for tt in range(NTOK):
                            taken(dve, ("z", tt))
                    yb_ready.mark(V.tensor_tensor(oacc[:, t, :], oacc[:, t, :], zs[:, t, :], ALU.mult), t)
                residual(dve, step, "out0", "m0", range(NTOK), lambda t: gate0[:, t // 2, :], bc_landed["g0",], rtmp0)
                for t in range(NTOK):
                    if t % 2 == 0:
                        dve.wait_ge(bc_landed["p0", t // 2], 16)
                    bc = modbcp[t // 2]
                    norm_dve(dve, step, "p0", t, hx2[:, t, :], bc[:, 1, :], bc[:, 0, :])
                    if t:
                        norm_take(dve, V.tensor_copy, "p0", t - 1, 1, t - 1)
                norm_take(dve, V.tensor_copy, "p0", 3, 1, 3)
                for t in range(NTOK):
                    for j in range(1, 4, 2):
                        bank = in_bank(dve, ("s0", t, j))
                        free_bank(V.tensor_copy(score[:, t, 2 * j:2 * j + 2, :],
                                                bank.rearrange("p (h n) -> p h n", h=2)), ("s0", t, j))

            @block.tensor
            def _(pe):
                M, TR = nc.tensor.matmul, nc.tensor.transpose

                def accumulate(dst, pairs):
                    for i, (l, r) in enumerate(pairs):
                        last = M(dst, l, r, start=(i == 0), stop=(i == len(pairs) - 1))
                    return last

                pe.wait_ge(silu_c, 1)
                pe.wait_ge(consts_landed, 7 * 16)
                for i in range(2):
                    for c in range(12):
                        w = weights(pe, ("mod", i, c)).rearrange("p (k n) -> p k n", k=KT)
                        bank = out_bank(pe, ("mod", i, c))
                        product.mark(accumulate(bank[0:2, :], [(sT[:, 2 * k:2 * k + 2], w[:, k, :]) for k in range(KT)]),
                                     ("mod", i, c))
                for t in range(NTOK):
                    norm_pe(pe, "m0", t, hbuf0[:, t % 2, :])
                for t in range(NTOK):
                    for half in range(2):
                        taken(pe, ("ht", "m0", t, half))
                for b in range(24):
                    w = weights(pe, ("w_in", b // 4)).rearrange("p (k n) -> p k n", k=KT)
                    c = (b % 4) * P
                    bank = out_bank(pe, ("proj", b))
                    product.mark(accumulate(bank, [(w[:, k, c:c + P], hT[:, k, :]) for k in range(KT)]), ("proj", b))
                w = weights(pe, ("w_in", 6)).rearrange("p (k n) -> p k n", k=KT)
                for t in range(NTOK):
                    bank = out_bank(pe, ("z", t))
                    product.mark(accumulate(bank, [(hT[:, k, tok(t)], w[:, k, :]) for k in range(KT)]), ("z", t))
                w = weights(pe, ("w_ab",))[:, 0:16 * KT].rearrange("p (k n) -> p k n", k=KT)
                bank = out_bank(pe, ("ab",))
                for t in range(NTOK):
                    last = accumulate(bank[:, 16 * t:16 * t + 16], [(hT[:, k, tok(t)], w[:, k, :]) for k in range(KT)])
                product.mark(last, ("ab",))
                pe.wait_ge(sp_dve, 2)
                bank = out_bank(pe, ("cum",))
                for j, masks in enumerate((SUM_TO, SUM_REST)):
                    for d in range(2):
                        at = 32 * j + 16 * d
                        M(bank[:, at:at + 16].rearrange("p (t h) -> p t h", t=NTOK), const(masks[d]),
                          gdec[:, :, 4 * d:4 * d + 4], start=True, stop=True)
                product.mark(M(bank[:, 64:96], const(ONES), small[:, 152:184], start=True, stop=True), ("cum",))
                for b in range(8):
                    pe.wait_ge(square_ready.sem, square_ready.count(("sq", b)))
                    bank = out_bank(pe, ("sumsq", b))
                    product.mark(M(bank, const(ONES), hT[:, b, :], start=True, stop=True), ("sumsq", b))
                pe.wait_ge(qk_ready.sem, 8)
                pe.wait_ge(silu_ready.sem, 12)
                for t in range(NTOK):
                    for n, first in (("ktok", 4), ("vtok", 8)):
                        bank = out_bank(pe, (n, t))
                        for h in range(HB):
                            last = TR(bank[:, h * P:(h + 1) * P], qkvT[:, first + h, tok(t)], const(IDENT))
                        product.mark(last, (n, t))

                def by_head(name, lhsT, rhs):
                    bank = out_bank(pe, name)
                    for h in range(HB):
                        last = M(bank[:, h * P:(h + 1) * P], lhsT(h), rhs(h), start=True, stop=True)
                    product.mark(last, name)

                def of(m, d):
                    return lambda h: m[:, d, h * P:(h + 1) * P]

                for q in range(4):
                    qT_ = lambda d: lambda h: qkvT[:, h, tok(unit(q, d))]
                    kT_ = lambda d: lambda h: qkvT[:, 4 + h, tok(unit(q, d))]
                    for d in range(2):
                        pe.wait_ge(lg_ready.sem, lg_ready.count((q, d)))
                        by_head(("D", q, d), of(lg, d), lambda h: const(SUM_REST[d]))
                    for d in range(2):
                        by_head(("KK", q, d), kT_(d), kT_(d))
                    for d in range(2):
                        by_head(("QK", q, d), qT_(d), kT_(d))
                    for d in range(2):
                        for n, m, key in (("AT", A, "A"), ("intraT", intra, "I")):
                            pe.wait_ge(ai_ready.sem, ai_ready.count((key, q, d)))
                            bank = out_bank(pe, (n, q, d))
                            for h in range(HB):
                                last = TR(bank[:, h * P:(h + 1) * P], of(m, d)(h), const(IDENT))
                            product.mark(last, (n, q, d))
                    for s in LEVELS[1:]:
                        for d in range(2):
                            pe.wait_ge(bm_ready.sem, bm_ready.count((q, d, s)))
                            pe.wait_ge(xy_ready.sem, xy_ready.count(("Y", q, d, s // 2)))
                            by_head(("P1", q, d, s), of(Bm, d), of(X, d))
                        for d in range(2):
                            taken(pe, ("P1", q, d, s))
                            by_head(("XBX", q, d, s), of(Y, d), of(P1s, d))
                            if s != LEVELS[-1]:
                                by_head(("YBY", q, d, s), of(P1s, d), of(Y, d))
                    for d in range(2):
                        pe.wait_ge(s_ready.sem, s_ready.count((q - 1, d)) if q else 1)
                        by_head(("KS", q, d), kT_(d), of(S, d))
                    for d in range(2):
                        by_head(("QS", q, d), qT_(d), of(S, d))
                    for d in range(2):
                        pe.wait_ge(r_ready.sem, r_ready.count((q, d)))
                        pe.wait_ge(xy_ready.sem, xy_ready.count(("X", q, d, LEVELS[-1])))
                        by_head(("vnew", q, d), of(X, d), of(R, d))
                    for d in range(2):
                        taken(pe, ("vnew", q, d))
                        taken(pe, ("intraT", q, d))
                        by_head(("intraV", q, d), of(intraT, d), of(vn, d))
                    for d in range(2):
                        pe.wait_ge(kd_ready.sem, kd_ready.count((q, d)))
                        by_head(("dS", q, d), of(kdK, d), of(vn, d))
                for t in range(NTOK):
                    pe.wait_ge(yb_ready.sem, yb_ready.count(t))
                    bank = out_bank(pe, ("ybT", t))
                    for h in range(HB):
                        last = TR(bank[:, h * P:(h + 1) * P], oacc[:, t, h * P:(h + 1) * P], const(IDENT))
                    product.mark(last, ("ybT", t))
                pe.wait_ge(ya_ready, 4)
                for t in range(NTOK):
                    taken(pe, ("ybT", t))
                    for c in range(2):
                        w = weights(pe, ("w_out0", c)).rearrange("p (k n) -> p k n", k=KT)
                        bank = out_bank(pe, ("out0", t, c))
                        product.mark(accumulate(bank, [(yT[:, k, tok(t)], w[:, k, :]) for k in range(KT)]), ("out0", t, c))
                for t in range(NTOK):
                    norm_pe(pe, "p0", t, hx2[:, t, :])
                peer_scores_pe(pe, "0", range(NTOK), bc_landed["keys0",])


        def peer_block(block, layer, tiles, table, turn0, tile0):
            NT = len(tiles)
            turn = lambda t, hp: (t * PAIRS + hp) + turn0
            RANK = 29
            GATES = 5

            @block.gpsimd
            def _(pool):
                with pool.Fori(0, NT) as t:
                    with pool.Fori(0, PAIRS) as hp:
                        pool_step.start(peer_base["pool"] + (t * PAIRS + hp) * 2)
                        for hh in range(2):
                            pool.wait_ge(ranked, (t + tile0) * PH + hp * 2 + hh + 1)
                            pool_step(nc.gpsimd.tensor_copy(
                                expert_cur[:, hh, :],
                                expert_all.rearrange("p h k -> p (h k)")[:, bass.ds((hp * 2 + hh) * TOPK, TOPK)]))
                            for k in range(TOPK):
                                kk = hh * TOPK + k
                                pool.wait_ge(slot_free, turn(t, hp) * PAIR + kk + 1)
                                pool_step.wait_apart()
                                nc.gpsimd.indirect_dma_start(
                                    ring[:, kk % RING, :], None, table,
                                    bass.IndirectOffsetOnAxis(ap=expert_cur[:, hh, k:k + 1], axis=0),
                                ).then_inc(slot_landed[kk % RING], 16)
                pool_step.start(peer_base["pool"] + NT * PAIRS * 2)
                peer_base["pool"] += NT * PAIRS * 2
                pool.wait_ge(slot_free, (turn0 + NT * PAIRS) * PAIR + RING)
                for s in range(2):
                    pool.dma_start(peer_gate[:, s, :], mods[layer, s, 5].partition_broadcast(P)).then_inc(
                        bc_landed[f"pg{layer}",], 16)
                if layer:
                    pool.dma_start(gain_f, T["norm_f"].partition_broadcast(P)).then_inc(bc_landed["nf",], 16)

            @block.scalar
            def _(act):
                with act.Fori(0, NT) as t:
                    act.wait_ge(sub_ready, t + tile0 + 1)
                    nc.scalar.activation(gate_tmp[:, :, :], gate_tmp[:, :, :], ACT.Exp).then_inc(gexp_ready, 1)
                    act.wait_ge(gates_ready, t + tile0 + 1)
                    with act.Fori(0, PAIRS) as hp:
                        act_step.start(peer_base["act"] + (t * PAIRS + hp) * (PAIR // GRP + PAIR))
                        nc.scalar.copy(gate_cur[:, :], gate_all.rearrange("p h k -> p (h k)")[:, bass.ds(hp * PAIR, PAIR)]
                                       ).then_inc(gates_taken, 1)
                        act.wait_ge(gates_taken, turn(t, hp) + 2)
                        for j in range(PAIR // GRP):
                            g = slice(j * GRP, (j + 1) * GRP)
                            act.wait_ge(dots_ready, turn(t, hp) * (PAIR // GRP) + j + 1)
                            act_step(nc.scalar.activation(acts[:, g], dots[:, g], ACT.Gelu))
                            act_step(*[nc.scalar.activation(coef[:, kk:kk + 1], acts[:, kk:kk + 1], ACT.Copy,
                                                            scale=gate_cur[:, kk:kk + 1])
                                       for kk in range(j * GRP, (j + 1) * GRP)])
                            for kk in range(j * GRP, (j + 1) * GRP):
                                nc.scalar.activation(diag[:, kk % RING, :], const(IDENT), ACT.Copy,
                                                     scale=coef[:, kk:kk + 1]).then_inc(diag_ready, 1)
                    act.wait_ge(slot_free, (t + tile0 + 1) * SLOTS + RING)
                    nc.scalar.copy(arena[:, bass.ds(t * D + 24576, D)].rearrange("p (a b) -> p a b", a=2),
                                   ps[:, 6:8, :]).then_inc(peer_taken, 1)
                act_step.start(peer_base["act"] + NT * PAIRS * (PAIR // GRP + PAIR))
                peer_base["act"] += NT * PAIRS * (PAIR // GRP + PAIR)
                if layer:
                    for i, t in enumerate(tiles):
                        norm_act(act, "f", t, hfin[:, i, :], (x_ready.sem, x_ready.count(("p1", t))))

            @block.tensor
            def _(pe):
                M = nc.tensor.matmul
                with pe.Fori(0, NT) as t:
                    pe.wait_ge(peer_taken, t + tile0 + 1)
                    for c in range(2):
                        M(ps[:, 6 + c, :], const(ZERO), consts[:, 0:512], start=True, stop=True)
                    with pe.Fori(0, PAIRS) as hp:
                        for kk in range(PAIR):
                            pe.wait_ge(diag_ready, turn(t, hp) * PAIR + kk + 1)
                            for c in range(2):
                                last = M(ps[:, 6 + c, :], diag[:, kk % RING, :],
                                         ring[:, kk % RING, D + 512 * c:D + 512 * c + 512],
                                         start=False, stop=True, skip_group_check=True)
                            last.then_inc(slot_free, 1)

            @block.vector
            def _(dve):
                V = nc.vector
                step = dve_step

                def rank_first(t, h):
                    step(V.tensor_copy(score_cur[:, :], arena[:, bass.ds((t * PH + h) * 256 + 16384, 256)]), apart=True)
                    both = [(p, score_cur[:, p * NKEY:(p + 1) * NKEY], score_left[:, p * NKEY:(p + 1) * NKEY])
                            for p in range(2)]
                    step(*[V.max(top_val[:, p, 0:8], cur) for p, cur, _ in both], apart=True)
                    step(*[V.max_index(top_idx[:, p, 0:8], top_val[:, p, 0:8], cur) for p, cur, _ in both],
                         *[V.match_replace(left, top_val[:, p, 0:8], cur, -3e38) for p, cur, left in both],
                         apart=True)

                def rank_second(t, h):
                    both = [(p, score_left[:, p * NKEY:(p + 1) * NKEY]) for p in range(2)]
                    step(*[V.max(top_val[:, p, 8:16], left) for p, left in both], apart=True)
                    step(*[V.max_index(top_idx[:, p, 8:16], top_val[:, p, 8:16], left) for p, left in both],
                         V.tensor_tensor(square(cand), top_val[:, 0, :].unsqueeze(2).broadcast_to((P, TOPK, TOPK)),
                                         top_val[:, 1, :].unsqueeze(1).broadcast_to((P, TOPK, TOPK)), ALU.add))

                def rank_pairs(t, h):
                    step(V.tensor_copy(top_idx_f[:, :, :], top_idx[:, :, :]), V.max(best[:, 0:8], cand[:, :]), apart=True)
                    step(V.max_index(best_pos[:, 0:8], best[:, 0:8], cand[:, :]),
                         V.match_replace(cand_left[:, :], best[:, 0:8], cand[:, :], -3e38), apart=True)
                    step(V.max(best[:, 8:16], cand_left[:, :]), apart=True)
                    step(V.max_index(best_pos[:, 8:16], best[:, 8:16], cand_left[:, :]))

                def rank_locate(t, h):
                    step(V.tensor_scalar(pos_ab[:, 0, :], best_pos[:, :], 4, None, ALU.logical_shift_right),
                         V.tensor_scalar(pos_ab[:, 1, :], best_pos[:, :], 15, None, ALU.bitwise_and))
                    step(V.tensor_copy(pos_ab_f[:, :, :], pos_ab[:, :, :]))
                    hot = (onehot, cand)
                    step(*[V.tensor_tensor(square(hot[i]), iota16[:, :].unsqueeze(1).broadcast_to((P, TOPK, TOPK)),
                                           pos_ab_f[:, i, :].unsqueeze(2).broadcast_to((P, TOPK, TOPK)), ALU.is_equal)
                           for i in range(2)])
                    step(*[V.tensor_tensor(square(hot[i]), square(hot[i]),
                                           top_idx_f[:, i, :].unsqueeze(1).broadcast_to((P, TOPK, TOPK)), ALU.mult)
                           for i in range(2)])
                    step(*[V.tensor_reduce(sel_ab[:, i, :], square(hot[i]), AX, ALU.add) for i in range(2)])
                    step(V.scalar_tensor_tensor(
                        out=expert_all.rearrange("p h k -> p (h k)")[:, bass.ds(h * TOPK, TOPK)], in0=sel_ab[:, 0, :],
                        scalar=float(NKEY), in1=sel_ab[:, 1, :], op0=ALU.mult, op1=ALU.add),
                        V.tensor_copy(best_all.rearrange("p h k -> p (h k)")[:, bass.ds(h * TOPK, TOPK)], best[:, :]))
                    dve.sem_inc(ranked, 1)

                PARTS = (rank_first, rank_second, rank_pairs, rank_locate)

                def square(m):
                    return m[:, :].rearrange("p (a b) -> p a b", a=TOPK)

                def gates(t):
                    step(V.tensor_tensor(gate_tmp[:, :, :], best_all[:, :, :],
                                         best_all[:, :, 0].unsqueeze(2).broadcast_to((P, PH, TOPK)), ALU.subtract),
                         V.tensor_copy(hx_cur[:, :], arena[:, bass.ds(t * D + 24576, D)]))
                    dve.sem_inc(sub_ready, 1)
                    dve.wait_ge(gexp_ready, t + tile0 + 1)
                    step(V.tensor_reduce(gate_sum[:, 0, :], gate_tmp[:, :, :], AX, ALU.add))
                    step(V.reciprocal(gate_sum[:, 1, :], gate_sum[:, 0, :]))
                    dve.wait_ge(gates_taken, (t + tile0) * PAIRS + 1)
                    step(V.tensor_tensor(gate_all[:, :, :], gate_tmp[:, :, :],
                                         gate_sum[:, 1, :].unsqueeze(2).broadcast_to((P, PH, TOPK)), ALU.mult))
                    dve.sem_inc(gates_ready, 1)

                def tile(t, base, last):
                    step.start(base)
                    gates(t)
                    assert step.n == GATES, step.n
                    with dve.Fori(0, PAIRS) as hp:
                        step.start(base + GATES + hp * (0 if last else 2 * RANK))
                        for kk in range(PAIR):
                            slot = kk % RING
                            dve.wait_ge(slot_landed[slot], (turn(t, hp) * (PAIR // RING) + kk // RING + 1) * 16)
                            ins = V.tensor_tensor_reduce(
                                out=ring[:, slot, 0:D], in0=ring[:, slot, 0:D], in1=hx_cur[:, :], scale=1.0, scalar=0.0,
                                op0=ALU.mult, op1=ALU.add, accum_out=dots[:, kk:kk + 1])
                            if kk % GRP == GRP - 1:
                                ins.then_inc(dots_ready, 1)
                                if not last:
                                    h = hp * 2 + kk // TOPK
                                    PARTS[kk % TOPK // GRP](t + 1, h)
                        assert last or step.n == 2 * RANK, step.n

                start = dve_step.base + dve_step.n
                with dve.Fori(0, PH) as h:
                    step.start(start + h * RANK)
                    for part in PARTS:
                        part(0, h)
                    assert step.n == RANK, step.n
                start += PH * RANK
                per_tile = GATES + PH * RANK
                with dve.Fori(0, NT - 1) as t:
                    tile(t, start + t * per_tile, False)
                start += (NT - 1) * per_tile
                tile(NT - 1, start, True)
                step.start(start + GATES)
                dve.wait_ge(bc_landed[f"pg{layer}",], 32)
                dve.wait_ge(peer_taken, tile0 + NT + 1)
                for i, t in enumerate(tiles):
                    step(V.tensor_tensor(hx2[:, i, :], hx2[:, i, :], peer_gate[:, t // 2, :], ALU.mult))
                    x_ready.mark(V.tensor_tensor(x[:, t, :], x[:, t, :], hx2[:, i, :], ALU.add), (f"p{layer}", t))
                if layer:
                    dve.wait_ge(bc_landed["nf",], 16)
                    for i, t in enumerate(tiles):
                        norm_dve(dve, step, "f", t, hfin[:, i, :], gain_f, None)

            if layer:
                @block.sync
                def _(sp):
                    for i, t in enumerate(tiles):
                        sp.wait_ge(h_ready.sem, h_ready.count(("f", t)))
                        sp.dma_start(out[tok(i), :], hfin[:, i, :]).then_inc(stored, 16)
                    sp.wait_ge(stored, 32)

        def second_block(block):
            SC = float(NOPE + ROPE) ** -0.5

            @block.sync
            def _(sp):
                load_weight(sp, ("w_kv1",), ktiles(T["od_w_in"], QL, QL + KVL + ROPE))
                load_weight(sp, ("w_q_1",), ktiles(T["od_w_in"], 0, QL))
                load_weight(sp, ("w_uq_n",), ktiles(T["uq_nope"], 0, HC * NOPE))
                load_weight(sp, ("w_uq_r",), ktiles(T["uq_rope"], 0, HC * ROPE))
                load_weight(sp, ("w_ukv",), ktiles(T["ukv"], 0, HC * (NOPE + VD)))
                for c in range(2):
                    load_weight(sp, ("w_out1", c), ktiles(T["od_w_out"], c * 512, (c + 1) * 512))
                for c in range(2):
                    load_weight(sp, ("w_q1", c), ktiles(T["p_w_q"][1], c * 512, (c + 1) * 512))

            @block.gpsimd
            def _(pool):
                for s in range(2):
                    pool.dma_start(modbc1[s], mods[1, s, 0:2].partition_broadcast(P)).then_inc(bc_landed["m1", s], 16)
                pool.dma_start(lat_gain[:, 0:QL], T["q_norm"].partition_broadcast(P)).then_inc(bc_landed["lat",], 16)
                pool.dma_start(lat_gain[:, QL:QL + KVL], T["kv_norm"].partition_broadcast(P)).then_inc(bc_landed["lat",], 16)
                pool.dma_start(rope_cs, T["rope"]).then_inc(bc_landed["lat",], 16)
                pool.wait_ge(h_ready.sem, h_ready.count(("m1", 3)))
                pool.dma_start(gate1, mods[1, 1, 2].partition_broadcast(P)).then_inc(bc_landed["g1",], 16)
                pool.dma_start(keysB[:, :, :], T["keys"][1]).then_inc(bc_landed["keys1",], 16)
                pool.wait_ge(product.sem, product.count(("cqT", 3)))
                pool.dma_start(modbcp[0], mods[1, 1, 3:5].partition_broadcast(P)).then_inc(bc_landed["p1",], 16)

            @block.scalar
            def _(act):
                A_ = nc.scalar.activation
                for t in range(NTOK):
                    first = ((x_ready.sem, x_ready.count(("p0", 3))) if t < 2
                             else (product.sem, product.count(("ht", "m1", t - 2, 1))))
                    norm_act(act, "m1", t, hbuf1[:, t % 2, :], first)
                    if t:
                        norm_take(act, nc.scalar.copy, "m1", t - 1, 0, t - 1)
                norm_take(act, nc.scalar.copy, "m1", 3, 0, 3)
                junk = area(16384, QL)
                for t in range(NTOK):
                    for name, lo, n, i in (("lkv", QL, KVL, 0), ("lq", 0, QL, 1)):
                        if name == "lq" and t < 2:
                            continue
                        bank = in_bank(act, (name, t))
                        col = slice(2 * t + i, 2 * t + i + 1)
                        act_step(A_(junk[:, 0:n], bank[:, 0:n], ACT.Square, accum_out=lssq[:, col]))
                        act_step(A_(lrst[:, col], lssq[:, col], ACT.Sqrt, bias=eps_col, scale=1.0 / n))
                        width = KVL + ROPE if name == "lkv" else QL
                        free_bank(nc.scalar.copy(lat[:, t, lo:lo + width], bank[:, 0:width]), (name, t))
                        taken(act, (name, t))
                    act.sem_inc(lsq_ready, 1)
                for t in range(NTOK):
                    bank = in_bank(act, ("ckvT", t))
                    act_step(nc.scalar.copy(krT[0:ROPE, tok(t)], bank[0:ROPE, 256:384]))
                    free_bank(nc.scalar.copy(ckvT[:, :, tok(t)], bank[:, 0:256].rearrange("p (k t) -> p k t", k=2)),
                              ("ckvT", t))
                    if t >= 2:
                        bank = in_bank(act, ("cqT", t))
                        free_bank(nc.scalar.copy(cqT[:, :, tok(t - 2)], bank[:, 0:384].rearrange("p (k t) -> p k t", k=3)),
                                  ("cqT", t))
                for h in range(HC):
                    free_bank(nc.scalar.copy(qnT[:, h, :], in_bank(act, ("qn", h))[:, 0:256]), ("qn", h))
                for t in (2, 3):
                    for g in range(2):
                        bank = in_bank(act, ("qrT", t, g))
                        free_bank(nc.scalar.copy(qrT[0:ROPE, 4 * g:4 * g + 4, tok(t - 2)],
                                                 bank[0:ROPE, :].rearrange("p (h t) -> p h t", h=4)), ("qrT", t, g))
                for h in range(HC):
                    if h % 2 == 0:
                        free_bank(nc.scalar.copy(knT[:, h, :], in_bank(act, ("kn", h))), ("kn", h))
                for t in range(NTOK):
                    free_bank(nc.scalar.copy(vatt[:, t, 0:512], in_bank(act, ("v", t, 0))), ("v", t, 0))

                def turn_probs(u):
                    free_bank(nc.scalar.copy(probT[:, u % 2, :], in_bank(act, ("pT", u))), ("pT", u))

                for u in range(2 * HC):
                    bank = in_bank(act, ("sc", u))
                    act.wait_ge(nmax_ready.sem, nmax_ready.count(u))
                    if u >= 2:
                        act.wait_ge(product.sem, product.count(("pT", u - 2)))
                    free_bank(A_(prob[:, u % 2, :], bank, ACT.Exp, bias=nsmax[:, u:u + 1], scale=SC,
                                 accum_out=ssum[:, u:u + 1]), ("sc", u))
                    if u:
                        turn_probs(u - 1)
                turn_probs(2 * HC - 1)
                for i, t in enumerate((2, 3)):
                    norm_act(act, "p1", t, hx2[:, i, :], (x_ready.sem, x_ready.count(("m1", t))))
                    if i:
                        norm_take(act, nc.scalar.copy, "p1", t - 1, 0, i - 1)
                norm_take(act, nc.scalar.copy, "p1", 3, 0, 1)
                for h in range(PH):
                    free_bank(nc.scalar.copy(qT[:, h, 0:256], in_bank(act, ("q1", h))[:, 0:256]), ("q1", h))
                for i, t in enumerate((2, 3)):
                    for j in range(0, 4, 2):
                        bank = in_bank(act, ("s1", t, j))
                        free_bank(nc.scalar.copy(score[:, i, 2 * j:2 * j + 2, :],
                                                 bank.rearrange("p (h n) -> p h n", h=2)), ("s1", t, j))

            @block.vector
            def _(dve):
                V = nc.vector
                step = dve_step

                def rope(dst, src, t, nh, last_read):
                    s4, d4 = (v.rearrange("p (h a b n) -> p h a b n", h=nh, a=2, b=2) for v in (src, dst))
                    cs = [rope_cs[:, t, i].unsqueeze(1).broadcast_to((P, nh, 2, 16)) for i in range(2)]
                    tmps = [rtmp[:, i, 0:nh * 32].rearrange("p (h a n) -> p h a n", h=nh, a=2) for i in range(4)]
                    parts = [(0, 0), (1, 1), (1, 0), (0, 1)]
                    ins = [V.tensor_tensor(tmps[i], s4[:, :, :, b, :], cs[c], ALU.mult)
                           for i, (b, c) in enumerate(parts)]
                    if last_read is None:
                        step(*ins)
                    else:
                        free_bank(ins[-1], last_read)
                        step(*ins[:-1])
                        taken(dve, last_read)
                    return (V.tensor_tensor(d4[:, :, :, 0, :], tmps[0], tmps[1], ALU.subtract),
                            V.tensor_tensor(d4[:, :, :, 1, :], tmps[2], tmps[3], ALU.add))

                for t in range(NTOK):
                    if t % 2 == 0:
                        dve.wait_ge(bc_landed["m1", t // 2], 16)
                    bc = modbc1[t // 2]
                    norm_dve(dve, step, "m1", t, hbuf1[:, t % 2, :], bc[:, 1, :], bc[:, 0, :])
                    if t:
                        norm_take(dve, V.tensor_copy, "m1", t - 1, 1, t - 1)
                norm_take(dve, V.tensor_copy, "m1", 3, 1, 3)
                dve.wait_ge(bc_landed["lat",], 48)
                for t in range(NTOK):
                    dve.wait_ge(lsq_ready, t + 1)
                    for i, lo, n in ((0, QL, KVL), (1, 0, QL)):
                        if i and t < 2:
                            continue
                        r = lrst[:, 2 * t + i:2 * t + i + 1]
                        step(V.reciprocal(r, r))
                        step(V.scalar_tensor_tensor(out=lat[:, t, lo:lo + n], in0=lat[:, t, lo:lo + n], scalar=r,
                                                    in1=lat_gain[:, lo:lo + n], op0=ALU.mult, op1=ALU.mult))
                    if t >= 2:
                        kr = lat[:, t, QL + KVL:QL + KVL + ROPE]
                        step(*rope(kr, kr, t - 2, 1, None))
                    dve.sem_inc(lat_ready.sem, 1)
                for t in (2, 3):
                    step(*rope(qrope[:, t - 2, :], in_bank(dve, ("qr", t)), t - 2, HC, ("qr", t)))
                    dve.sem_inc(qr_ready.sem, 1)
                for h in range(HC):
                    if h % 2:
                        free_bank(V.tensor_copy(knT[:, h, :], in_bank(dve, ("kn", h))), ("kn", h))
                for t in range(NTOK):
                    free_bank(V.tensor_copy(vatt[:, t, 512:1024], in_bank(dve, ("v", t, 1))), ("v", t, 1))

                def take_o(u):
                    free_bank(V.tensor_copy(oT[:, u // 2, tok(u % 2)], in_bank(dve, ("oT", u))[:, 0:P]), ("oT", u))

                for u in range(2 * HC):
                    bank = in_bank(dve, ("sc", u))
                    c = slice(u, u + 1)
                    step(V.tensor_reduce(smax[:, c], bank, AX, ALU.max))
                    nmax_ready.mark(V.tensor_scalar(nsmax[:, c], smax[:, c], -SC, None, ALU.mult), u)
                    taken(dve, ("sc", u))
                    step(V.reciprocal(srec[:, c], ssum[:, c]))
                    prob_ready.mark(V.tensor_scalar(prob[:, u % 2, :], prob[:, u % 2, :], srec[:, c], None, ALU.mult), u)
                    if u:
                        take_o(u - 1)
                take_o(2 * HC - 1)
                residual(dve, step, "out1", "m1", (2, 3), lambda t: gate1, bc_landed["g1",], rtmp.rearrange(
                    "p (a b) n -> p a (b n)", a=2))
                dve.wait_ge(bc_landed["p1",], 16)
                for i, t in enumerate((2, 3)):
                    norm_dve(dve, step, "p1", t, hx2[:, i, :], modbcp[0][:, 1, :], modbcp[0][:, 0, :])
                    if i:
                        norm_take(dve, V.tensor_copy, "p1", t - 1, 1, i - 1)
                norm_take(dve, V.tensor_copy, "p1", 3, 1, 1)
                for i, t in enumerate((2, 3)):
                    for j in range(1, 4, 2):
                        bank = in_bank(dve, ("s1", t, j))
                        free_bank(V.tensor_copy(score[:, i, 2 * j:2 * j + 2, :],
                                                bank.rearrange("p (h n) -> p h n", h=2)), ("s1", t, j))

            @block.tensor
            def _(pe):
                M, TR = nc.tensor.matmul, nc.tensor.transpose

                def accumulate(dst, pairs):
                    for i, (l, r) in enumerate(pairs):
                        last = M(dst, l, r, start=(i == 0), stop=(i == len(pairs) - 1))
                    return last

                for t in range(NTOK):
                    norm_pe(pe, "m1", t, hbuf1[:, t % 2, :])
                for t in range(NTOK):
                    for half in range(2):
                        taken(pe, ("ht", "m1", t, half))
                for t in range(NTOK):
                    for name, key, n in (("lkv", "w_kv1", KVL + ROPE), ("lq", "w_q_1", QL)):
                        if name == "lq" and t < 2:
                            continue
                        w = weights(pe, (key,))[:, 0:KT * n].rearrange("p (k n) -> p k n", k=KT)
                        bank = out_bank(pe, (name, t))
                        product.mark(accumulate(bank[:, 0:n], [(hT[:, k, tok(t)], w[:, k, :]) for k in range(KT)]),
                                     (name, t))
                for t in range(NTOK):
                    pe.wait_ge(lat_ready.sem, t + 1)
                    bank = out_bank(pe, ("ckvT", t))
                    for k in range(2):
                        TR(bank[:, k * P:(k + 1) * P], lat[:, t, QL + k * P:QL + (k + 1) * P], const(IDENT))
                    product.mark(TR(bank[0:ROPE, 256:384], lat[:, t, QL + KVL:QL + KVL + ROPE], const(IDENT)),
                                 ("ckvT", t))
                    if t >= 2:
                        bank = out_bank(pe, ("cqT", t))
                        for k in range(3):
                            last = TR(bank[:, k * P:(k + 1) * P], lat[:, t, k * P:(k + 1) * P], const(IDENT))
                        product.mark(last, ("cqT", t))
                for t in range(NTOK):
                    taken(pe, ("ckvT", t))
                for t in (2, 3):
                    taken(pe, ("cqT", t))
                w = weights(pe, ("w_uq_n",))[:, 0:3 * D].rearrange("p (k n) -> p k n", k=3)
                for h in range(HC):
                    bank = out_bank(pe, ("qn", h))
                    product.mark(accumulate(bank[:, 0:256], [(w[:, k, h * P:(h + 1) * P], cqT[:, k, :])
                                                             for k in range(3)]), ("qn", h))
                w = weights(pe, ("w_uq_r",))[:, 0:3 * 512].rearrange("p (k n) -> p k n", k=3)
                for t in (2, 3):
                    bank = out_bank(pe, ("qr", t))
                    product.mark(accumulate(bank, [(cqT[:, k, tok(t - 2)], w[:, k, :]) for k in range(3)]), ("qr", t))
                for t in (2, 3):
                    pe.wait_ge(qr_ready.sem, t - 1)
                    for g in range(2):
                        bank = out_bank(pe, ("qrT", t, g))
                        for j in range(4):
                            h = 4 * g + j
                            last = TR(bank[0:ROPE, j * P:(j + 1) * P], qrope[:, t - 2, h * ROPE:(h + 1) * ROPE],
                                      const(IDENT))
                        product.mark(last, ("qrT", t, g))
                w = weights(pe, ("w_ukv",)).rearrange("p (k n) -> p k n", k=2)
                for h in range(HC):
                    bank = out_bank(pe, ("kn", h))
                    product.mark(accumulate(bank, [(w[:, k, h * P:(h + 1) * P], ckvT[:, k, :]) for k in range(2)]),
                                 ("kn", h))
                for t in range(NTOK):
                    for c in range(2):
                        bank = out_bank(pe, ("v", t, c))
                        product.mark(accumulate(bank, [(ckvT[:, k, tok(t)], w[:, k, D + 512 * c:D + 512 * c + 512])
                                                       for k in range(2)]), ("v", t, c))
                for h in range(HC):
                    taken(pe, ("kn", h))
                    taken(pe, ("qn", h))
                for t in (2, 3):
                    for g in range(2):
                        taken(pe, ("qrT", t, g))
                for t in range(NTOK):
                    for c in range(2):
                        taken(pe, ("v", t, c))

                def attend(u):
                    h = u // 2
                    pe.wait_ge(prob_ready.sem, prob_ready.count(u))
                    bank = out_bank(pe, ("pT", u))
                    for k in range(4):
                        last = TR(bank[:, k * P:(k + 1) * P], prob[:, u % 2, k * P:(k + 1) * P], const(IDENT))
                    product.mark(last, ("pT", u))
                    taken(pe, ("pT", u))
                    bank = out_bank(pe, ("oT", u))
                    product.mark(accumulate(bank[:, 0:P], [(vatt[:, k, h * P:(h + 1) * P],
                                                            probT[:, u % 2, k * P:(k + 1) * P]) for k in range(4)]),
                                 ("oT", u))

                for u in range(2 * HC):
                    h = u // 2
                    bank = out_bank(pe, ("sc", u))
                    product.mark(accumulate(bank, [(qnT[:, h, tok(u % 2)], knT[:, h, :]),
                                                   (qrT[0:ROPE, h, tok(u % 2)], krT[0:ROPE, :])]), ("sc", u))
                    if u:
                        attend(u - 1)
                attend(2 * HC - 1)
                for u in range(2 * HC):
                    taken(pe, ("oT", u))
                for i, t in enumerate((2, 3)):
                    for c in range(2):
                        w = weights(pe, ("w_out1", c)).rearrange("p (k n) -> p k n", k=KT)
                        bank = out_bank(pe, ("out1", t, c))
                        product.mark(accumulate(bank, [(oT[:, k, tok(i)], w[:, k, :]) for k in range(KT)]),
                                     ("out1", t, c))
                for i, t in enumerate((2, 3)):
                    norm_pe(pe, "p1", t, hx2[:, i, :])
                peer_scores_pe(pe, "1", (2, 3), bc_landed["keys1",])

        peer_base = {"pool": 0, "act": 0}
        with nc.Block() as block:
            first_block(block)
        peer_base["act"] = act_step.n
        with nc.Block() as block:
            peer_block(block, 0, range(NTOK), T["experts0"], 0, 0)
        with nc.Block() as block:
            second_block(block)
        peer_base["act"] = act_step.base + act_step.n
        with nc.Block() as block:
            peer_block(block, 1, (2, 3), T["experts1"], NTOK * PAIRS, NTOK)


def constants():
    r, c = np.mgrid[0:P, 0:P]
    mats = [r == c, r >= 0, r <= c, r > c, r >= c, r < c, r < 0]
    lower = [(r // s == c // s + 1) & (c // s % 2 == 0) for s in LEVELS]
    mats += lower + [m.T for m in lower]
    consts = np.concatenate([m.astype(np.float32) for m in mats], axis=1)
    iota = np.tile(np.arange(TOPK, dtype=np.float32), (P, 1))
    n = ROPE // 4
    freqs = (np.float32(10000.0) ** (-np.arange(n, dtype=np.float32) / np.float32(n))).astype(np.float32)
    t = np.arange(2 * P)
    ang = np.stack([(t // GRID_W).astype(np.float32)[:, None] * freqs, (t % GRID_W).astype(np.float32)[:, None] * freqs], 1)
    rope = np.stack([np.cos(ang), np.sin(ang)], 1).astype(np.float32)
    rope = rope.reshape(2, P, 2, 2, n).transpose(1, 0, 2, 3, 4)
    return consts, iota, np.ascontiguousarray(rope)


def kernel(**inputs):
    import concourse.bacc as bacc
    from concourse.bass_utils import run_bass_kernel_spmd

    a = {k: np.asarray(v) for k, v in inputs.items()}
    consts, iota, rope = constants()
    uq = a["od_w_uq"][0].reshape(QL, HC, NOPE + ROPE)
    ukv = a["od_w_ukv"][0].reshape(KVL, HC, NOPE + VD)
    keys = np.zeros((2, P, PH, 2, NKEY), np.float32)
    for p in range(2):
        keys[:, 64 * p:64 * p + 64, :, p, :] = a["p_keys"][:, :, p].transpose(0, 3, 1, 2)
    arrays = {
        "x": a["x"][0], "ctx": a["ctx"][0],
        "c_cols": np.stack([a["c_ctx"].reshape(KT, P), a["c"][0].reshape(KT, P)], 2).transpose(1, 0, 2).reshape(P, 2 * KT),
        "w_mod": a["w_mod"], "b_mod": a["b_mod"].reshape(2, 6, D),
        "norms": np.stack([a["norm1"], a["norm2"]], 1)[None],
        "ev_w_in": a["ev_w_in"][0],
        "conv_w": np.concatenate([a["ev_a_conv"][0], a["ev_qkv_conv"][0]], 1).reshape(3, 16, P).transpose(2, 1, 0),
        "a_log": a["ev_a_log"].reshape(8), "dt_bias": a["ev_dt_bias"].reshape(8),
        "o_norm": a["ev_o_norm"][0], "ev_w_out": a["ev_w_out"][0],
        "od_w_in": a["od_w_in"][0], "q_norm": a["od_q_norm"][0], "kv_norm": a["od_kv_norm"][0],
        "uq_nope": uq[:, :, :NOPE].reshape(QL, -1), "uq_rope": uq[:, :, NOPE:].reshape(QL, -1),
        "ukv": np.concatenate([ukv[:, :, :NOPE].reshape(KVL, -1), ukv[:, :, NOPE:].reshape(KVL, -1)], 1),
        "od_w_out": a["od_w_out"][0], "p_w_q": a["p_w_q"], "keys": keys.reshape(2, P, PH, 2 * NKEY),
        "experts0": np.concatenate([a["p_u"][0], a["p_v"][0]], 1),
        "experts1": np.concatenate([a["p_u"][1], a["p_v"][1]], 1),
        "norm_f": a["norm_f"], "consts": consts, "iota16": iota, "rope": rope,
    }
    nc = bacc.Bacc("TRN2", target_bir_lowering=False, num_devices=1)
    feed, T = {}, {}
    for name, v in arrays.items():
        feed[f"in_{name}"] = np.ascontiguousarray(v)
        T[name] = nc.dram_tensor(f"in_{name}", v.shape, F32, kind="ExternalInput").ap()
    out = nc.dram_tensor("out", (2 * P, D), F32, kind="ExternalOutput").ap()
    build(nc, T, out)
    r = run_bass_kernel_spmd(nc, [feed], core_ids=[0])
    return r.results[0]["out"].reshape(1, 2 * P, D)
```

```python
from contextlib import ExitStack

import numpy as np
import concourse.bass as bass
from concourse import mybir

F32 = mybir.dt.float32
U32 = mybir.dt.uint32
ALU = mybir.AluOpType
ACT = mybir.ActivationFunctionType
AX = mybir.AxisListType.X

P = 128
D = 1024
KT = D // P
NTOK = 4
EPS = 1e-6
HB = 4
DK = 128
HC = 8
NOPE, ROPE, VD = 128, 64, 128
QL, KVL = 384, 256
PH = 8
NKEY = 128
TOPK = 16
GRID_W = 64
LEVELS = [1, 2, 4, 8, 16, 32, 64]

IDENT, ONES, LE, GT, GE, LT, ZERO = range(7)
LOWER = {s: 7 + i for i, s in enumerate(LEVELS)}
UPPER = {s: 14 + i for i, s in enumerate(LEVELS)}
NCONST = 21

RING = 8
GRP = 2
SLOTS = PH * TOPK
NBANK = 6


class Order:

    def __init__(self, sem, events):
        self.sem = sem
        self.events = list(events)
        self.at = {e: i + 1 for i, e in enumerate(self.events)}
        assert len(self.at) == len(self.events)
        self.done = 0

    def count(self, event):
        return self.at[event]

    def mark(self, ins, event):
        assert self.events[self.done] == event, (self.events[self.done], event)
        self.done += 1
        ins.then_inc(self.sem, 1)


class Steps:

    def __init__(self, eng, sem, waited):
        self.eng, self.sem, self.waited, self.base, self.n = eng, sem, waited, 0, 0

    def start(self, base):
        self.base, self.n = base, 0

    def __call__(self, *instructions, apart=False):
        for ins in instructions:
            ins.then_inc(self.sem, 1)
            self.n += 1
        self.eng.wait_ge(self.sem, self.base + self.n)
        if apart:
            self.wait_apart()

    def wait_apart(self):
        self.eng.sem_inc(self.waited, 1)


def mixer_groups(s):
    tiles = (2 * s, 2 * s + 1)
    g = [(n, t) for t in tiles for n in ("ktok", "vtok")]
    for q in tiles:
        g += [(n, q, d) for n in ("D", "KK", "AT", "QK") for d in range(2)]
        for lv in LEVELS[1:]:
            g += [("P1", q, d, lv) for d in range(2)]
            if lv == LEVELS[1]:
                g += [("intraT", q, d) for d in range(2)]
            if lv == LEVELS[-1]:
                g += [(n, q, d) for n in ("KS", "QS") for d in range(2)]
            for d in range(2):
                g += [("XBX", q, d, lv)] + ([("YBY", q, d, lv)] if lv != LEVELS[-1] else [])
        g += [(n, q, d) for n in ("vnew", "intraV", "dS") for d in range(2)]
    g += [("ybT", t) for t in tiles] + [("out0", t, c) for t in tiles for c in range(2)]
    g += [("ht", "p0", t, h) for t in tiles for h in range(2)]
    for j in range(5):
        if j < 4:
            g += [("q0", s, 2 * j), ("q0", s, 2 * j + 1)]
        if j:
            g += [("s0", t, j - 1) for t in tiles]
    return g


def group_names():
    first = [("mod", i, c) for i in range(2) for c in range(12)]
    first += [("ht", "m0", t, h) for t in range(NTOK) for h in range(2)]
    first += [("proj", b) for b in range(24)]
    first += [("z", t) for t in range(NTOK)] + [("ab",), ("cum",)]
    first += [("sumsq", b) for b in range(8)]
    first += mixer_groups(0) + mixer_groups(1)
    second = [("ht", "m1", t, h) for t in range(NTOK) for h in range(2)]
    second += [(n, t) for t in range(NTOK) for n in (("lkv", "lq") if t >= 2 else ("lkv",))]
    second += [(n, t) for t in range(NTOK) for n in (("ckvT", "cqT") if t >= 2 else ("ckvT",))]
    second += [("qn", h) for h in range(HC)] + [("qr", t) for t in (2, 3)]
    second += [("qrT", t, g) for t in (2, 3) for g in range(2)]
    second += [("kn", h) for h in range(HC)] + [("v", t, h) for t in range(NTOK) for h in range(2)]
    for u in range(2 * HC):
        second += [("sc", u)]
        if u:
            second += [("pT", u - 1), ("oT", u - 1)]
    second += [("pT", 2 * HC - 1), ("oT", 2 * HC - 1)]
    second += [("out1", t, h) for t in (2, 3) for h in range(2)]
    second += [("ht", "p1", t, h) for t in (2, 3) for h in range(2)]
    second += [("q1", h) for h in range(PH)] + [("s1", t, j) for t in (2, 3) for j in range(4)]
    return first + second


def weight_loads():
    loads = [(("mod", i, c), ("mod", i, c)) for i in range(2) for c in range(12)]
    loads += [(("w_in", c), ("proj", 4 * c + 3)) for c in range(6)]
    loads += [(("w_in", 6), ("z", 3)), (("w_ab",), ("ab",))]
    loads += [(("w_out0", 0, c), ("out0", 1, c)) for c in range(2)]
    loads += [(("w_q0", 0, c), ("q0", 0, 4 * c + 3)) for c in range(2)]
    loads = [(n, last, i % 3) for i, (n, last) in enumerate(loads)]
    loads += [(("w_out0", 1, c), ("out0", 3, c), c) for c in range(2)]
    loads += [(("w_q0", 1, c), ("q0", 1, 4 * c + 3), c) for c in range(2)]
    second = [(("w_kv1",), ("lkv", 3)), (("w_q_1",), ("lq", 3))]
    second += [(("w_uq_n",), ("qn", 7)), (("w_uq_r",), ("qr", 3)), (("w_ukv",), ("v", 3, 1))]
    second += [(("w_out1", c), ("out1", 3, c)) for c in range(2)]
    second += [(("w_q1", c), ("q1", 4 * c + 3)) for c in range(2)]
    return loads + [(n, last, i % 3) for i, (n, last) in enumerate(second)]


def build(nc, T, out):
    with ExitStack() as ctx:
        def sb(name, shape, dt=F32):
            return ctx.enter_context(nc.sbuf_tensor(name, shape, dt))

        def sem(name):
            return ctx.enter_context(nc.semaphore(name))

        consts = sb("consts", [P, NCONST * P])
        x = sb("x", [P, NTOK, D])
        wring = sb("wring", [P, 3 * 4096])
        arena = sb("arena", [P, 28672])
        small = sb("small", [P, 1024])
        conv_w = sb("conv_w", [P, 16, 3])
        hx_cur = sb("hx_cur", [P, D])
        score_cur = sb("score_cur", [P, 2 * NKEY])
        score_left = sb("score_left", [P, 2 * NKEY])
        cand = sb("cand", [P, TOPK * TOPK])
        cand_left = sb("cand_left", [P, TOPK * TOPK])
        onehot = sb("onehot", [P, TOPK * TOPK])
        iota16 = sb("iota16", [P, TOPK])
        top_val = sb("top_val", [P, 2, TOPK])
        top_idx = sb("top_idx", [P, 2, TOPK], U32)
        top_idx_f = sb("top_idx_f", [P, 2, TOPK])
        best = sb("best", [P, TOPK])
        best_pos = sb("best_pos", [P, TOPK], U32)
        pos_ab = sb("pos_ab", [P, 2, TOPK], U32)
        pos_ab_f = sb("pos_ab_f", [P, 2, TOPK])
        sel_ab = sb("sel_ab", [P, 2, TOPK])
        gate_stat = sb("gate_stat", [P, 3])
        gate_exp = sb("gate_exp", [P, TOPK])
        expert_cur = sb("expert_cur", [P, 2, TOPK], U32)
        gate_cur = sb("gate_cur", [P, 2, TOPK])
        dots = sb("dots", [P, 2, TOPK])
        acts = sb("acts", [P, 2, TOPK])
        coef = sb("coef", [P, 2, TOPK])
        diag = sb("diag", [P, RING, P])
        ps = ctx.enter_context(nc.psum_tensor("ps", [P, 8, 512], F32))
        mods = nc.dram_tensor("mods", (2, 2, 6, D), F32, kind="Internal").ap()

        def const(i):
            return consts[:, i * P:(i + 1) * P]

        def area(at, *shape, of=None):
            n = int(np.prod(shape))
            flat = arena if of is None else of
            assert at + n <= flat.shape[1]
            a = flat[:, at:at + n]
            if len(shape) == 1:
                return a
            names = "abcd"[:len(shape)]
            return a.rearrange(f"p ({' '.join(names)}) -> p {' '.join(names)}",
                               **{k: s for k, s in zip(names[:-1], shape)})

        mod_rows = [area(6144 * i, 6, D)[0:2] for i in range(2)]
        norm_rows = area(12288, 2, 2, D)[0:2]
        hT = area(0, KT, 512)
        bgcg = area(4096, 8, 512)
        STREAM = 12288

        def both_streams(at):
            low = at % 4096
            start = at - low
            return arena[:, start:start + STREAM + 4096].rearrange("p (s r) -> p s r", r=4096)[
                :, 0:4:3, low:low + 256]

        def qkv_block(b):
            return both_streams(8192 + 256 * b)

        def ya_block(b):
            return both_streams(14336 + 256 * b)

        conv_in = area(12288, 4, 512)
        hbuf0 = area(16384, 2, D)
        modbc0 = [area(18432, 2, D), area(24576, 2, D)]

        def mixer_memory(s):
            base, flat = (0, arena) if s == 0 else (0, wring)
            names = ("lg", "A", "gam", "intra", "intraT", "X", "Y", "Bm")
            m = {n: area(base + 1024 * i, 2, 512, of=flat) for i, n in enumerate(names)}
            shift = STREAM * s
            m["qkv"] = area(8192 + shift, 12, 256)
            m["z"] = area(11264 + shift, 2, 512)
            m["ya"] = area(14336 + shift, 4, 256)
            m["score"] = area(16384 + 4096 * s, 2, PH, 256)
            m["hx2"] = area(24576 + 2048 * s, 2, D)
            if s == 0:
                m |= {"yb": area(15360, 4, 256), "ktok": area(12288, 2, 512), "vtok": area(13312, 2, 512),
                      "P1s": area(16384, 2, 512), "oacc": area(18432, 2, 512), "gate": area(19456, D),
                      "rows": area(17408, 2, 512), "modbc": area(0, 2, D), "hT": area(2048, KT, 256),
                      "qT": area(4096, PH, 256), "keys": area(6144, PH, 256), "osq": area(0, 2, 512)}
            else:
                w = lambda at, *shape: area(at, *shape, of=wring)
                m |= {"yb": area(20480, 4, 256), "ktok": w(10240, 2, 512), "vtok": w(11264, 2, 512),
                      "P1s": w(8192, 2, 512), "oacc": w(9216, 2, 512), "gate": w(8192, D),
                      "rows": w(9216, 2, 512), "modbc": w(10240, 2, D), "hT": w(8192, KT, 256),
                      "qT": area(16384, PH, 256), "keys": w(10240, PH, 256), "osq": w(0, 2, 512)}
            m |= {"R": m["gam"], "vn": m["lg"], "tmp": m["intra"], "kdK": m["Bm"]}
            return m

        MEM = [mixer_memory(s) for s in range(2)]
        S = area(27648, 2, 512)
        qT = area(4096, PH, 512)
        keysB = area(8192, PH, 256)
        modbcp = area(10240, 2, D)
        score = area(16384, NTOK, PH, 256)
        hx2 = area(24576, NTOK, D)
        ring = area(0, RING, 2 * D)
        peer_gate = area(0, 2, D)
        hbuf1 = area(4096, 2, D)
        modbc1 = [area(6144, 2, D), area(8192, 2, D)]
        lat = area(10240, NTOK, 704)
        cqT = area(13056, 3, 256)
        ckvT = area(13824, 2, 512)
        krT = area(14848, 512)
        lat_gain = area(15360, 640)
        rope_cs = area(16000, 2, 2, 2, 16)
        knT = area(16384, HC, 512)
        vatt = area(20480, NTOK, D)
        qnT = area(24576, HC, 256)
        qrope = area(26624, 2, 512)
        rtmp = area(27648, 4, 256)
        qrT = area(0, HC, 256)
        prob = area(2048, 2, 512)
        probT = area(3072, 2, 512)
        oT = area(4096, HC, 256)
        gate1 = area(6144, D)
        kdup = area(7168, 128)
        hfin = area(2048, 2, D)
        gain_f = area(4096, D)

        sT = small[:, 0:16]
        ab = small[:, 16:80].rearrange("p (t c) -> p t c", t=NTOK)
        ssq = small[:, 80:104]
        rstd = small[:, 104:128]
        alog = small[:, 128:136]
        dtb = small[:, 136:144]
        nexpa = small[:, 144:152]
        gdec = small[:, 152:184].rearrange("p (t c) -> p t c", t=NTOK)
        g1 = small[:, 184:216].rearrange("p (t c) -> p t c", t=NTOK)
        g2 = small[:, 216:248].rearrange("p (t c) -> p t c", t=NTOK)
        beta = small[:, 248:280].rearrange("p (t c) -> p t c", t=NTOK)
        expo = small[:, 280:376]
        edec = expo[:, 0:32].rearrange("p (d t h) -> p d t h", d=2, t=NTOK)
        erest = expo[:, 32:64].rearrange("p (d t h) -> p d t h", d=2, t=NTOK)
        eall = expo[:, 64:96].rearrange("p (t d h) -> p t d h", t=NTOK, d=2)
        ossq = small[:, 376:392]
        orst = small[:, 392:408]
        lssq = small[:, 408:416]
        lrst = small[:, 416:424]
        smax = small[:, 424:440]
        nsmax = small[:, 440:456]
        ssum = small[:, 456:472]
        srec = small[:, 472:488]
        sTin = small[:, 488:504]
        eps_col = small[:, 504:505]
        ogain = small[:, 512:640]

        GROUPS = group_names()
        product = Order(sem("product_done"), GROUPS)
        bank_free = [sem(f"bank_free{b}") for b in range(NBANK)]
        w_landed = [sem(f"w_landed{i}") for i in range(3)]
        x_landed = sem("x_landed")
        consts_landed = sem("consts_landed")
        row_landed = [sem(f"mod_bias_landed{i}") for i in range(2)]
        rows_stored = sem("mod_rows_stored")
        bc_names = [("m0", 0), ("m0", 1), ("g0", 0), ("g0", 1), ("p0", 0), ("p0", 1), ("keys0", 0), ("keys0", 1),
                    ("m1", 0), ("m1", 1), ("lat",), ("g1",), ("p1",), ("keys1",), ("pg0",), ("pg1",), ("nf",)]
        bc_landed = {n: sem("landed_" + "_".join(map(str, n))) for n in bc_names}
        act_steps = sem("act_steps")
        dve_steps = sem("dve_steps")
        pool_steps = sem("pool_steps")
        norm_events = ([("m0", t) for t in range(NTOK)] + [("p0", t) for t in range(NTOK)]
                       + [("m1", t) for t in range(NTOK)] + [("p1", t) for t in (2, 3)]
                       + [("f", t) for t in (2, 3)])
        ssq_ready = Order(sem("ssq_ready"), norm_events)
        h_ready = Order(sem("h_ready"), norm_events)
        silu_c = sem("silu_c_ready")
        rows_ready = sem("mod_rows_ready")
        xa_conv = Order(sem("xa_scaled"), [("xa", b) for b in range(4)])
        u_ready = Order(sem("gated_input_ready"), [("u", b) for b in range(4)])
        conv_ready = Order(sem("conv_ready"), [("conv", b) for b in range(12)])
        centre_ready = Order(sem("centre_tap_ready"), list(range(12)))
        eps_ready = sem("eps_ready")
        silu_ready = Order(sem("qkv_silu_ready"), [("silu", b) for b in range(12)])
        square_ready = Order(sem("qk_square_ready"), [("sq", b) for b in range(8)])
        qk_ready = Order(sem("qk_normed"), [("qk", b) for b in range(8)])
        ya_ready = sem("y_a_ready")
        sp_act = sem("softplus_act")
        sp_dve = sem("softplus_dve")
        pq = [(q, d) for q in range(4) for d in range(2)]
        lg_ready = Order(sem("lg_ready"), pq)
        ai_ready = Order(sem("a_intra_ready"), [(n, q, d) for q in range(4) for n in "AI" for d in range(2)])
        xy_ready = Order(sem("xy_ready"), [(n, q, d, s) for q in range(4) for s in LEVELS for d in range(2)
                                           for n in ("XY" if s != LEVELS[-1] else "X")])
        bm_ready = Order(sem("level_ready"), [(q, d, s) for q in range(4) for s in LEVELS[1:] for d in range(2)])
        kd_ready = Order(sem("kd_ready"), pq)
        r_ready = Order(sem("r_ready"), pq)
        s_ready = Order(sem("state_ready"), ["zero"] + pq)
        osq_ready = Order(sem("o_square_ready"), list(range(NTOK)))
        yb_ready = Order(sem("y_b_ready"), list(range(NTOK)))
        x_ready = Order(sem("x_ready"), [("m0", t) for t in range(NTOK)] + [("p0", t) for t in range(NTOK)]
                        + [("m1", t) for t in (2, 3)] + [("p1", t) for t in (2, 3)])
        lsq_ready = sem("latent_square_ready")
        lat_ready = Order(sem("latent_ready"), list(range(NTOK)))
        qr_ready = Order(sem("q_rope_ready"), [2, 3])
        nmax_ready = Order(sem("row_max_ready"), list(range(2 * HC)))
        pexp_ready = Order(sem("exp_ready"), list(range(2 * HC)))
        prob_ready = Order(sem("prob_ready"), list(range(2 * HC)))
        stored = sem("stored")
        slot_landed = [sem(f"slot_landed{k}") for k in range(RING)]
        slot_free = sem("slot_free")
        dots_ready = sem("dots_ready")
        coef_ready = sem("coef_ready")
        diag_ready = sem("diag_ready")
        ranked = sem("head_ranked")
        gmax_ready = sem("gate_max_ready")
        gexp_ready = sem("gate_exp_ready")
        peer_taken = sem("peer_tile_taken")

        def bank_of(name):
            return (product.count(name) - 1) % NBANK

        def out_bank(pe, name):
            n = product.count(name) - 1
            if n >= NBANK:
                pe.wait_ge(bank_free[n % NBANK], n // NBANK)
            return ps[:, n % NBANK, :]

        def in_bank(eng, name):
            eng.wait_ge(product.sem, product.count(name))
            return ps[:, bank_of(name), :]

        def free_bank(ins, name):
            ins.then_inc(bank_free[bank_of(name)], 1)

        def taken(eng, name):
            n = product.count(name) - 1
            eng.wait_ge(bank_free[n % NBANK], n // NBANK + 1)

        LOADS = weight_loads()
        load_at, slot_uses, last_use = {}, [0, 0, 0], [None, None, None]
        for name, last, slot in LOADS:
            slot_uses[slot] += 1
            load_at[name] = (slot, slot_uses[slot], last_use[slot])
            last_use[slot] = last

        def weights(eng, name):
            slot, use, _ = load_at[name]
            eng.wait_ge(w_landed[slot], 16 * use)
            return wring[:, slot * 4096:(slot + 1) * 4096]

        def load_weight(sp, name, src):
            slot, _, before = load_at[name]
            if before is not None:
                sp.wait_ge(product.sem, product.count(before))
            k, n = src.shape[1], src.shape[2]
            dst = wring[:, slot * 4096:slot * 4096 + k * n].rearrange("p (k n) -> p k n", k=k)
            sp.dma_start(dst, src).then_inc(w_landed[slot], 16)

        def ktiles(w, lo, hi):
            return w.rearrange("(k p) n -> p k n", p=P)[:, :, lo:hi]

        def heads(ap):
            return ap.rearrange("p (h c) -> p h c", h=HB)

        def over_heads(matrix):
            return matrix.unsqueeze(1).broadcast_to((P, HB, P))

        def per_head(col):
            return col.unsqueeze(2).broadcast_to((P, HB, P))

        def tok(t):
            return slice(t * P, (t + 1) * P)

        def unit(q, d):
            s, k = q // 2, q % 2
            return 2 * s + (k if d == 0 else 1 - k)

        INCL = (GE, LE)
        SUM_TO = (LE, GE)
        SUM_REST = (GT, LT)
        MASK = (LOWER, UPPER)

        def norm_act(act, stage, t, dst, first):
            e = ssq_ready.count((stage, t)) - 1
            act.wait_ge(*first)
            act_step(nc.scalar.activation(dst, x[:, t, :], ACT.Square, accum_out=ssq[:, e:e + 1]))
            ssq_ready.mark(nc.scalar.activation(rstd[:, e:e + 1], ssq[:, e:e + 1], ACT.Sqrt, bias=eps_col,
                                                scale=1.0 / D), (stage, t))

        def norm_dve(dve, step, stage, t, dst, gain, shift):
            e = ssq_ready.count((stage, t)) - 1
            dve.wait_ge(ssq_ready.sem, e + 1)
            step(nc.vector.reciprocal(rstd[:, e:e + 1], rstd[:, e:e + 1]))
            last = nc.vector.scalar_tensor_tensor(out=dst, in0=x[:, t, :], scalar=rstd[:, e:e + 1], in1=gain,
                                                  op0=ALU.mult, op1=ALU.mult)
            if shift is not None:
                step(last)
                last = nc.vector.tensor_tensor(dst, dst, shift, ALU.add)
            h_ready.mark(last, (stage, t))

        def norm_pe(pe, stage, t, src):
            pe.wait_ge(h_ready.sem, h_ready.count((stage, t)))
            for half in range(2):
                name = ("ht", stage, t, half)
                bank = out_bank(pe, name)
                for j in range(4):
                    c = 4 * half + j
                    last = nc.tensor.transpose(bank[:, j * P:(j + 1) * P], src[:, c * P:(c + 1) * P], const(IDENT))
                product.mark(last, name)

        def norm_take(eng, copy, stage, t, half, slot, dst=None):
            bank = in_bank(eng, ("ht", stage, t, half))
            free_bank(copy((hT if dst is None else dst)[:, 4 * half:4 * half + 4, tok(slot)], bank.rearrange("p (k t) -> p k t", k=4)),
                      ("ht", stage, t, half))

        def residual_half(dve, product_name, stage, t, c, gate, rows):
            cols = slice(512 * c, 512 * c + 512)
            bank = in_bank(dve, (product_name, t, c))
            free_bank(nc.vector.tensor_tensor(rows[:, c, :], bank, gate[:, cols], ALU.mult), (product_name, t, c))
            taken(dve, (product_name, t, c))
            last = nc.vector.tensor_tensor(x[:, t, cols], x[:, t, cols], rows[:, c, :], ALU.add)
            if c:
                x_ready.mark(last, (stage, t))

        def peer_scores_pe(pe, layer, tiles, keys_landed):
            n = P * len(tiles)
            for t in tiles:
                for half in range(2):
                    taken(pe, ("ht", "p" + layer, t, half))
            for h in range(PH):
                w = weights(pe, ("w_q" + layer, h // 4)).rearrange("p (k n) -> p k n", k=KT)
                c = (h % 4) * P
                bank = out_bank(pe, ("q" + layer, h))
                for k in range(KT):
                    last = nc.tensor.matmul(bank[:, 0:n], w[:, k, c:c + P], hT[:, k, 0:n],
                                            start=(k == 0), stop=(k == KT - 1))
                product.mark(last, ("q" + layer, h))
            pe.wait_ge(keys_landed, 16)
            for i, t in enumerate(tiles):
                for j in range(4):
                    bank = out_bank(pe, ("s" + layer, t, j))
                    for k in range(2):
                        h = 2 * j + k
                        taken(pe, ("q" + layer, h))
                        last = nc.tensor.matmul(bank[:, 256 * k:256 * k + 256], qT[:, h, tok(i)], keysB[:, h, :],
                                                start=True, stop=True)
                    product.mark(last, ("s" + layer, t, j))

        pool_step, act_step, dve_step = (Steps(e, s, sem("waited_" + n)) for e, s, n in (
            (nc.gpsimd, pool_steps, "pool"), (nc.scalar, act_steps, "act"), (nc.vector, dve_steps, "dve")))

        def mixer_dma(sp, s):
            m = MEM[s]
            last = 2 * s + 1
            if s == 1:
                sp.wait_ge(product.sem, product.count(("dS", 3, 1)))
                sp.wait_ge(s_ready.sem, s_ready.count((3, 1)))
                sp.wait_ge(osq_ready.sem, osq_ready.count(3))
            for c in range(2):
                load_weight(sp, ("w_out0", s, c), ktiles(T["ev_w_out"], c * 512, (c + 1) * 512))
            if s == 0:
                sp.wait_ge(h_ready.sem, h_ready.count(("m0", 1)))
            sp.dma_start(m["gate"], mods[0, s, 2].partition_broadcast(P)).then_inc(bc_landed["g0", s], 16)
            if s == 0:
                sp.wait_ge(osq_ready.sem, osq_ready.count(1))
            sp.dma_start(m["modbc"], mods[0, s, 3:5].partition_broadcast(P)).then_inc(bc_landed["p0", s], 16)
            for c in range(2):
                load_weight(sp, ("w_q0", s, c), ktiles(T["p_w_q"][0], c * 512, (c + 1) * 512))
            if s == 1:
                sp.wait_ge(h_ready.sem, h_ready.count(("p0", last)))
            else:
                sp.wait_ge(osq_ready.sem, osq_ready.count(1))
            sp.dma_start(m["keys"], T["keys"][0]).then_inc(bc_landed["keys0", s], 16)

        def mixer_act(act, s):
            A_, copy = nc.scalar.activation, nc.scalar.copy
            m = MEM[s]
            tiles = (2 * s, 2 * s + 1)
            for i, t in enumerate(tiles):
                free_bank(copy(m["vtok"][:, i, :], in_bank(act, ("vtok", t))), ("vtok", t))
            yield
            for q in tiles:
                for d in range(2):
                    free_bank(A_(m["gam"][:, d, :], in_bank(act, ("D", q, d)), ACT.Exp), ("D", q, d))
                yield
                yield
                for lv in LEVELS[1:]:
                    for d in range(2):
                        free_bank(copy(m["P1s"][:, d, :], in_bank(act, ("P1", q, d, lv))), ("P1", q, d, lv))
                    if lv == LEVELS[1]:
                        for d in range(2):
                            free_bank(copy(m["intraT"][:, d, :], in_bank(act, ("intraT", q, d))), ("intraT", q, d))
                    yield
                    yield
                for d in range(2):
                    free_bank(copy(m["vn"][:, d, :], in_bank(act, ("vnew", q, d))), ("vnew", q, d))
                yield
                yield
            act.wait_ge(s_ready.sem, s_ready.count((2 * s + 1, 1)))
            act.wait_ge(product.sem, product.count(("dS", 2 * s + 1, 1)))
            for i, t in enumerate(tiles):
                act_step(*[A_(m["osq"][:, i, h * P:(h + 1) * P], m["oacc"][:, i, h * P:(h + 1) * P],
                              ACT.Square, accum_out=ossq[:, 4 * t + h:4 * t + h + 1]) for h in range(HB)])
                osq_ready.mark(A_(orst[:, 4 * t:4 * t + 4], ossq[:, 4 * t:4 * t + 4], ACT.Sqrt, bias=eps_col,
                                  scale=1.0 / DK), t)
            yield
            for i, t in enumerate(tiles):
                free_bank(copy(m["yb"][:, :, tok(i)], heads(in_bank(act, ("ybT", t)))), ("ybT", t))
            yield
            for _ in range(4):
                yield
            for i, t in enumerate(tiles):
                norm_act(act, "p0", t, m["hx2"][:, i, :], (x_ready.sem, x_ready.count(("m0", tiles[1]))))
            yield
            for i, t in enumerate(tiles):
                norm_take(act, copy, "p0", t, 0, i, m["hT"])
            yield
            for j in range(5):
                if j < 4:
                    for h in (2 * j, 2 * j + 1):
                        free_bank(copy(m["qT"][:, h, :], in_bank(act, ("q0", s, h))[:, 0:256]), ("q0", s, h))
                if j:
                    t = tiles[0]
                    free_bank(copy(m["score"][:, 0, 2 * j - 2:2 * j, :],
                                   in_bank(act, ("s0", t, j - 1)).rearrange("p (h n) -> p h n", h=2)),
                              ("s0", t, j - 1))
                yield

        def mixer_dve(dve, s):
            V, step = nc.vector, dve_step
            m = MEM[s]
            tiles = (2 * s, 2 * s + 1)
            A, gam, intra, X, Y, Bm, R, tmp = (m[n] for n in ("A", "gam", "intra", "X", "Y", "Bm", "R", "tmp"))
            TT = V.tensor_tensor

            def scaled_masks(q):
                for d in range(2):
                    t = unit(q, d)
                    last = [V.tensor_scalar(m["lg"][:, d, h * P:(h + 1) * P], const(SUM_TO[d]),
                                            gdec[:, t, 4 * d + h:4 * d + h + 1], None, ALU.mult)
                            for h in range(HB)][-1]
                    lg_ready.mark(last, (q, d))

            def level(q, lv):
                for d in range(2):
                    bm_ready.mark(TT(heads(Bm[:, d, :]), heads(A[:, d, :]), over_heads(const(MASK[d][lv])), ALU.mult),
                                  (q, d, lv))

            for i, t in enumerate(tiles):
                free_bank(V.tensor_copy(m["ktok"][:, i, :], in_bank(dve, ("ktok", t))), ("ktok", t))
            scaled_masks(2 * s)
            yield
            for q in tiles:
                for d in range(2):
                    taken(dve, ("D", q, d))
                    free_bank(TT(A[:, d, :], in_bank(dve, ("KK", q, d)), gam[:, d, :], ALU.mult), ("KK", q, d))
                for d in range(2):
                    taken(dve, ("KK", q, d))
                    ai_ready.mark(TT(heads(A[:, d, :]), heads(A[:, d, :]),
                                     per_head(beta[:, unit(q, d), 4 * d:4 * d + 4]), ALU.mult), ("A", q, d))
                dve.wait_ge(ai_ready.sem, ai_ready.count(("A", q, 1)))
                step(*[TT(heads(Y[:, d, :]), heads(A[:, d, :]), over_heads(const(MASK[d][1])), ALU.mult)
                       for d in range(2)])
                level(q, LEVELS[1])
                yield
                for d in range(2):
                    free_bank(TT(heads(X[:, d, :]), heads(in_bank(dve, ("AT", q, d))),
                                 over_heads(const(MASK[1 - d][1])), ALU.mult), ("AT", q, d))
                for d in range(2):
                    taken(dve, ("AT", q, d))
                    for n, mat in (("X", X), ("Y", Y)):
                        xy_ready.mark(TT(heads(mat[:, d, :]), over_heads(const(IDENT)), heads(mat[:, d, :]),
                                         ALU.subtract), (n, q, d, 1))
                for d in range(2):
                    free_bank(TT(intra[:, d, :], in_bank(dve, ("QK", q, d)), gam[:, d, :], ALU.mult), ("QK", q, d))
                for d in range(2):
                    taken(dve, ("QK", q, d))
                    ai_ready.mark(TT(heads(intra[:, d, :]), heads(intra[:, d, :]), over_heads(const(INCL[d])),
                                     ALU.mult), ("I", q, d))
                yield
                for lv in LEVELS[1:]:
                    if lv == LEVELS[-1]:
                        for d in range(2):
                            free_bank(TT(heads(R[:, d, :]), heads(in_bank(dve, ("KS", q, d))),
                                         per_head(edec[:, d, unit(q, d), :]), ALU.mult), ("KS", q, d))
                        for i, t in enumerate(tiles):
                            taken(dve, ("vtok", t))
                        for d in range(2):
                            taken(dve, ("KS", q, d))
                        step(*[TT(R[:, d, :], m["vtok"][:, unit(q, d) - 2 * s, :], R[:, d, :], ALU.subtract)
                               for d in range(2)])
                        for d in range(2):
                            r_ready.mark(TT(heads(R[:, d, :]), heads(R[:, d, :]),
                                            per_head(beta[:, unit(q, d), 4 * d:4 * d + 4]), ALU.mult), (q, d))
                        for d in range(2):
                            free_bank(TT(heads(tmp[:, d, :]), heads(in_bank(dve, ("QS", q, d))),
                                         per_head(edec[:, d, unit(q, d), :]), ALU.mult), ("QS", q, d))
                    yield
                    for d in range(2):
                        for n, mat in (("X", X), ("Y", Y)):
                            if n == "Y" and lv == LEVELS[-1]:
                                continue
                            name = (n + "B" + n, q, d, lv)
                            dve.wait_ge(xy_ready.sem, xy_ready.count((n, q, d, lv // 2)))
                            free_bank(TT(mat[:, d, :], mat[:, d, :], in_bank(dve, name), ALU.subtract), name)
                            taken(dve, name)
                            dve.sem_inc(xy_ready.sem, 1)
                            xy_ready.done += 1
                    if lv != LEVELS[-1]:
                        level(q, 2 * lv)
                    else:
                        for d in range(2):
                            if d == 0:
                                for t in tiles:
                                    taken(dve, ("ktok", t))
                            kd_ready.mark(TT(heads(m["kdK"][:, d, :]), heads(m["ktok"][:, unit(q, d) - 2 * s, :]),
                                             per_head(erest[:, d, unit(q, d), :]), ALU.mult), (q, d))
                    yield
                yield
                for d in range(2):
                    t = unit(q, d)
                    o = m["oacc"][:, t - 2 * s, :]
                    taken(dve, ("QS", q, d))
                    bank = in_bank(dve, ("intraV", q, d))
                    if q % 2 == 0:
                        free_bank(TT(o, tmp[:, d, :], bank, ALU.add), ("intraV", q, d))
                    else:
                        free_bank(TT(tmp[:, d, :], tmp[:, d, :], bank, ALU.add), ("intraV", q, d))
                        taken(dve, ("intraV", q, d))
                        taken(dve, ("intraV", q - 1, 1 - d))
                        step(TT(o, o, tmp[:, d, :], ALU.add))
                    step(TT(heads(S[:, d, :]), heads(S[:, d, :]), per_head(eall[:, t, d, :]), ALU.mult))
                    free_bank(TT(S[:, d, :], S[:, d, :], in_bank(dve, ("dS", q, d)), ALU.add), ("dS", q, d))
                    taken(dve, ("dS", q, d))
                    dve.sem_inc(s_ready.sem, 1)
                    s_ready.done += 1
                if q == 2 * s:
                    scaled_masks(q + 1)
                yield
            for i, t in enumerate(tiles):
                o = m["oacc"][:, i, :]
                dve.wait_ge(osq_ready.sem, osq_ready.count(t))
                r4 = orst[:, 4 * t:4 * t + 4]
                step(V.reciprocal(r4, r4))
                step(TT(heads(o), heads(o), per_head(r4), ALU.mult))
                step(TT(heads(o), heads(o), over_heads(ogain), ALU.mult))
                taken(dve, ("z", t))
                yb_ready.mark(TT(o, o, m["z"][:, i, :], ALU.mult), t)
            yield
            yield
            dve.wait_ge(bc_landed["g0", s], 16)
            for t in tiles:
                for c in range(2):
                    residual_half(dve, "out0", "m0", t, c, m["gate"], m["rows"])
                    yield
            dve.wait_ge(bc_landed["p0", s], 16)
            for i, t in enumerate(tiles):
                norm_dve(dve, step, "p0", t, m["hx2"][:, i, :], m["modbc"][:, 1, :], m["modbc"][:, 0, :])
            yield
            for i, t in enumerate(tiles):
                norm_take(dve, V.tensor_copy, "p0", t, 1, i, m["hT"])
            yield
            for j in range(5):
                if j:
                    t = tiles[1]
                    free_bank(V.tensor_copy(m["score"][:, 1, 2 * j - 2:2 * j, :],
                                            in_bank(dve, ("s0", t, j - 1)).rearrange("p (h n) -> p h n", h=2)),
                              ("s0", t, j - 1))
                yield

        def mixer_pe(pe, s):
            M, TR = nc.tensor.matmul, nc.tensor.transpose
            m = MEM[s]
            tiles = (2 * s, 2 * s + 1)

            def by_head(name, lhsT, rhs, op=M):
                bank = out_bank(pe, name)
                for h in range(HB):
                    dst = bank[:, h * P:(h + 1) * P]
                    last = M(dst, lhsT(h), rhs(h), start=True, stop=True) if op is M else TR(dst, lhsT(h), rhs(h))
                product.mark(last, name)

            def of(n, d):
                return lambda h: m[n][:, d, h * P:(h + 1) * P]

            def qT_(q, d):
                return lambda h: m["qkv"][:, h, tok(unit(q, d) - 2 * s)]

            def kT_(q, d):
                return lambda h: m["qkv"][:, 4 + h, tok(unit(q, d) - 2 * s)]

            ident = lambda h: const(IDENT)
            for i, t in enumerate(tiles):
                for n, first in (("ktok", 4), ("vtok", 8)):
                    by_head((n, t), lambda h: m["qkv"][:, first + h, tok(i)], ident, TR)
            yield
            for q in tiles:
                for d in range(2):
                    pe.wait_ge(lg_ready.sem, lg_ready.count((q, d)))
                    by_head(("D", q, d), of("lg", d), lambda h: const(SUM_REST[d]))
                for d in range(2):
                    by_head(("KK", q, d), kT_(q, d), kT_(q, d))
                yield
                for d in range(2):
                    pe.wait_ge(ai_ready.sem, ai_ready.count(("A", q, d)))
                    by_head(("AT", q, d), of("A", d), ident, TR)
                for d in range(2):
                    by_head(("QK", q, d), qT_(q, d), kT_(q, d))
                yield
                for lv in LEVELS[1:]:
                    for d in range(2):
                        pe.wait_ge(bm_ready.sem, bm_ready.count((q, d, lv)))
                        pe.wait_ge(xy_ready.sem, xy_ready.count(("Y", q, d, lv // 2)))
                        by_head(("P1", q, d, lv), of("Bm", d), of("X", d))
                    if lv == LEVELS[1]:
                        for d in range(2):
                            pe.wait_ge(ai_ready.sem, ai_ready.count(("I", q, d)))
                            by_head(("intraT", q, d), of("intra", d), ident, TR)
                    if lv == LEVELS[-1]:
                        for d in range(2):
                            pe.wait_ge(s_ready.sem, s_ready.count((q - 1, d)) if q else 1)
                            by_head(("KS", q, d), kT_(q, d), of_state(d))
                        for d in range(2):
                            by_head(("QS", q, d), qT_(q, d), of_state(d))
                    yield
                    for d in range(2):
                        taken(pe, ("P1", q, d, lv))
                        by_head(("XBX", q, d, lv), of("Y", d), of("P1s", d))
                        if lv != LEVELS[-1]:
                            by_head(("YBY", q, d, lv), of("P1s", d), of("Y", d))
                    yield
                for d in range(2):
                    pe.wait_ge(r_ready.sem, r_ready.count((q, d)))
                    pe.wait_ge(xy_ready.sem, xy_ready.count(("X", q, d, LEVELS[-1])))
                    by_head(("vnew", q, d), of("X", d), of("R", d))
                yield
                for d in range(2):
                    taken(pe, ("vnew", q, d))
                    taken(pe, ("intraT", q, d))
                    by_head(("intraV", q, d), of("intraT", d), of("vn", d))
                for d in range(2):
                    pe.wait_ge(kd_ready.sem, kd_ready.count((q, d)))
                    by_head(("dS", q, d), of("kdK", d), of("vn", d))
                yield
            yield
            for i, t in enumerate(tiles):
                pe.wait_ge(yb_ready.sem, yb_ready.count(t))
                by_head(("ybT", t), lambda h: m["oacc"][:, i, h * P:(h + 1) * P], ident, TR)
            yield
            pe.wait_ge(ya_ready, 4)
            for i, t in enumerate(tiles):
                taken(pe, ("ybT", t))
                for c in range(2):
                    w = weights(pe, ("w_out0", s, c)).rearrange("p (k n) -> p k n", k=KT)
                    bank = out_bank(pe, ("out0", t, c))
                    for k in range(KT):
                        y = m["ya"][:, k, tok(i)] if k < 4 else m["yb"][:, k - 4, tok(i)]
                        last = M(bank, y, w[:, k, :], start=(k == 0), stop=(k == KT - 1))
                    product.mark(last, ("out0", t, c))
                    yield
            yield
            for i, t in enumerate(tiles):
                norm_pe(pe, "p0", t, m["hx2"][:, i, :])
            yield
            for t in tiles:
                for half in range(2):
                    taken(pe, ("ht", "p0", t, half))
            for j in range(5):
                if j < 4:
                    w = weights(pe, ("w_q0", s, j // 2)).rearrange("p (k n) -> p k n", k=KT)
                    for h in (2 * j, 2 * j + 1):
                        bank = out_bank(pe, ("q0", s, h))
                        for k in range(KT):
                            last = M(bank[:, 0:256], w[:, k, (h % 4) * P:(h % 4 + 1) * P], m["hT"][:, k, :],
                                     start=(k == 0), stop=(k == KT - 1))
                        product.mark(last, ("q0", s, h))
                if j:
                    pe.wait_ge(bc_landed["keys0", s], 16)
                    for i, t in enumerate(tiles):
                        bank = out_bank(pe, ("s0", t, j - 1))
                        for k in range(2):
                            h = 2 * j - 2 + k
                            taken(pe, ("q0", s, h))
                            last = M(bank[:, 256 * k:256 * k + 256], m["qT"][:, h, tok(i)], m["keys"][:, h, :],
                                     start=True, stop=True)
                        product.mark(last, ("s0", t, j - 1))
                yield

        def of_state(d):
            return lambda h: S[:, d, h * P:(h + 1) * P]

        def whole(stages):
            for _ in stages:
                pass

        def first_block(block):
            @block.sync
            def _(sp):
                sp.dma_start(x[:, 0:2, :], T["ctx"].rearrange("(t p) d -> p t d", p=P)).then_inc(x_landed, 16)
                sp.dma_start(x[:, 2:4, :], T["x"].rearrange("(t p) d -> p t d", p=P)).then_inc(x_landed, 16)
                for i in range(2):
                    for c in range(12):
                        load_weight(sp, ("mod", i, c), ktiles(T["w_mod"][i], c * 512, (c + 1) * 512))
                for c in range(7):
                    load_weight(sp, ("w_in", c), ktiles(T["ev_w_in"], c * 512, (c + 1) * 512))
                load_weight(sp, ("w_ab",), ktiles(T["ev_w_in"], 3584, 3600))
                mixer_dma(sp, 0)

            @block.gpsimd
            def _(pool):
                nc.gpsimd.memset(eps_col, EPS).then_inc(eps_ready, 1)
                pool.dma_start(sTin, T["c_cols"]).then_inc(consts_landed, 16)
                pool.dma_start(consts[:, :], T["consts"]).then_inc(consts_landed, 16)
                pool.dma_start(iota16[:, :], T["iota16"]).then_inc(consts_landed, 16)
                pool.dma_start(conv_w[:, :, :], T["conv_w"]).then_inc(consts_landed, 16)
                pool.dma_start(alog, T["a_log"].partition_broadcast(P)).then_inc(consts_landed, 16)
                pool.dma_start(dtb, T["dt_bias"].partition_broadcast(P)).then_inc(consts_landed, 16)
                pool.dma_start(ogain, T["o_norm"].partition_broadcast(P)).then_inc(consts_landed, 16)
                for i in range(2):
                    for s in range(2):
                        pool.dma_start(mod_rows[i][s:s + 1], T["b_mod"][i:i + 1]).then_inc(row_landed[i], 16)
                for s in range(2):
                    pool.dma_start(norm_rows[s:s + 1], T["norms"]).then_inc(row_landed[0], 16)
                pool.wait_ge(rows_ready, 1)
                pool.dma_start(mods[0], mod_rows[0]).then_inc(rows_stored, 16)
                pool.wait_ge(rows_ready, 2)
                pool.dma_start(mods[1], mod_rows[1]).then_inc(rows_stored, 16)
                pool.wait_ge(rows_stored, 32)
                for s in range(2):
                    pool.dma_start(modbc0[s], mods[0, s, 0:2].partition_broadcast(P)).then_inc(bc_landed["m0", s], 16)

            @block.scalar
            def _(act):
                A_, copy = nc.scalar.activation, nc.scalar.copy
                halves = lambda bank: bank.rearrange("p (s t) -> p s t", s=2)
                act.wait_ge(consts_landed, 7 * 16)
                A_(sT, sTin, ACT.Silu).then_inc(silu_c, 1)
                act.wait_ge(x_landed, 32)
                act.wait_ge(eps_ready, 1)
                for t in range(NTOK):
                    first = (x_landed, 32) if t < 2 else (product.sem, product.count(("ht", "m0", t - 2, 1)))
                    norm_act(act, "m0", t, hbuf0[:, t % 2, :], first)
                    if t:
                        norm_take(act, copy, "m0", t - 1, 0, t - 1)
                norm_take(act, copy, "m0", 3, 0, 3)
                for b in range(8):
                    free_bank(copy(bgcg[:, b, :], in_bank(act, ("proj", b))), ("proj", b))
                for b in range(4):
                    act.wait_ge(u_ready.sem, u_ready.count(("u", b)))
                    xa_conv.mark(A_(ya_block(b), halves(conv_in[:, b, :]), ACT.Copy, scale=conv_w[:, b, 1:2]),
                                 ("xa", b))
                for b in range(12):
                    bank = in_bank(act, ("proj", 12 + b))
                    centre_ready.mark(A_(qkv_block(b), halves(bank), ACT.Copy, scale=conv_w[:, 4 + b, 1:2]), b)
                    act.wait_ge(conv_ready.sem, conv_ready.count(("conv", b)))
                    silu_ready.mark(A_(qkv_block(b), qkv_block(b), ACT.Silu), ("silu", b))
                for t in range(NTOK):
                    free_bank(A_(MEM[t // 2]["z"][:, t % 2, :], in_bank(act, ("z", t)), ACT.Silu), ("z", t))
                act.wait_ge(sp_dve, 1)
                A_(beta, ab[:, :, 8:16], ACT.Sigmoid).then_inc(sp_act, 1)
                A_(g2, g2, ACT.Exp).then_inc(sp_act, 1)
                A_(nexpa, alog, ACT.Exp).then_inc(sp_act, 1)
                act.wait_ge(sp_act, 3)
                A_(g2, g2, ACT.Ln, bias=1.0).then_inc(sp_act, 1)
                free_bank(A_(expo, in_bank(act, ("cum",))[:, 0:96], ACT.Exp), ("cum",))
                taken(act, ("cum",))
                act.sem_inc(sp_act, 1)
                for b in range(8):
                    act.wait_ge(silu_ready.sem, silu_ready.count(("silu", b)))
                    square_ready.mark(A_(halves(hT[:, b, :]), qkv_block(b), ACT.Square), ("sq", b))
                for b in range(8):
                    free_bank(A_(hT[:, b, :], in_bank(act, ("sumsq", b)), ACT.Sqrt, bias=eps_col), ("sumsq", b))
                whole(mixer_act(act, 0))

            @block.vector
            def _(dve):
                V, step = nc.vector, dve_step
                halves = lambda bank: bank.rearrange("p (s t) -> p s t", s=2)
                for i in range(2):
                    dve.wait_ge(row_landed[i], 64 if i == 0 else 32)
                    for c in range(12):
                        bank = in_bank(dve, ("mod", i, c))
                        row = mod_rows[i][:, c // 2, (c % 2) * 512:(c % 2) * 512 + 512]
                        free_bank(V.tensor_tensor(row, bank[0:2, :], row, ALU.add), ("mod", i, c))
                    for c in range(12):
                        taken(dve, ("mod", i, c))
                    step(*[V.scalar_tensor_tensor(out=mod_rows[i][:, 1 + 3 * n, :], in0=mod_rows[i][:, 1 + 3 * n, :],
                                                  scalar=1.0, in1=norm_rows[:, i, n, :], op0=ALU.add, op1=ALU.mult)
                           for n in range(2)])
                    dve.sem_inc(rows_ready, 1)
                for t in range(NTOK):
                    if t % 2 == 0:
                        dve.wait_ge(bc_landed["m0", t // 2], 16)
                    bc = modbc0[t // 2]
                    norm_dve(dve, step, "m0", t, hbuf0[:, t % 2, :], bc[:, 1, :], bc[:, 0, :])
                    if t:
                        norm_take(dve, V.tensor_copy, "m0", t - 1, 1, t - 1)
                norm_take(dve, V.tensor_copy, "m0", 3, 1, 3)

                def other_taps(a3, u3, w):
                    step(V.scalar_tensor_tensor(out=a3[:, :, 1:256], in0=u3[:, :, 0:255], scalar=w[:, 0:1],
                                                in1=a3[:, :, 1:256], op0=ALU.mult, op1=ALU.add))
                    return V.scalar_tensor_tensor(out=a3[:, :, 0:255], in0=u3[:, :, 1:256], scalar=w[:, 2:3],
                                                  in1=a3[:, :, 0:255], op0=ALU.mult, op1=ALU.add)

                for b in range(4):
                    bank = in_bank(dve, ("proj", 8 + b))
                    taken(dve, ("proj", 4 + b))
                    free_bank(V.tensor_tensor(conv_in[:, b, :], bank, bgcg[:, 4 + b, :], ALU.mult), ("proj", 8 + b))
                    taken(dve, ("proj", 8 + b))
                    dve.sem_inc(u_ready.sem, 1)
                    u_ready.done += 1
                    dve.wait_ge(xa_conv.sem, xa_conv.count(("xa", b)))
                    step(other_taps(ya_block(b), halves(conv_in[:, b, :]), conv_w[:, b, :]))
                    taken(dve, ("proj", b))
                    last = V.tensor_tensor(ya_block(b), ya_block(b), halves(bgcg[:, b, :]), ALU.mult)
                    last.then_inc(ya_ready, 1)
                for b in range(12):
                    bank = in_bank(dve, ("proj", 12 + b))
                    dve.wait_ge(centre_ready.sem, centre_ready.count(b))
                    free_bank(other_taps(qkv_block(b), halves(bank), conv_w[:, 4 + b, :]), ("proj", 12 + b))
                    taken(dve, ("proj", 12 + b))
                    dve.sem_inc(conv_ready.sem, 1)
                    conv_ready.done += 1
                free_bank(V.tensor_copy(small[:, 16:80], in_bank(dve, ("ab",))[:, 0:64]), ("ab",))
                taken(dve, ("ab",))
                step(V.tensor_tensor(g1, ab[:, :, 0:8], dtb.unsqueeze(1).broadcast_to((P, NTOK, 8)), ALU.add))
                step(V.scalar_tensor_tensor(out=g2, in0=g1, scalar=-1.0, in1=g1, op0=ALU.mult, op1=ALU.min))
                dve.sem_inc(sp_dve, 1)
                step(V.tensor_scalar(g1, g1, 0.0, None, ALU.max))
                dve.wait_ge(sp_act, 4)
                step(V.tensor_tensor(g1, g1, g2, ALU.add))
                step(V.scalar_tensor_tensor(out=gdec, in0=g1, scalar=-1.0,
                                            in1=nexpa.unsqueeze(1).broadcast_to((P, NTOK, 8)),
                                            op0=ALU.mult, op1=ALU.mult))
                dve.sem_inc(sp_dve, 1)
                for b in range(8):
                    r = hT[:, b, :]
                    taken(dve, ("sumsq", b))
                    step(V.reciprocal(r, r))
                    step(V.scalar_tensor_tensor(out=qkv_block(b), in0=qkv_block(b),
                                                scalar=float(DK) ** -0.5 if b < 4 else 1.0, in1=halves(r),
                                                op0=ALU.mult, op1=ALU.mult))
                    dve.sem_inc(qk_ready.sem, 1)
                qk_ready.done = 8
                dve.sem_inc(slot_free, RING)
                dve.sem_inc(peer_taken, 1)
                dve.wait_ge(sp_act, 5)
                step(V.memset(S[:, :, :], 0.0))
                dve.sem_inc(s_ready.sem, 1)
                s_ready.done += 1
                whole(mixer_dve(dve, 0))

            @block.tensor
            def _(pe):
                M = nc.tensor.matmul

                def accumulate(dst, pairs):
                    for i, (l, r) in enumerate(pairs):
                        last = M(dst, l, r, start=(i == 0), stop=(i == len(pairs) - 1))
                    return last

                pe.wait_ge(silu_c, 1)
                pe.wait_ge(consts_landed, 7 * 16)
                for i in range(2):
                    for c in range(12):
                        w = weights(pe, ("mod", i, c)).rearrange("p (k n) -> p k n", k=KT)
                        bank = out_bank(pe, ("mod", i, c))
                        product.mark(accumulate(bank[0:2, :], [(sT[:, 2 * k:2 * k + 2], w[:, k, :])
                                                               for k in range(KT)]), ("mod", i, c))
                for t in range(NTOK):
                    norm_pe(pe, "m0", t, hbuf0[:, t % 2, :])
                for t in range(NTOK):
                    for half in range(2):
                        taken(pe, ("ht", "m0", t, half))
                for b in range(24):
                    w = weights(pe, ("w_in", b // 4)).rearrange("p (k n) -> p k n", k=KT)
                    c = (b % 4) * P
                    bank = out_bank(pe, ("proj", b))
                    product.mark(accumulate(bank, [(w[:, k, c:c + P], hT[:, k, :]) for k in range(KT)]), ("proj", b))
                w = weights(pe, ("w_in", 6)).rearrange("p (k n) -> p k n", k=KT)
                for t in range(NTOK):
                    bank = out_bank(pe, ("z", t))
                    product.mark(accumulate(bank, [(hT[:, k, tok(t)], w[:, k, :]) for k in range(KT)]), ("z", t))
                w = weights(pe, ("w_ab",))[:, 0:16 * KT].rearrange("p (k n) -> p k n", k=KT)
                bank = out_bank(pe, ("ab",))
                for t in range(NTOK):
                    last = accumulate(bank[:, 16 * t:16 * t + 16], [(hT[:, k, tok(t)], w[:, k, :]) for k in range(KT)])
                product.mark(last, ("ab",))
                pe.wait_ge(sp_dve, 2)
                bank = out_bank(pe, ("cum",))
                for j, masks in enumerate((SUM_TO, SUM_REST)):
                    for d in range(2):
                        at = 32 * j + 16 * d
                        M(bank[:, at:at + 16].rearrange("p (t h) -> p t h", t=NTOK), const(masks[d]),
                          gdec[:, :, 4 * d:4 * d + 4], start=True, stop=True)
                product.mark(M(bank[:, 64:96], const(ONES), small[:, 152:184], start=True, stop=True), ("cum",))
                for b in range(8):
                    pe.wait_ge(square_ready.sem, square_ready.count(("sq", b)))
                    bank = out_bank(pe, ("sumsq", b))
                    product.mark(M(bank, const(ONES), hT[:, b, :], start=True, stop=True), ("sumsq", b))
                pe.wait_ge(qk_ready.sem, 8)
                pe.wait_ge(silu_ready.sem, 12)
                whole(mixer_pe(pe, 0))

        GROUPS_OF_HEAD = TOPK // GRP

        def sums_pool(pool, G, par, k, table):
            pool.wait_ge(slot_free, G * TOPK + k + 1)
            pool_step.wait_apart()
            nc.gpsimd.indirect_dma_start(
                ring[:, k % RING, :], None, table,
                bass.IndirectOffsetOnAxis(ap=expert_cur[:, par, k:k + 1], axis=0),
            ).then_inc(slot_landed[k % RING], 16)

        def sums_act(act, G, par, j):
            g = slice(j * GRP, (j + 1) * GRP)
            act.wait_ge(dots_ready, G * GROUPS_OF_HEAD + j + 1)
            act_step(nc.scalar.activation(acts[:, par, g], dots[:, par, g], ACT.Gelu))
            act_step(*[nc.scalar.activation(coef[:, par, k:k + 1], acts[:, par, k:k + 1], ACT.Copy,
                                            scale=gate_cur[:, par, k:k + 1])
                       for k in range(j * GRP, (j + 1) * GRP)])
            for k in range(j * GRP, (j + 1) * GRP):
                nc.scalar.activation(diag[:, k % RING, :], const(IDENT), ACT.Copy,
                                     scale=coef[:, par, k:k + 1]).then_inc(diag_ready, 1)

        def gate_exp_act(act, G):
            act.wait_ge(gmax_ready, G + 1)
            nc.scalar.activation(gate_exp[:, :], best[:, :], ACT.Exp, bias=gate_stat[:, 0:1],
                                 accum_out=gate_stat[:, 1:2]).then_inc(gexp_ready, 1)

        def head_act(act, G, par, rank_next, between=lambda: None):
            act.wait_ge(ranked, G + 1)
            for j in range(GROUPS_OF_HEAD):
                if j in STAGE_AT:
                    between()
                sums_act(act, G, par, j)
                if j == 2 and rank_next:
                    gate_exp_act(act, G + 1)

        def tile_sum_act(act, T_, place):
            act.wait_ge(slot_free, (T_ + 1) * SLOTS + RING)
            nc.scalar.copy(arena[:, place].rearrange("p (a b) -> p a b", a=2), ps[:, 6:8, :]).then_inc(peer_taken, 1)

        def tile_open_pe(pe, T_):
            pe.wait_ge(peer_taken, T_ + 1)
            for c in range(2):
                nc.tensor.matmul(ps[:, 6 + c, :], const(ZERO), consts[:, 0:512], start=True, stop=True)

        def head_pe(pe, G, between=lambda: None):
            for k in range(TOPK):
                if k % GRP == 0 and k // GRP in STAGE_AT:
                    between()
                pe.wait_ge(diag_ready, G * TOPK + k + 1)
                for c in range(2):
                    last = nc.tensor.matmul(ps[:, 6 + c, :], diag[:, k % RING, :],
                                            ring[:, k % RING, D + 512 * c:D + 512 * c + 512],
                                            start=False, stop=True, skip_group_check=True)
                last.then_inc(slot_free, 1)

        def square(mat):
            return mat[:, :].rearrange("p (a b) -> p a b", a=TOPK)

        def rank_dve(G, n, par):
            V, step = nc.vector, dve_step
            step(V.tensor_copy(score_cur[:, :], arena[:, bass.ds(n * 256 + 16384, 256)]), apart=True)
            yield
            both = [(p, score_cur[:, p * NKEY:(p + 1) * NKEY], score_left[:, p * NKEY:(p + 1) * NKEY])
                    for p in range(2)]
            step(*[V.max(top_val[:, p, 0:8], cur) for p, cur, _ in both], apart=True)
            yield
            step(*[V.max_index(top_idx[:, p, 0:8], top_val[:, p, 0:8], cur) for p, cur, _ in both],
                 *[V.match_replace(left, top_val[:, p, 0:8], cur, -3e38) for p, cur, left in both], apart=True)
            yield
            step(*[V.max(top_val[:, p, 8:16], left) for p, _, left in both], apart=True)
            yield
            step(*[V.max_index(top_idx[:, p, 8:16], top_val[:, p, 8:16], left) for p, _, left in both],
                 V.tensor_tensor(square(cand), top_val[:, 0, :].unsqueeze(2).broadcast_to((P, TOPK, TOPK)),
                                 top_val[:, 1, :].unsqueeze(1).broadcast_to((P, TOPK, TOPK)), ALU.add))
            yield
            step(V.tensor_copy(top_idx_f[:, :, :], top_idx[:, :, :]), V.max(best[:, 0:8], cand[:, :]), apart=True)
            yield
            step(V.max_index(best_pos[:, 0:8], best[:, 0:8], cand[:, :]),
                 V.match_replace(cand_left[:, :], best[:, 0:8], cand[:, :], -3e38),
                 V.tensor_scalar(gate_stat[:, 0:1], best[:, 0:1], -1.0, None, ALU.mult), apart=True)
            yield
            step(V.max(best[:, 8:16], cand_left[:, :]), apart=True)
            dve_step.eng.sem_inc(gmax_ready, 1)
            yield
            step(V.max_index(best_pos[:, 8:16], best[:, 8:16], cand_left[:, :]))
            yield
            step(V.tensor_scalar(pos_ab[:, 0, :], best_pos[:, :], 4, None, ALU.logical_shift_right),
                 V.tensor_scalar(pos_ab[:, 1, :], best_pos[:, :], 15, None, ALU.bitwise_and))
            yield
            step(V.tensor_copy(pos_ab_f[:, :, :], pos_ab[:, :, :]))
            yield
            hot = (onehot, cand)
            step(*[V.tensor_tensor(square(hot[i]), iota16[:, :].unsqueeze(1).broadcast_to((P, TOPK, TOPK)),
                                   pos_ab_f[:, i, :].unsqueeze(2).broadcast_to((P, TOPK, TOPK)), ALU.is_equal)
                   for i in range(2)])
            yield
            step(*[V.tensor_tensor(square(hot[i]), square(hot[i]),
                                   top_idx_f[:, i, :].unsqueeze(1).broadcast_to((P, TOPK, TOPK)), ALU.mult)
                   for i in range(2)])
            yield
            step(*[V.tensor_reduce(sel_ab[:, i, :], square(hot[i]), AX, ALU.add) for i in range(2)])
            yield
            dve_step.eng.wait_ge(gexp_ready, G + 1)
            step(V.scalar_tensor_tensor(out=expert_cur[:, par, :], in0=sel_ab[:, 0, :],
                                        scalar=float(NKEY), in1=sel_ab[:, 1, :], op0=ALU.mult, op1=ALU.add),
                 V.reciprocal(gate_stat[:, 2:3], gate_stat[:, 1:2]))
            yield
            step(V.tensor_scalar(gate_cur[:, par, :], gate_exp[:, :], gate_stat[:, 2:3], None, ALU.mult))
            dve_step.eng.sem_inc(ranked, 1)
            yield

        RANK = 31
        RANK_SLOTS = range(1, 9)
        STAGE_AT = (0, 4, 6)

        def tile_start_dve(T_, place):
            if not (isinstance(T_, int) and T_ == 0):
                dve_step.eng.wait_ge(dots_ready, T_ * (PH * GROUPS_OF_HEAD))
            dve_step(nc.vector.tensor_copy(hx_cur[:, :], arena[:, place]))

        def head_dve(dve, G, n, par, rank_next, between=lambda: None):
            rank = rank_dve(G + 1, n + 1, 1 - par)
            for k in range(TOPK):
                slot = k % RING
                dve.wait_ge(slot_landed[slot], (G * (TOPK // RING) + k // RING + 1) * 16)
                ins = nc.vector.tensor_tensor_reduce(
                    out=ring[:, slot, 0:D], in0=ring[:, slot, 0:D], in1=hx_cur[:, :], scale=1.0, scalar=0.0,
                    op0=ALU.mult, op1=ALU.add, accum_out=dots[:, par, k:k + 1])
                if k % GRP == GRP - 1:
                    ins.then_inc(dots_ready, 1)
                    if k // GRP in STAGE_AT:
                        between()
                if rank_next and k in RANK_SLOTS:
                    next(rank)
                    next(rank)

        def tile_place(i):
            return bass.ds(i * D + 24576, D)

        def loop_act(act, tiles, T0, G0, last):
            n = len(tiles)
            start = act_step.base + act_step.n
            per_pair = 2 * GROUPS_OF_HEAD * (1 + GRP)

            def pair(i, hp, follows):
                act_step.start(start + (i * 4 + hp) * per_pair)
                for par in range(2):
                    head_act(act, G0 + i * PH + hp * 2 + par, par, follows or par == 0)
                assert act_step.n == per_pair

            with act.Fori(0, n - 1) as i:
                with act.Fori(0, 4) as hp:
                    pair(i, hp, True)
                tile_sum_act(act, i + T0, tile_place(i + tiles[0]))
            with act.Fori(0, 3) as hp:
                pair(n - 1, hp, True)
            pair(n - 1, 3, not last)
            tile_sum_act(act, n - 1 + T0, tile_place(n - 1 + tiles[0]))

        def loop_pe(pe, tiles, T0, G0):
            with pe.Fori(0, len(tiles)) as i:
                tile_open_pe(pe, i + T0)
                with pe.Fori(0, PH) as h:
                    head_pe(pe, G0 + i * PH + h)

        def loop_pool(pool, tiles, G0, table):
            with pool.Fori(0, len(tiles)) as i:
                with pool.Fori(0, 4) as hp:
                    for par in range(2):
                        G = G0 + i * PH + hp * 2 + par
                        pool.wait_ge(ranked, G + 1)
                        for k in range(TOPK):
                            sums_pool(pool, G, par, k, table)

        def loop_dve(dve, tiles, G0, n0):
            n = len(tiles)
            T0 = G0 // PH
            start = dve_step.base + dve_step.n
            per_tile = 1 + PH * RANK

            def pair(i, hp, follows):
                dve_step.start(start + i * per_tile + 1 + hp * (2 * RANK))
                for par in range(2):
                    h = i * PH + hp * 2 + par
                    head_dve(dve, G0 + h, n0 + h, par, follows or par == 0)
                assert dve_step.n == (2 * RANK if follows else RANK), dve_step.n

            with dve.Fori(0, n - 1) as i:
                dve_step.start(start + i * per_tile)
                tile_start_dve(i + T0, tile_place(i + tiles[0]))
                with dve.Fori(0, 4) as hp:
                    pair(i, hp, True)
            dve_step.start(start + (n - 1) * per_tile)
            tile_start_dve(n - 1 + T0, tile_place(n - 1 + tiles[0]))
            with dve.Fori(0, 3) as hp:
                pair(n - 1, hp, True)
            pair(n - 1, 3, False)

        def first_rank_dve(G, n):
            for _ in rank_dve(G, n, 0):
                pass

        def peer_gate_dma(pool, layer, heads_done):
            pool.wait_ge(slot_free, heads_done * TOPK + RING)
            for s in range(2):
                pool.dma_start(peer_gate[:, s, :], mods[layer, s, 5].partition_broadcast(P)).then_inc(
                    bc_landed[f"pg{layer}",], 16)

        def peer_residual_dve(dve, layer, tiles, tiles_done):
            dve.wait_ge(bc_landed[f"pg{layer}",], 32)
            dve.wait_ge(peer_taken, tiles_done + 1)
            for i, t in enumerate(tiles):
                dve_step(nc.vector.tensor_tensor(hx2[:, i, :], hx2[:, i, :], peer_gate[:, t // 2, :], ALU.mult))
                x_ready.mark(nc.vector.tensor_tensor(x[:, t, :], x[:, t, :], hx2[:, i, :], ALU.add), (f"p{layer}", t))

        def sums_and_mixer(block):
            table = T["experts0"]
            HEADS = 2 * PH

            def weave(stages):
                return lambda: next(stages, None)

            @block.sync
            def _(sp):
                mixer_dma(sp, 1)

            @block.gpsimd
            def _(pool):
                for G in range(HEADS):
                    pool.wait_ge(ranked, G + 1)
                    for k in range(TOPK):
                        sums_pool(pool, G, G % 2, k, table)
                loop_pool(pool, (2, 3), HEADS, table)
                peer_gate_dma(pool, 0, 4 * PH)

            @block.scalar
            def _(act):
                between = weave(mixer_act(act, 1))
                gate_exp_act(act, 0)
                for G in range(HEADS):
                    head_act(act, G, G % 2, True, between)
                    if G % PH == PH - 1:
                        tile_sum_act(act, G // PH, tile_place(G // PH))
                loop_act(act, (2, 3), 2, HEADS, True)

            @block.tensor
            def _(pe):
                between = weave(mixer_pe(pe, 1))
                for G in range(HEADS):
                    if G % PH == 0:
                        tile_open_pe(pe, G // PH)
                    head_pe(pe, G, between)
                loop_pe(pe, (2, 3), 2, HEADS)

            @block.vector
            def _(dve):
                between = weave(mixer_dve(dve, 1))
                first_rank_dve(0, 0)
                for G in range(HEADS):
                    if G % PH == 0:
                        tile_start_dve(G // PH, tile_place(G // PH))
                    head_dve(dve, G, G, G % 2, True, between)
                loop_dve(dve, (2, 3), HEADS, HEADS)
                peer_residual_dve(dve, 0, range(NTOK), 4)

        def last_sums(block):
            tiles, G0, T0 = (2, 3), 4 * PH, 4

            @block.gpsimd
            def _(pool):
                loop_pool(pool, (0, 1), G0, T["experts1"])
                peer_gate_dma(pool, 1, 6 * PH)
                pool.dma_start(gain_f, T["norm_f"].partition_broadcast(P)).then_inc(bc_landed["nf",], 16)

            @block.scalar
            def _(act):
                gate_exp_act(act, G0)
                loop_act(act, (0, 1), T0, G0, True)
                for i, t in enumerate(tiles):
                    norm_act(act, "f", t, hfin[:, i, :], (x_ready.sem, x_ready.count(("p1", t))))

            @block.tensor
            def _(pe):
                loop_pe(pe, (0, 1), T0, G0)

            @block.vector
            def _(dve):
                first_rank_dve(G0, 0)
                loop_dve(dve, (0, 1), G0, 0)
                peer_residual_dve(dve, 1, tiles, 6)
                dve.wait_ge(bc_landed["nf",], 16)
                for i, t in enumerate(tiles):
                    norm_dve(dve, dve_step, "f", t, hfin[:, i, :], gain_f, None)

            @block.sync
            def _(sp):
                for i, t in enumerate(tiles):
                    sp.wait_ge(h_ready.sem, h_ready.count(("f", t)))
                    sp.dma_start(out[tok(i), :], hfin[:, i, :]).then_inc(stored, 16)
                sp.wait_ge(stored, 32)

        def second_block(block):
            SC = float(NOPE + ROPE) ** -0.5

            @block.sync
            def _(sp):
                load_weight(sp, ("w_kv1",), ktiles(T["od_w_in"], QL, QL + KVL + ROPE))
                load_weight(sp, ("w_q_1",), ktiles(T["od_w_in"], 0, QL))
                load_weight(sp, ("w_uq_n",), ktiles(T["uq_nope"], 0, HC * NOPE))
                load_weight(sp, ("w_uq_r",), ktiles(T["uq_rope"], 0, HC * ROPE))
                load_weight(sp, ("w_ukv",), ktiles(T["ukv"], 0, HC * (NOPE + VD)))
                for c in range(2):
                    load_weight(sp, ("w_out1", c), ktiles(T["od_w_out"], c * 512, (c + 1) * 512))
                for c in range(2):
                    load_weight(sp, ("w_q1", c), ktiles(T["p_w_q"][1], c * 512, (c + 1) * 512))

            @block.gpsimd
            def _(pool):
                for s in range(2):
                    pool.dma_start(modbc1[s], mods[1, s, 0:2].partition_broadcast(P)).then_inc(bc_landed["m1", s], 16)
                pool.dma_start(lat_gain[:, 0:QL], T["q_norm"].partition_broadcast(P)).then_inc(bc_landed["lat",], 16)
                pool.dma_start(lat_gain[:, QL:QL + KVL], T["kv_norm"].partition_broadcast(P)).then_inc(bc_landed["lat",], 16)
                pool.dma_start(rope_cs, T["rope"]).then_inc(bc_landed["lat",], 16)
                pool.wait_ge(h_ready.sem, h_ready.count(("m1", 3)))
                pool.dma_start(gate1, mods[1, 1, 2].partition_broadcast(P)).then_inc(bc_landed["g1",], 16)
                pool.dma_start(keysB[:, :, :], T["keys"][1]).then_inc(bc_landed["keys1",], 16)
                pool.wait_ge(product.sem, product.count(("cqT", 3)))
                pool.dma_start(modbcp, mods[1, 1, 3:5].partition_broadcast(P)).then_inc(bc_landed["p1",], 16)

            @block.scalar
            def _(act):
                A_ = nc.scalar.activation
                for t in range(NTOK):
                    first = ((x_ready.sem, x_ready.count(("p0", 3))) if t < 2
                             else (product.sem, product.count(("ht", "m1", t - 2, 1))))
                    norm_act(act, "m1", t, hbuf1[:, t % 2, :], first)
                    if t:
                        norm_take(act, nc.scalar.copy, "m1", t - 1, 0, t - 1)
                norm_take(act, nc.scalar.copy, "m1", 3, 0, 3)
                junk = area(16384, QL)
                for t in range(NTOK):
                    for name, lo, n, i in (("lkv", QL, KVL, 0), ("lq", 0, QL, 1)):
                        if name == "lq" and t < 2:
                            continue
                        bank = in_bank(act, (name, t))
                        col = slice(2 * t + i, 2 * t + i + 1)
                        act_step(A_(junk[:, 0:n], bank[:, 0:n], ACT.Square, accum_out=lssq[:, col]))
                        act_step(A_(lrst[:, col], lssq[:, col], ACT.Sqrt, bias=eps_col, scale=1.0 / n))
                        width = KVL + ROPE if name == "lkv" else QL
                        free_bank(nc.scalar.copy(lat[:, t, lo:lo + width], bank[:, 0:width]), (name, t))
                        taken(act, (name, t))
                    act.sem_inc(lsq_ready, 1)
                for t in range(NTOK):
                    bank = in_bank(act, ("ckvT", t))
                    act_step(nc.scalar.copy(krT[0:ROPE, tok(t)], bank[0:ROPE, 256:384]))
                    free_bank(nc.scalar.copy(ckvT[:, :, tok(t)], bank[:, 0:256].rearrange("p (k t) -> p k t", k=2)),
                              ("ckvT", t))
                    if t >= 2:
                        bank = in_bank(act, ("cqT", t))
                        free_bank(nc.scalar.copy(cqT[:, :, tok(t - 2)], bank[:, 0:384].rearrange("p (k t) -> p k t", k=3)),
                                  ("cqT", t))
                for h in range(HC):
                    free_bank(nc.scalar.copy(qnT[:, h, :], in_bank(act, ("qn", h))[:, 0:256]), ("qn", h))
                for t in (2, 3):
                    for g in range(2):
                        bank = in_bank(act, ("qrT", t, g))
                        free_bank(nc.scalar.copy(qrT[0:ROPE, 4 * g:4 * g + 4, tok(t - 2)],
                                                 bank[0:ROPE, :].rearrange("p (h t) -> p h t", h=4)), ("qrT", t, g))
                for h in range(HC):
                    if h % 2 == 0:
                        free_bank(nc.scalar.copy(knT[:, h, :], in_bank(act, ("kn", h))), ("kn", h))
                for t in range(NTOK):
                    free_bank(nc.scalar.copy(vatt[:, t, 0:512], in_bank(act, ("v", t, 0))), ("v", t, 0))

                def turn_probs(u):
                    free_bank(nc.scalar.copy(probT[:, u % 2, :], in_bank(act, ("pT", u))), ("pT", u))

                for u in range(2 * HC):
                    bank = in_bank(act, ("sc", u))
                    act.wait_ge(nmax_ready.sem, nmax_ready.count(u))
                    if u >= 2:
                        act.wait_ge(product.sem, product.count(("pT", u - 2)))
                    free_bank(A_(prob[:, u % 2, :], bank, ACT.Exp, bias=nsmax[:, u:u + 1], scale=SC,
                                 accum_out=ssum[:, u:u + 1]), ("sc", u))
                    if u:
                        turn_probs(u - 1)
                turn_probs(2 * HC - 1)
                for i, t in enumerate((2, 3)):
                    norm_act(act, "p1", t, hx2[:, i, :], (x_ready.sem, x_ready.count(("m1", t))))
                    if i:
                        norm_take(act, nc.scalar.copy, "p1", t - 1, 0, i - 1)
                norm_take(act, nc.scalar.copy, "p1", 3, 0, 1)
                for h in range(PH):
                    free_bank(nc.scalar.copy(qT[:, h, 0:256], in_bank(act, ("q1", h))[:, 0:256]), ("q1", h))
                for i, t in enumerate((2, 3)):
                    for j in range(0, 4, 2):
                        bank = in_bank(act, ("s1", t, j))
                        free_bank(nc.scalar.copy(score[:, i, 2 * j:2 * j + 2, :],
                                                 bank.rearrange("p (h n) -> p h n", h=2)), ("s1", t, j))

            @block.vector
            def _(dve):
                V = nc.vector
                step = dve_step

                def rope(dst, src, t, nh, last_read):
                    s4, d4 = (v.rearrange("p (h a b n) -> p h a b n", h=nh, a=2, b=2) for v in (src, dst))
                    cs = [rope_cs[:, t, i].unsqueeze(1).broadcast_to((P, nh, 2, 16)) for i in range(2)]
                    tmps = [rtmp[:, i, 0:nh * 32].rearrange("p (h a n) -> p h a n", h=nh, a=2) for i in range(4)]
                    parts = [(0, 0), (1, 1), (1, 0), (0, 1)]
                    ins = [V.tensor_tensor(tmps[i], s4[:, :, :, b, :], cs[c], ALU.mult)
                           for i, (b, c) in enumerate(parts)]
                    if last_read is None:
                        step(*ins)
                    else:
                        free_bank(ins[-1], last_read)
                        step(*ins[:-1])
                        taken(dve, last_read)
                    return (V.tensor_tensor(d4[:, :, :, 0, :], tmps[0], tmps[1], ALU.subtract),
                            V.tensor_tensor(d4[:, :, :, 1, :], tmps[2], tmps[3], ALU.add))

                for t in range(NTOK):
                    if t % 2 == 0:
                        dve.wait_ge(bc_landed["m1", t // 2], 16)
                    bc = modbc1[t // 2]
                    norm_dve(dve, step, "m1", t, hbuf1[:, t % 2, :], bc[:, 1, :], bc[:, 0, :])
                    if t:
                        norm_take(dve, V.tensor_copy, "m1", t - 1, 1, t - 1)
                norm_take(dve, V.tensor_copy, "m1", 3, 1, 3)
                dve.wait_ge(bc_landed["lat",], 48)
                for t in range(NTOK):
                    dve.wait_ge(lsq_ready, t + 1)
                    for i, lo, n in ((0, QL, KVL), (1, 0, QL)):
                        if i and t < 2:
                            continue
                        r = lrst[:, 2 * t + i:2 * t + i + 1]
                        step(V.reciprocal(r, r))
                        step(V.scalar_tensor_tensor(out=lat[:, t, lo:lo + n], in0=lat[:, t, lo:lo + n], scalar=r,
                                                    in1=lat_gain[:, lo:lo + n], op0=ALU.mult, op1=ALU.mult))
                    if t >= 2:
                        kr = lat[:, t, QL + KVL:QL + KVL + ROPE]
                        step(*rope(kr, kr, t - 2, 1, None))
                    dve.sem_inc(lat_ready.sem, 1)
                for t in (2, 3):
                    step(*rope(qrope[:, t - 2, :], in_bank(dve, ("qr", t)), t - 2, HC, ("qr", t)))
                    dve.sem_inc(qr_ready.sem, 1)
                for h in range(HC):
                    if h % 2:
                        free_bank(V.tensor_copy(knT[:, h, :], in_bank(dve, ("kn", h))), ("kn", h))
                for t in range(NTOK):
                    free_bank(V.tensor_copy(vatt[:, t, 512:1024], in_bank(dve, ("v", t, 1))), ("v", t, 1))

                def take_o(u):
                    free_bank(V.tensor_copy(oT[:, u // 2, tok(u % 2)], in_bank(dve, ("oT", u))[:, 0:P]), ("oT", u))

                for u in range(2 * HC):
                    bank = in_bank(dve, ("sc", u))
                    c = slice(u, u + 1)
                    step(V.tensor_reduce(smax[:, c], bank, AX, ALU.max))
                    nmax_ready.mark(V.tensor_scalar(nsmax[:, c], smax[:, c], -SC, None, ALU.mult), u)
                    taken(dve, ("sc", u))
                    step(V.reciprocal(srec[:, c], ssum[:, c]))
                    prob_ready.mark(V.tensor_scalar(prob[:, u % 2, :], prob[:, u % 2, :], srec[:, c], None, ALU.mult), u)
                    if u:
                        take_o(u - 1)
                take_o(2 * HC - 1)
                dve.wait_ge(bc_landed["g1",], 16)
                for t in (2, 3):
                    for c in range(2):
                        residual_half(dve, "out1", "m1", t, c, gate1, rtmp.rearrange("p (a b) n -> p a (b n)", a=2))
                dve.wait_ge(bc_landed["p1",], 16)
                for i, t in enumerate((2, 3)):
                    norm_dve(dve, step, "p1", t, hx2[:, i, :], modbcp[:, 1, :], modbcp[:, 0, :])
                    if i:
                        norm_take(dve, V.tensor_copy, "p1", t - 1, 1, i - 1)
                norm_take(dve, V.tensor_copy, "p1", 3, 1, 1)
                for i, t in enumerate((2, 3)):
                    for j in range(1, 4, 2):
                        bank = in_bank(dve, ("s1", t, j))
                        free_bank(V.tensor_copy(score[:, i, 2 * j:2 * j + 2, :],
                                                bank.rearrange("p (h n) -> p h n", h=2)), ("s1", t, j))

            @block.tensor
            def _(pe):
                M, TR = nc.tensor.matmul, nc.tensor.transpose

                def accumulate(dst, pairs):
                    for i, (l, r) in enumerate(pairs):
                        last = M(dst, l, r, start=(i == 0), stop=(i == len(pairs) - 1))
                    return last

                for t in range(NTOK):
                    norm_pe(pe, "m1", t, hbuf1[:, t % 2, :])
                for t in range(NTOK):
                    for half in range(2):
                        taken(pe, ("ht", "m1", t, half))
                for t in range(NTOK):
                    for name, key, n in (("lkv", "w_kv1", KVL + ROPE), ("lq", "w_q_1", QL)):
                        if name == "lq" and t < 2:
                            continue
                        w = weights(pe, (key,))[:, 0:KT * n].rearrange("p (k n) -> p k n", k=KT)
                        bank = out_bank(pe, (name, t))
                        product.mark(accumulate(bank[:, 0:n], [(hT[:, k, tok(t)], w[:, k, :]) for k in range(KT)]),
                                     (name, t))
                for t in range(NTOK):
                    pe.wait_ge(lat_ready.sem, t + 1)
                    bank = out_bank(pe, ("ckvT", t))
                    for k in range(2):
                        TR(bank[:, k * P:(k + 1) * P], lat[:, t, QL + k * P:QL + (k + 1) * P], const(IDENT))
                    product.mark(TR(bank[0:ROPE, 256:384], lat[:, t, QL + KVL:QL + KVL + ROPE], const(IDENT)),
                                 ("ckvT", t))
                    if t >= 2:
                        bank = out_bank(pe, ("cqT", t))
                        for k in range(3):
                            last = TR(bank[:, k * P:(k + 1) * P], lat[:, t, k * P:(k + 1) * P], const(IDENT))
                        product.mark(last, ("cqT", t))
                for t in range(NTOK):
                    taken(pe, ("ckvT", t))
                for t in (2, 3):
                    taken(pe, ("cqT", t))
                w = weights(pe, ("w_uq_n",))[:, 0:3 * D].rearrange("p (k n) -> p k n", k=3)
                for h in range(HC):
                    bank = out_bank(pe, ("qn", h))
                    product.mark(accumulate(bank[:, 0:256], [(w[:, k, h * P:(h + 1) * P], cqT[:, k, :])
                                                             for k in range(3)]), ("qn", h))
                w = weights(pe, ("w_uq_r",))[:, 0:3 * 512].rearrange("p (k n) -> p k n", k=3)
                for t in (2, 3):
                    bank = out_bank(pe, ("qr", t))
                    product.mark(accumulate(bank, [(cqT[:, k, tok(t - 2)], w[:, k, :]) for k in range(3)]), ("qr", t))
                for t in (2, 3):
                    pe.wait_ge(qr_ready.sem, t - 1)
                    for g in range(2):
                        bank = out_bank(pe, ("qrT", t, g))
                        for j in range(4):
                            h = 4 * g + j
                            last = TR(bank[0:ROPE, j * P:(j + 1) * P], qrope[:, t - 2, h * ROPE:(h + 1) * ROPE],
                                      const(IDENT))
                        product.mark(last, ("qrT", t, g))
                w = weights(pe, ("w_ukv",)).rearrange("p (k n) -> p k n", k=2)
                for h in range(HC):
                    bank = out_bank(pe, ("kn", h))
                    product.mark(accumulate(bank, [(w[:, k, h * P:(h + 1) * P], ckvT[:, k, :]) for k in range(2)]),
                                 ("kn", h))
                for t in range(NTOK):
                    for c in range(2):
                        bank = out_bank(pe, ("v", t, c))
                        product.mark(accumulate(bank, [(ckvT[:, k, tok(t)], w[:, k, D + 512 * c:D + 512 * c + 512])
                                                       for k in range(2)]), ("v", t, c))
                for h in range(HC):
                    taken(pe, ("kn", h))
                    taken(pe, ("qn", h))
                for t in (2, 3):
                    for g in range(2):
                        taken(pe, ("qrT", t, g))
                for t in range(NTOK):
                    for c in range(2):
                        taken(pe, ("v", t, c))

                def attend(u):
                    h = u // 2
                    pe.wait_ge(prob_ready.sem, prob_ready.count(u))
                    bank = out_bank(pe, ("pT", u))
                    for k in range(4):
                        last = TR(bank[:, k * P:(k + 1) * P], prob[:, u % 2, k * P:(k + 1) * P], const(IDENT))
                    product.mark(last, ("pT", u))
                    taken(pe, ("pT", u))
                    bank = out_bank(pe, ("oT", u))
                    product.mark(accumulate(bank[:, 0:P], [(vatt[:, k, h * P:(h + 1) * P],
                                                            probT[:, u % 2, k * P:(k + 1) * P]) for k in range(4)]),
                                 ("oT", u))

                for u in range(2 * HC):
                    h = u // 2
                    bank = out_bank(pe, ("sc", u))
                    product.mark(accumulate(bank, [(qnT[:, h, tok(u % 2)], knT[:, h, :]),
                                                   (qrT[0:ROPE, h, tok(u % 2)], krT[0:ROPE, :])]), ("sc", u))
                    if u:
                        attend(u - 1)
                attend(2 * HC - 1)
                for u in range(2 * HC):
                    taken(pe, ("oT", u))
                for i, t in enumerate((2, 3)):
                    for c in range(2):
                        w = weights(pe, ("w_out1", c)).rearrange("p (k n) -> p k n", k=KT)
                        bank = out_bank(pe, ("out1", t, c))
                        product.mark(accumulate(bank, [(oT[:, k, tok(i)], w[:, k, :]) for k in range(KT)]),
                                     ("out1", t, c))
                for i, t in enumerate((2, 3)):
                    norm_pe(pe, "p1", t, hx2[:, i, :])
                peer_scores_pe(pe, "1", (2, 3), bc_landed["keys1",])

        for part in (first_block, sums_and_mixer, second_block, last_sums):
            with nc.Block() as block:
                part(block)


def constants():
    r, c = np.mgrid[0:P, 0:P]
    mats = [r == c, r >= 0, r <= c, r > c, r >= c, r < c, r < 0]
    lower = [(r // s == c // s + 1) & (c // s % 2 == 0) for s in LEVELS]
    mats += lower + [m.T for m in lower]
    consts = np.concatenate([m.astype(np.float32) for m in mats], axis=1)
    iota = np.tile(np.arange(TOPK, dtype=np.float32), (P, 1))
    n = ROPE // 4
    freqs = (np.float32(10000.0) ** (-np.arange(n, dtype=np.float32) / np.float32(n))).astype(np.float32)
    t = np.arange(2 * P)
    ang = np.stack([(t // GRID_W).astype(np.float32)[:, None] * freqs, (t % GRID_W).astype(np.float32)[:, None] * freqs], 1)
    rope = np.stack([np.cos(ang), np.sin(ang)], 1).astype(np.float32)
    rope = rope.reshape(2, P, 2, 2, n).transpose(1, 0, 2, 3, 4)
    return consts, iota, np.ascontiguousarray(rope)


def kernel(**inputs):
    import concourse.bacc as bacc
    from concourse.bass_utils import run_bass_kernel_spmd

    a = {k: np.asarray(v) for k, v in inputs.items()}
    consts, iota, rope = constants()
    uq = a["od_w_uq"][0].reshape(QL, HC, NOPE + ROPE)
    ukv = a["od_w_ukv"][0].reshape(KVL, HC, NOPE + VD)
    keys = np.zeros((2, P, PH, 2, NKEY), np.float32)
    for p in range(2):
        keys[:, 64 * p:64 * p + 64, :, p, :] = a["p_keys"][:, :, p].transpose(0, 3, 1, 2)
    arrays = {
        "x": a["x"][0], "ctx": a["ctx"][0],
        "c_cols": np.stack([a["c_ctx"].reshape(KT, P), a["c"][0].reshape(KT, P)], 2).transpose(1, 0, 2).reshape(P, 2 * KT),
        "w_mod": a["w_mod"], "b_mod": a["b_mod"].reshape(2, 6, D),
        "norms": np.stack([a["norm1"], a["norm2"]], 1)[None],
        "ev_w_in": a["ev_w_in"][0],
        "conv_w": np.concatenate([a["ev_a_conv"][0], a["ev_qkv_conv"][0]], 1).reshape(3, 16, P).transpose(2, 1, 0),
        "a_log": a["ev_a_log"].reshape(8), "dt_bias": a["ev_dt_bias"].reshape(8),
        "o_norm": a["ev_o_norm"][0], "ev_w_out": a["ev_w_out"][0],
        "od_w_in": a["od_w_in"][0], "q_norm": a["od_q_norm"][0], "kv_norm": a["od_kv_norm"][0],
        "uq_nope": uq[:, :, :NOPE].reshape(QL, -1), "uq_rope": uq[:, :, NOPE:].reshape(QL, -1),
        "ukv": np.concatenate([ukv[:, :, :NOPE].reshape(KVL, -1), ukv[:, :, NOPE:].reshape(KVL, -1)], 1),
        "od_w_out": a["od_w_out"][0], "p_w_q": a["p_w_q"], "keys": keys.reshape(2, P, PH, 2 * NKEY),
        "experts0": np.concatenate([a["p_u"][0], a["p_v"][0]], 1),
        "experts1": np.concatenate([a["p_u"][1], a["p_v"][1]], 1),
        "norm_f": a["norm_f"], "consts": consts, "iota16": iota, "rope": rope,
    }
    nc = bacc.Bacc("TRN2", target_bir_lowering=False, num_devices=1)
    feed, T = {}, {}
    for name, v in arrays.items():
        feed[f"in_{name}"] = np.ascontiguousarray(v)
        T[name] = nc.dram_tensor(f"in_{name}", v.shape, F32, kind="ExternalInput").ap()
    out = nc.dram_tensor("out", (2 * P, D), F32, kind="ExternalOutput").ap()
    build(nc, T, out)
    r = run_bass_kernel_spmd(nc, [feed], core_ids=[0])
    return r.results[0]["out"].reshape(1, 2 * P, D)
```

```python
from contextlib import ExitStack

import numpy as np
import concourse.bass as bass
from concourse import mybir

F32 = mybir.dt.float32
U32 = mybir.dt.uint32
ALU = mybir.AluOpType
ACT = mybir.ActivationFunctionType
AX = mybir.AxisListType.X

P = 128
D = 1024
KT = D // P
NTOK = 4
EPS = 1e-6
HB = 4
DK = 128
HC = 8
NOPE, ROPE, VD = 128, 64, 128
QL, KVL = 384, 256
UNITS = 2 * HC
PH = 8
NKEY = 128
TOPK = 16
GRID_W = 64
LEVELS = [1, 2, 4, 8, 16, 32, 64]

IDENT, ONES, LE, GT, GE, LT, ZERO = range(7)
LOWER = {s: 7 + i for i, s in enumerate(LEVELS)}
UPPER = {s: 14 + i for i, s in enumerate(LEVELS)}
NCONST = 21

RING = 8
GRP = 2
SLOTS = PH * TOPK
NBANK = 6


class Order:

    def __init__(self, sem, events):
        self.sem = sem
        self.events = list(events)
        self.at = {e: i + 1 for i, e in enumerate(self.events)}
        assert len(self.at) == len(self.events)
        self.done = 0

    def count(self, event):
        return self.at[event]

    def mark(self, ins, event):
        assert self.events[self.done] == event, (self.events[self.done], event)
        self.done += 1
        ins.then_inc(self.sem, 1)


class Steps:

    def __init__(self, eng, sem, waited):
        self.eng, self.sem, self.waited, self.base, self.n = eng, sem, waited, 0, 0

    def start(self, base):
        self.base, self.n = base, 0

    def __call__(self, *instructions, apart=False):
        for ins in instructions:
            ins.then_inc(self.sem, 1)
            self.n += 1
        self.eng.wait_ge(self.sem, self.base + self.n)
        if apart:
            self.wait_apart()

    def wait_apart(self):
        self.eng.sem_inc(self.waited, 1)


def mixer_groups(s):
    tiles = (2 * s, 2 * s + 1)
    g = [(n, t) for t in tiles for n in ("ktok", "vtok")]
    for q in tiles:
        g += [(n, q, d) for n in ("D", "KK", "AT", "QK") for d in range(2)]
        for lv in LEVELS[1:]:
            g += [("P1", q, d, lv) for d in range(2)]
            if lv == LEVELS[1]:
                g += [("intraT", q, d) for d in range(2)]
            if lv == LEVELS[-1]:
                g += [(n, q, d) for n in ("KS", "QS") for d in range(2)]
            for d in range(2):
                g += [("XBX", q, d, lv)] + ([("YBY", q, d, lv)] if lv != LEVELS[-1] else [])
        g += [(n, q, d) for n in ("vnew", "intraV", "dS") for d in range(2)]
    g += [("ybT", t) for t in tiles] + [("out0", t, c) for t in tiles for c in range(2)]
    g += [("ht", "p0", t, h) for t in tiles for h in range(2)]
    for j in range(5):
        if j < 4:
            g += [("q0", s, 2 * j), ("q0", s, 2 * j + 1)]
        if j:
            g += [("s0", t, j - 1) for t in tiles]
    return g


def group_names():
    first = [("ht", "m0", t, h) for t in range(NTOK) for h in range(2)]
    for b in range(24):
        first += [("proj", b)] + ([("sumsq", b - 14)] if 14 <= b < 22 else [])
    first += [("z", t) for t in range(NTOK)] + [("ab",), ("cum",)]
    first += mixer_groups(0) + mixer_groups(1)
    second = [("ht", "m1", t, h) for t in range(NTOK) for h in range(2)]
    second += [(n, t) for t in range(NTOK) for n in (("lkv", "lq") if t >= 2 else ("lkv",))]
    second += [(n, t) for t in range(NTOK) for n in (("ckvT", "cqT") if t >= 2 else ("ckvT",))]
    second += [("qn", h) for h in range(HC)] + [("qr", t) for t in (2, 3)]
    second += [("qrT", t, g) for t in (2, 3) for g in range(2)]
    second += [("kn", h) for h in range(HC)] + [("v", t, h) for t in range(NTOK) for h in range(2)]
    for u in range(UNITS + 3):
        second += [(n, v) for n, v in (("sc", u), ("pT", u - 2), ("oT", u - 3)) if 0 <= v < UNITS]
    second += [("out1", t, h) for t in (2, 3) for h in range(2)]
    second += [("ht", "p1", t, h) for t in (2, 3) for h in range(2)]
    for j in range(5):
        second += [("q1", h) for h in (2 * j, 2 * j + 1) if h < PH]
        second += [("s1", t, j - 1) for t in (2, 3) if j]
    return first + second


MODS = [(i, c) for i in range(2) for c in range(12)]
MODS_FIRST = 6
MODS_SECOND = 2


def weight_loads():
    mods = [(("mod", i, c), ("mod", i, c)) for i, c in MODS]
    loads = mods[:MODS_FIRST]
    loads += [(("w_in", c), ("proj", 4 * c + 3)) for c in range(6)]
    loads += [(("w_in", 6), ("z", 3)), (("w_ab",), ("ab",))] + mods[MODS_FIRST:]
    loads += [(("w_out0", 0, c), ("out0", 1, c)) for c in range(2)]
    loads += [(("w_q0", 0, c), ("q0", 0, 4 * c + 3)) for c in range(2)]
    loads = [(n, last, i % 3) for i, (n, last) in enumerate(loads)]
    loads += [(("w_out0", 1, c), ("out0", 3, c), c) for c in range(2)]
    loads += [(("w_q0", 1, c), ("q0", 1, 4 * c + 3), c) for c in range(2)]
    second = [(("w_kv1",), ("lkv", 3)), (("w_q_1",), ("lq", 3))]
    second += [(("w_uq_n",), ("qn", 7)), (("w_uq_r",), ("qr", 3)), (("w_ukv",), ("v", 3, 1))]
    second += [(("w_out1", c), ("out1", 3, c)) for c in range(2)]
    second += [(("w_q1", c), ("q1", 4 * c + 3)) for c in range(2)]
    return loads + [(n, last, i % 3) for i, (n, last) in enumerate(second)]


def build(nc, T, out):
    with ExitStack() as ctx:
        def sb(name, shape, dt=F32):
            return ctx.enter_context(nc.sbuf_tensor(name, shape, dt))

        def sem(name):
            return ctx.enter_context(nc.semaphore(name))

        consts = sb("consts", [P, NCONST * P])
        x = sb("x", [P, NTOK, D])
        wring = sb("wring", [P, 3 * 4096])
        arena = sb("arena", [P, 28672])
        small = sb("small", [P, 1024])
        conv_w = sb("conv_w", [P, 16, 3])
        hx_cur = sb("hx_cur", [P, D])
        score_cur = sb("score_cur", [P, 2 * NKEY])
        score_left = sb("score_left", [P, 2 * NKEY])
        cand = sb("cand", [P, TOPK * TOPK])
        cand_left = sb("cand_left", [P, TOPK * TOPK])
        onehot = sb("onehot", [P, TOPK * TOPK])
        iota16 = sb("iota16", [P, TOPK])
        top_val = sb("top_val", [P, 2, TOPK])
        top_idx = sb("top_idx", [P, 2, TOPK], U32)
        top_idx_f = sb("top_idx_f", [P, 2, TOPK])
        best = sb("best", [P, TOPK])
        best_pos = sb("best_pos", [P, TOPK], U32)
        pos_ab = sb("pos_ab", [P, 2, TOPK], U32)
        pos_ab_f = sb("pos_ab_f", [P, 2, TOPK])
        sel_ab = sb("sel_ab", [P, 2, TOPK])
        gate_stat = sb("gate_stat", [P, 3])
        gate_exp = sb("gate_exp", [P, TOPK])
        expert_cur = sb("expert_cur", [P, 2, TOPK], U32)
        gate_cur = sb("gate_cur", [P, 2, TOPK])
        dots = sb("dots", [P, 2, TOPK])
        acts = sb("acts", [P, 2, TOPK])
        coef = sb("coef", [P, 2, TOPK])
        diag = sb("diag", [P, RING, P])
        ps = ctx.enter_context(nc.psum_tensor("ps", [P, 8, 512], F32))
        mods = nc.dram_tensor("mods", (2, 2, 6, D), F32, kind="Internal").ap()

        def const(i):
            return consts[:, i * P:(i + 1) * P]

        def area(at, *shape, of=None):
            n = int(np.prod(shape))
            flat = arena if of is None else of
            assert at + n <= flat.shape[1]
            a = flat[:, at:at + n]
            if len(shape) == 1:
                return a
            names = "abcd"[:len(shape)]
            return a.rearrange(f"p ({' '.join(names)}) -> p {' '.join(names)}",
                               **{k: s for k, s in zip(names[:-1], shape)})

        mod_row = [hx_cur[:, P * k:P * k + P] for k in range(4)]
        norm_row = [diag[:, k, :] for k in range(4)]
        hT = area(0, KT, 512)
        bgcg = area(4096, 8, 512)
        STREAM = 12288

        def both_streams(at):
            low = at % 4096
            start = at - low
            return arena[:, start:start + STREAM + 4096].rearrange("p (s r) -> p s r", r=4096)[
                :, 0:4:3, low:low + 256]

        def qkv_block(b):
            return both_streams(8192 + 256 * b)

        def ya_block(b):
            return both_streams(14336 + 256 * b)

        conv_in = area(12288, 4, 512)
        hbuf0 = area(16384, 2, D)
        modbc0 = [area(18432, 2, D), area(24576, 2, D)]

        def mixer_memory(s):
            base, flat = (0, arena) if s == 0 else (0, wring)
            names = ("lg", "A", "gam", "intra", "intraT", "X", "Y", "Bm")
            m = {n: area(base + 1024 * i, 2, 512, of=flat) for i, n in enumerate(names)}
            shift = STREAM * s
            m["qkv"] = area(8192 + shift, 12, 256)
            m["z"] = area(11264 + shift, 2, 512)
            m["ya"] = area(14336 + shift, 4, 256)
            m["score"] = area(16384 + 4096 * s, 2, PH, 256)
            m["hx2"] = area(24576 + 2048 * s, 2, D)
            if s == 0:
                m |= {"yb": area(15360, 4, 256), "ktok": area(12288, 2, 512), "vtok": area(13312, 2, 512),
                      "P1s": area(16384, 2, 512), "oacc": area(18432, 2, 512), "gate": area(19456, D),
                      "rows": area(17408, 2, 512), "modbc": area(0, 2, D), "hT": area(2048, KT, 256),
                      "qT": area(4096, PH, 256), "keys": area(6144, PH, 256), "osq": area(0, 2, 512)}
            else:
                w = lambda at, *shape: area(at, *shape, of=wring)
                m |= {"yb": area(20480, 4, 256), "ktok": w(10240, 2, 512), "vtok": w(11264, 2, 512),
                      "P1s": w(8192, 2, 512), "oacc": w(9216, 2, 512), "gate": w(8192, D),
                      "rows": w(9216, 2, 512), "modbc": w(10240, 2, D), "hT": w(8192, KT, 256),
                      "qT": area(16384, PH, 256), "keys": w(10240, PH, 256), "osq": w(0, 2, 512)}
            m |= {"R": m["gam"], "vn": m["lg"], "tmp": m["intra"], "kdK": m["Bm"]}
            return m

        MEM = [mixer_memory(s) for s in range(2)]
        S = area(27648, 2, 512)
        qT = area(4096, PH, 512)
        keysB = area(8192, PH, 256)
        modbcp = area(10240, 2, D)
        score = area(16384, NTOK, PH, 256)
        hx2 = area(24576, NTOK, D)
        ring = area(0, RING, 2 * D)
        peer_gate = area(8192, 2, D, of=wring)
        hbuf1 = area(4096, 2, D)
        modbc1 = [area(16384, 2, D), area(18432, 2, D)]
        lat = area(10240, NTOK, 704)
        cqT = area(13056, 3, 256)
        ckvT = area(13824, 2, 512)
        krT = area(14848, 512)
        lat_gain = area(15360, 640)
        rope_cs = area(16000, 2, 2, 2, 16)
        knT = area(16384, HC, 512)
        vatt = area(20480, NTOK, D)
        qnT = area(24576, HC, 256)
        qrope = area(26624, 2, 512)
        rtmp = area(27648, 4, 256)
        qrT = area(0, HC, 256)
        prob = area(2048, 3, 512)
        probT = area(26624, 2, 512)
        oT = area(4096, HC, 256)
        gate1 = area(6144, D)
        kdup = area(7168, 128)
        hfin = area(2048, 2, D)
        gain_f = area(0, D, of=wring)

        sT = small[:, 0:16]
        ab = small[:, 16:80].rearrange("p (t c) -> p t c", t=NTOK)
        ssq = small[:, 80:104]
        rstd = small[:, 104:128]
        alog = small[:, 128:136]
        dtb = small[:, 136:144]
        nexpa = small[:, 144:152]
        gdec = small[:, 152:184].rearrange("p (t c) -> p t c", t=NTOK)
        g1 = small[:, 184:216].rearrange("p (t c) -> p t c", t=NTOK)
        g2 = small[:, 216:248].rearrange("p (t c) -> p t c", t=NTOK)
        beta = small[:, 248:280].rearrange("p (t c) -> p t c", t=NTOK)
        expo = small[:, 280:376]
        edec = expo[:, 0:32].rearrange("p (d t h) -> p d t h", d=2, t=NTOK)
        erest = expo[:, 32:64].rearrange("p (d t h) -> p d t h", d=2, t=NTOK)
        eall = expo[:, 64:96].rearrange("p (t d h) -> p t d h", t=NTOK, d=2)
        ossq = small[:, 376:392]
        orst = small[:, 392:408]
        lssq = small[:, 408:416]
        lrst = small[:, 416:424]
        smax = small[:, 424:440]
        nsmax = small[:, 440:456]
        ssum = small[:, 456:472]
        srec = small[:, 472:488]
        sTin = small[:, 488:504]
        eps_col = small[:, 504:505]
        ogain = small[:, 512:640]

        GROUPS = group_names()
        product = Order(sem("product_done"), GROUPS)
        bank_free = [sem(f"bank_free{b}") for b in range(NBANK)]
        w_landed = [sem(f"w_landed{i}") for i in range(3)]
        x_landed = sem("x_landed")
        consts_landed = sem("consts_landed")
        c_landed = sem("c_landed")
        row_landed = [sem(f"mod_bias_landed{i}") for i in range(4)]
        mod_done = sem("mod_chunk_done")
        mod_taken = sem("mod_chunk_taken")
        rows_stored = [sem(f"mod_rows_stored{i}") for i in range(2)]
        bc_names = [("m0", 0), ("m0", 1), ("g0", 0), ("g0", 1), ("p0", 0), ("p0", 1), ("keys0", 0), ("keys0", 1),
                    ("m1", 0), ("m1", 1), ("lat",), ("g1",), ("p1",), ("keys1",), ("pg0",), ("pg1",), ("nf",)]
        bc_landed = {n: sem("landed_" + "_".join(map(str, n))) for n in bc_names}
        act_steps = sem("act_steps")
        dve_steps = sem("dve_steps")
        pool_steps = sem("pool_steps")
        norm_events = ([("m0", t) for t in range(NTOK)] + [("p0", t) for t in range(NTOK)]
                       + [("m1", t) for t in range(NTOK)] + [("p1", t) for t in (2, 3)]
                       + [("f", t) for t in (2, 3)])
        ssq_ready = Order(sem("ssq_ready"), norm_events)
        h_ready = Order(sem("h_ready"), norm_events)
        silu_c = sem("silu_c_ready")
        rows_ready = sem("mod_rows_ready")
        xa_conv = Order(sem("xa_scaled"), [("xa", b) for b in range(4)])
        u_ready = Order(sem("gated_input_ready"), [("u", b) for b in range(4)])
        conv_ready = Order(sem("conv_ready"), [("conv", b) for b in range(12)])
        centre_ready = Order(sem("centre_tap_ready"), list(range(12)))
        eps_ready = sem("eps_ready")
        silu_ready = Order(sem("qkv_silu_ready"), [("silu", b) for b in range(12)])
        square_ready = Order(sem("qk_square_ready"), [("sq", b) for b in range(8)])
        qk_ready = sem("qk_normed")
        ya_ready = sem("y_a_ready")
        sp_act = sem("softplus_act")
        sp_dve = sem("softplus_dve")
        pq = [(q, d) for q in range(4) for d in range(2)]
        lg_ready = Order(sem("lg_ready"), pq)
        ai_ready = Order(sem("a_intra_ready"), [(n, q, d) for q in range(4) for n in "AI" for d in range(2)])
        xy_ready = Order(sem("xy_ready"), [(n, q, d, s) for q in range(4) for s in LEVELS for d in range(2)
                                           for n in ("XY" if s != LEVELS[-1] else "X")])
        bm_ready = Order(sem("level_ready"), [(q, d, s) for q in range(4) for s in LEVELS[1:] for d in range(2)])
        kd_ready = Order(sem("kd_ready"), pq)
        r_ready = Order(sem("r_ready"), pq)
        s_ready = Order(sem("state_ready"), ["zero"] + pq)
        osq_ready = Order(sem("o_square_ready"), list(range(NTOK)))
        yb_ready = Order(sem("y_b_ready"), list(range(NTOK)))
        x_ready = Order(sem("x_ready"), [("m0", t) for t in range(NTOK)] + [("p0", t) for t in range(NTOK)]
                        + [("m1", t) for t in (2, 3)] + [("p1", t) for t in (2, 3)])
        lsq_ready = sem("latent_square_ready")
        lat_ready = Order(sem("latent_ready"), list(range(NTOK)))
        qr_ready = Order(sem("q_rope_ready"), [2, 3])
        nmax_ready = Order(sem("row_max_ready"), list(range(2 * HC)))
        pexp_ready = Order(sem("exp_ready"), list(range(2 * HC)))
        prob_ready = Order(sem("prob_ready"), list(range(2 * HC)))
        stored = sem("stored")
        slot_landed = [sem(f"slot_landed{k}") for k in range(RING)]
        slot_free = sem("slot_free")
        dots_ready = sem("dots_ready")
        coef_ready = sem("coef_ready")
        diag_ready = sem("diag_ready")
        ranked = sem("head_ranked")
        gmax_ready = sem("gate_max_ready")
        gexp_ready = sem("gate_exp_ready")
        peer_taken = sem("peer_tile_taken")
        gated = Order(sem("gated_sum_ready"), [(0, t) for t in range(NTOK)] + [(1, t) for t in (2, 3)])

        def bank_of(name):
            return (product.count(name) - 1) % NBANK

        def out_bank(pe, name):
            n = product.count(name) - 1
            if n >= NBANK:
                pe.wait_ge(bank_free[n % NBANK], n // NBANK)
            return ps[:, n % NBANK, :]

        def in_bank(eng, name):
            eng.wait_ge(product.sem, product.count(name))
            return ps[:, bank_of(name), :]

        def free_bank(ins, name):
            ins.then_inc(bank_free[bank_of(name)], 1)

        def taken(eng, name):
            n = product.count(name) - 1
            eng.wait_ge(bank_free[n % NBANK], n // NBANK + 1)

        LOADS = weight_loads()
        load_at, slot_uses, last_use = {}, [0, 0, 0], [None, None, None]
        for name, last, slot in LOADS:
            slot_uses[slot] += 1
            load_at[name] = (slot, slot_uses[slot], last_use[slot])
            last_use[slot] = last

        def weights(eng, name):
            slot, use, _ = load_at[name]
            eng.wait_ge(w_landed[slot], 16 * use)
            return wring[:, slot * 4096:(slot + 1) * 4096]

        def load_weight(sp, name, src):
            slot, _, before = load_at[name]
            if before is not None and before[0] == "mod":
                sp.wait_ge(mod_done, MODS.index(before[1:]) + 1)
            elif before is not None:
                sp.wait_ge(product.sem, product.count(before))
            k, n = src.shape[1], src.shape[2]
            dst = wring[:, slot * 4096:slot * 4096 + k * n].rearrange("p (k n) -> p k n", k=k)
            sp.dma_start(dst, src).then_inc(w_landed[slot], 16)

        def ktiles(w, lo, hi):
            return w.rearrange("(k p) n -> p k n", p=P)[:, :, lo:hi]

        def heads(ap):
            return ap.rearrange("p (h c) -> p h c", h=HB)

        def over_heads(matrix):
            return matrix.unsqueeze(1).broadcast_to((P, HB, P))

        def per_head(col):
            return col.unsqueeze(2).broadcast_to((P, HB, P))

        def tok(t):
            return slice(t * P, (t + 1) * P)

        def unit(q, d):
            s, k = q // 2, q % 2
            return 2 * s + (k if d == 0 else 1 - k)

        INCL = (GE, LE)
        SUM_TO = (LE, GE)
        SUM_REST = (GT, LT)
        MASK = (LOWER, UPPER)

        def norm_act(act, stage, t, dst, first):
            e = ssq_ready.count((stage, t)) - 1
            act.wait_ge(*first)
            act_step(nc.scalar.activation(dst, x[:, t, :], ACT.Square, accum_out=ssq[:, e:e + 1]))
            ssq_ready.mark(nc.scalar.activation(rstd[:, e:e + 1], ssq[:, e:e + 1], ACT.Sqrt, bias=eps_col,
                                                scale=1.0 / D), (stage, t))

        def norm_dve(dve, step, stage, t, dst, gain, shift):
            e = ssq_ready.count((stage, t)) - 1
            dve.wait_ge(ssq_ready.sem, e + 1)
            step(nc.vector.reciprocal(rstd[:, e:e + 1], rstd[:, e:e + 1]))
            last = nc.vector.scalar_tensor_tensor(out=dst, in0=x[:, t, :], scalar=rstd[:, e:e + 1], in1=gain,
                                                  op0=ALU.mult, op1=ALU.mult)
            if shift is not None:
                step(last)
                last = nc.vector.tensor_tensor(dst, dst, shift, ALU.add)
            h_ready.mark(last, (stage, t))

        def norm_pe(pe, stage, t, src):
            pe.wait_ge(h_ready.sem, h_ready.count((stage, t)))
            for half in range(2):
                name = ("ht", stage, t, half)
                bank = out_bank(pe, name)
                for j in range(4):
                    c = 4 * half + j
                    last = nc.tensor.transpose(bank[:, j * P:(j + 1) * P], src[:, c * P:(c + 1) * P], const(IDENT))
                product.mark(last, name)

        def norm_take(eng, copy, stage, t, half, slot, dst=None):
            bank = in_bank(eng, ("ht", stage, t, half))
            free_bank(copy((hT if dst is None else dst)[:, 4 * half:4 * half + 4, tok(slot)], bank.rearrange("p (k t) -> p k t", k=4)),
                      ("ht", stage, t, half))

        def residual_half(dve, product_name, stage, t, c, gate, rows):
            cols = slice(512 * c, 512 * c + 512)
            bank = in_bank(dve, (product_name, t, c))
            free_bank(nc.vector.tensor_tensor(rows[:, c, :], bank, gate[:, cols], ALU.mult), (product_name, t, c))
            taken(dve, (product_name, t, c))
            last = nc.vector.tensor_tensor(x[:, t, cols], x[:, t, cols], rows[:, c, :], ALU.add)
            if c:
                x_ready.mark(last, (stage, t))

        def peer_scores_pe(pe, layer, tiles, keys_landed):
            n = P * len(tiles)
            for t in tiles:
                for half in range(2):
                    taken(pe, ("ht", "p" + layer, t, half))
            for j in range(5):
                for h in (2 * j, 2 * j + 1) if j < 4 else ():
                    w = weights(pe, ("w_q" + layer, h // 4)).rearrange("p (k n) -> p k n", k=KT)
                    c = (h % 4) * P
                    bank = out_bank(pe, ("q" + layer, h))
                    for k in range(KT):
                        last = nc.tensor.matmul(bank[:, 0:n], w[:, k, c:c + P], hT[:, k, 0:n],
                                                start=(k == 0), stop=(k == KT - 1))
                    product.mark(last, ("q" + layer, h))
                if j:
                    pe.wait_ge(keys_landed, 16)
                for i, t in enumerate(tiles) if j else ():
                    bank = out_bank(pe, ("s" + layer, t, j - 1))
                    for k in range(2):
                        h = 2 * j - 2 + k
                        taken(pe, ("q" + layer, h))
                        last = nc.tensor.matmul(bank[:, 256 * k:256 * k + 256], qT[:, h, tok(i)], keysB[:, h, :],
                                                start=True, stop=True)
                    product.mark(last, ("s" + layer, t, j - 1))

        pool_step, act_step, dve_step = (Steps(e, s, sem("waited_" + n)) for e, s, n in (
            (nc.gpsimd, pool_steps, "pool"), (nc.scalar, act_steps, "act"), (nc.vector, dve_steps, "dve")))

        def wait_stored(eng, n):
            for m in (n - 1, n):
                eng.wait_ge(rows_stored[m % 2], 32 * (m // 2 + 1))

        def mixer_dma(sp, s):
            m = MEM[s]
            last = 2 * s + 1
            if s == 1:
                sp.wait_ge(product.sem, product.count(("dS", 3, 1)))
                sp.wait_ge(s_ready.sem, s_ready.count((3, 1)))
                sp.wait_ge(osq_ready.sem, osq_ready.count(3))
            for c in range(2):
                load_weight(sp, ("w_out0", s, c), ktiles(T["ev_w_out"], c * 512, (c + 1) * 512))
            if s == 0:
                sp.wait_ge(h_ready.sem, h_ready.count(("m0", 1)))
            wait_stored(sp, 5)
            sp.dma_start(m["gate"], mods[0, s, 2].partition_broadcast(P)).then_inc(bc_landed["g0", s], 16)
            if s == 0:
                sp.wait_ge(osq_ready.sem, osq_ready.count(1))
            wait_stored(sp, 9)
            sp.dma_start(m["modbc"], mods[0, s, 3:5].partition_broadcast(P)).then_inc(bc_landed["p0", s], 16)
            for c in range(2):
                load_weight(sp, ("w_q0", s, c), ktiles(T["p_w_q"][0], c * 512, (c + 1) * 512))
            if s == 1:
                sp.wait_ge(h_ready.sem, h_ready.count(("p0", last)))
            else:
                sp.wait_ge(osq_ready.sem, osq_ready.count(1))
            sp.dma_start(m["keys"], T["keys"][0]).then_inc(bc_landed["keys0", s], 16)

        def mixer_act(act, s):
            A_, copy = nc.scalar.activation, nc.scalar.copy
            m = MEM[s]
            tiles = (2 * s, 2 * s + 1)
            for i, t in enumerate(tiles):
                free_bank(copy(m["vtok"][:, i, :], in_bank(act, ("vtok", t))), ("vtok", t))
            yield
            for q in tiles:
                for d in range(2):
                    free_bank(A_(m["gam"][:, d, :], in_bank(act, ("D", q, d)), ACT.Exp), ("D", q, d))
                yield
                yield
                for lv in LEVELS[1:]:
                    for d in range(2):
                        free_bank(copy(m["P1s"][:, d, :], in_bank(act, ("P1", q, d, lv))), ("P1", q, d, lv))
                    if lv == LEVELS[1]:
                        for d in range(2):
                            free_bank(copy(m["intraT"][:, d, :], in_bank(act, ("intraT", q, d))), ("intraT", q, d))
                    yield
                    yield
                for d in range(2):
                    free_bank(copy(m["vn"][:, d, :], in_bank(act, ("vnew", q, d))), ("vnew", q, d))
                yield
                yield
            act.wait_ge(s_ready.sem, s_ready.count((2 * s + 1, 1)))
            act.wait_ge(product.sem, product.count(("dS", 2 * s + 1, 1)))
            for i, t in enumerate(tiles):
                act_step(*[A_(m["osq"][:, i, h * P:(h + 1) * P], m["oacc"][:, i, h * P:(h + 1) * P],
                              ACT.Square, accum_out=ossq[:, 4 * t + h:4 * t + h + 1]) for h in range(HB)])
                osq_ready.mark(A_(orst[:, 4 * t:4 * t + 4], ossq[:, 4 * t:4 * t + 4], ACT.Sqrt, bias=eps_col,
                                  scale=1.0 / DK), t)
            yield
            for i, t in enumerate(tiles):
                free_bank(copy(m["yb"][:, :, tok(i)], heads(in_bank(act, ("ybT", t)))), ("ybT", t))
            yield
            for _ in range(4):
                yield
            for i, t in enumerate(tiles):
                norm_act(act, "p0", t, m["hx2"][:, i, :], (x_ready.sem, x_ready.count(("m0", tiles[1]))))
            yield
            for i, t in enumerate(tiles):
                norm_take(act, copy, "p0", t, 0, i, m["hT"])
            yield
            for j in range(5):
                if j < 4:
                    for h in (2 * j, 2 * j + 1):
                        free_bank(copy(m["qT"][:, h, :], in_bank(act, ("q0", s, h))[:, 0:256]), ("q0", s, h))
                if j:
                    t = tiles[0]
                    free_bank(copy(m["score"][:, 0, 2 * j - 2:2 * j, :],
                                   in_bank(act, ("s0", t, j - 1)).rearrange("p (h n) -> p h n", h=2)),
                              ("s0", t, j - 1))
                if s == 0 and j == 4:
                    gate_exp_act(act, 0)
                yield

        def mixer_dve(dve, s):
            V, step = nc.vector, dve_step
            m = MEM[s]
            tiles = (2 * s, 2 * s + 1)
            A, gam, intra, X, Y, Bm, R, tmp = (m[n] for n in ("A", "gam", "intra", "X", "Y", "Bm", "R", "tmp"))
            TT = V.tensor_tensor

            def scaled_masks(q):
                for d in range(2):
                    t = unit(q, d)
                    last = [V.tensor_scalar(m["lg"][:, d, h * P:(h + 1) * P], const(SUM_TO[d]),
                                            gdec[:, t, 4 * d + h:4 * d + h + 1], None, ALU.mult)
                            for h in range(HB)][-1]
                    lg_ready.mark(last, (q, d))

            def level(q, lv):
                for d in range(2):
                    bm_ready.mark(TT(heads(Bm[:, d, :]), heads(A[:, d, :]), over_heads(const(MASK[d][lv])), ALU.mult),
                                  (q, d, lv))

            for i, t in enumerate(tiles):
                free_bank(V.tensor_copy(m["ktok"][:, i, :], in_bank(dve, ("ktok", t))), ("ktok", t))
            scaled_masks(2 * s)
            yield
            for q in tiles:
                for d in range(2):
                    taken(dve, ("D", q, d))
                    free_bank(TT(A[:, d, :], in_bank(dve, ("KK", q, d)), gam[:, d, :], ALU.mult), ("KK", q, d))
                for d in range(2):
                    taken(dve, ("KK", q, d))
                    ai_ready.mark(TT(heads(A[:, d, :]), heads(A[:, d, :]),
                                     per_head(beta[:, unit(q, d), 4 * d:4 * d + 4]), ALU.mult), ("A", q, d))
                dve.wait_ge(ai_ready.sem, ai_ready.count(("A", q, 1)))
                step(*[TT(heads(Y[:, d, :]), heads(A[:, d, :]), over_heads(const(MASK[d][1])), ALU.mult)
                       for d in range(2)])
                level(q, LEVELS[1])
                yield
                for d in range(2):
                    free_bank(TT(heads(X[:, d, :]), heads(in_bank(dve, ("AT", q, d))),
                                 over_heads(const(MASK[1 - d][1])), ALU.mult), ("AT", q, d))
                for d in range(2):
                    taken(dve, ("AT", q, d))
                    for n, mat in (("X", X), ("Y", Y)):
                        xy_ready.mark(TT(heads(mat[:, d, :]), over_heads(const(IDENT)), heads(mat[:, d, :]),
                                         ALU.subtract), (n, q, d, 1))
                for d in range(2):
                    free_bank(TT(intra[:, d, :], in_bank(dve, ("QK", q, d)), gam[:, d, :], ALU.mult), ("QK", q, d))
                for d in range(2):
                    taken(dve, ("QK", q, d))
                    ai_ready.mark(TT(heads(intra[:, d, :]), heads(intra[:, d, :]), over_heads(const(INCL[d])),
                                     ALU.mult), ("I", q, d))
                yield
                for lv in LEVELS[1:]:
                    if lv == LEVELS[-1]:
                        for d in range(2):
                            free_bank(TT(heads(R[:, d, :]), heads(in_bank(dve, ("KS", q, d))),
                                         per_head(edec[:, d, unit(q, d), :]), ALU.mult), ("KS", q, d))
                        for i, t in enumerate(tiles):
                            taken(dve, ("vtok", t))
                        for d in range(2):
                            taken(dve, ("KS", q, d))
                        step(*[TT(R[:, d, :], m["vtok"][:, unit(q, d) - 2 * s, :], R[:, d, :], ALU.subtract)
                               for d in range(2)])
                        for d in range(2):
                            r_ready.mark(TT(heads(R[:, d, :]), heads(R[:, d, :]),
                                            per_head(beta[:, unit(q, d), 4 * d:4 * d + 4]), ALU.mult), (q, d))
                        for d in range(2):
                            free_bank(TT(heads(tmp[:, d, :]), heads(in_bank(dve, ("QS", q, d))),
                                         per_head(edec[:, d, unit(q, d), :]), ALU.mult), ("QS", q, d))
                    yield
                    for d in range(2):
                        for n, mat in (("X", X), ("Y", Y)):
                            if n == "Y" and lv == LEVELS[-1]:
                                continue
                            name = (n + "B" + n, q, d, lv)
                            dve.wait_ge(xy_ready.sem, xy_ready.count((n, q, d, lv // 2)))
                            free_bank(TT(mat[:, d, :], mat[:, d, :], in_bank(dve, name), ALU.subtract), name)
                            taken(dve, name)
                            dve.sem_inc(xy_ready.sem, 1)
                            xy_ready.done += 1
                    if lv != LEVELS[-1]:
                        level(q, 2 * lv)
                    else:
                        for d in range(2):
                            if d == 0:
                                for t in tiles:
                                    taken(dve, ("ktok", t))
                            kd_ready.mark(TT(heads(m["kdK"][:, d, :]), heads(m["ktok"][:, unit(q, d) - 2 * s, :]),
                                             per_head(erest[:, d, unit(q, d), :]), ALU.mult), (q, d))
                    yield
                yield
                for d in range(2):
                    t = unit(q, d)
                    o = m["oacc"][:, t - 2 * s, :]
                    taken(dve, ("QS", q, d))
                    bank = in_bank(dve, ("intraV", q, d))
                    if q % 2 == 0:
                        free_bank(TT(o, tmp[:, d, :], bank, ALU.add), ("intraV", q, d))
                    else:
                        free_bank(TT(tmp[:, d, :], tmp[:, d, :], bank, ALU.add), ("intraV", q, d))
                        taken(dve, ("intraV", q, d))
                        taken(dve, ("intraV", q - 1, 1 - d))
                        step(TT(o, o, tmp[:, d, :], ALU.add))
                    step(TT(heads(S[:, d, :]), heads(S[:, d, :]), per_head(eall[:, t, d, :]), ALU.mult))
                    free_bank(TT(S[:, d, :], S[:, d, :], in_bank(dve, ("dS", q, d)), ALU.add), ("dS", q, d))
                    taken(dve, ("dS", q, d))
                    dve.sem_inc(s_ready.sem, 1)
                    s_ready.done += 1
                if q == 2 * s:
                    scaled_masks(q + 1)
                yield
            for i, t in enumerate(tiles):
                o = m["oacc"][:, i, :]
                dve.wait_ge(osq_ready.sem, osq_ready.count(t))
                r4 = orst[:, 4 * t:4 * t + 4]
                step(V.reciprocal(r4, r4))
                step(TT(heads(o), heads(o), per_head(r4), ALU.mult))
                step(TT(heads(o), heads(o), over_heads(ogain), ALU.mult))
                taken(dve, ("z", t))
                yb_ready.mark(TT(o, o, m["z"][:, i, :], ALU.mult), t)
            yield
            yield
            dve.wait_ge(bc_landed["g0", s], 16)
            for t in tiles:
                for c in range(2):
                    residual_half(dve, "out0", "m0", t, c, m["gate"], m["rows"])
                    yield
            dve.wait_ge(bc_landed["p0", s], 16)
            for i, t in enumerate(tiles):
                norm_dve(dve, step, "p0", t, m["hx2"][:, i, :], m["modbc"][:, 1, :], m["modbc"][:, 0, :])
            yield
            for i, t in enumerate(tiles):
                norm_take(dve, V.tensor_copy, "p0", t, 1, i, m["hT"])
            yield
            for j in range(5):
                if j:
                    t = tiles[1]
                    free_bank(V.tensor_copy(m["score"][:, 1, 2 * j - 2:2 * j, :],
                                            in_bank(dve, ("s0", t, j - 1)).rearrange("p (h n) -> p h n", h=2)),
                              ("s0", t, j - 1))
                if s == 0 and j == 2:
                    taken(dve, ("s0", 0, 0))
                    first_rank_dve(0, 0)
                yield

        def mixer_pe(pe, s):
            M, TR = nc.tensor.matmul, nc.tensor.transpose
            m = MEM[s]
            tiles = (2 * s, 2 * s + 1)

            def by_head(name, lhsT, rhs, op=M):
                bank = out_bank(pe, name)
                for h in range(HB):
                    dst = bank[:, h * P:(h + 1) * P]
                    last = M(dst, lhsT(h), rhs(h), start=True, stop=True) if op is M else TR(dst, lhsT(h), rhs(h))
                product.mark(last, name)

            def of(n, d):
                return lambda h: m[n][:, d, h * P:(h + 1) * P]

            def qT_(q, d):
                return lambda h: m["qkv"][:, h, tok(unit(q, d) - 2 * s)]

            def kT_(q, d):
                return lambda h: m["qkv"][:, 4 + h, tok(unit(q, d) - 2 * s)]

            ident = lambda h: const(IDENT)
            for i, t in enumerate(tiles):
                for n, first in (("ktok", 4), ("vtok", 8)):
                    by_head((n, t), lambda h: m["qkv"][:, first + h, tok(i)], ident, TR)
            yield
            for q in tiles:
                for d in range(2):
                    pe.wait_ge(lg_ready.sem, lg_ready.count((q, d)))
                    by_head(("D", q, d), of("lg", d), lambda h: const(SUM_REST[d]))
                for d in range(2):
                    by_head(("KK", q, d), kT_(q, d), kT_(q, d))
                yield
                for d in range(2):
                    pe.wait_ge(ai_ready.sem, ai_ready.count(("A", q, d)))
                    by_head(("AT", q, d), of("A", d), ident, TR)
                for d in range(2):
                    by_head(("QK", q, d), qT_(q, d), kT_(q, d))
                yield
                for lv in LEVELS[1:]:
                    for d in range(2):
                        pe.wait_ge(bm_ready.sem, bm_ready.count((q, d, lv)))
                        pe.wait_ge(xy_ready.sem, xy_ready.count(("Y", q, d, lv // 2)))
                        by_head(("P1", q, d, lv), of("Bm", d), of("X", d))
                    if lv == LEVELS[1]:
                        for d in range(2):
                            pe.wait_ge(ai_ready.sem, ai_ready.count(("I", q, d)))
                            by_head(("intraT", q, d), of("intra", d), ident, TR)
                    if lv == LEVELS[-1]:
                        for d in range(2):
                            pe.wait_ge(s_ready.sem, s_ready.count((q - 1, d)) if q else 1)
                            by_head(("KS", q, d), kT_(q, d), of_state(d))
                        for d in range(2):
                            by_head(("QS", q, d), qT_(q, d), of_state(d))
                    yield
                    for d in range(2):
                        taken(pe, ("P1", q, d, lv))
                        by_head(("XBX", q, d, lv), of("Y", d), of("P1s", d))
                        if lv != LEVELS[-1]:
                            by_head(("YBY", q, d, lv), of("P1s", d), of("Y", d))
                    yield
                for d in range(2):
                    pe.wait_ge(r_ready.sem, r_ready.count((q, d)))
                    pe.wait_ge(xy_ready.sem, xy_ready.count(("X", q, d, LEVELS[-1])))
                    by_head(("vnew", q, d), of("X", d), of("R", d))
                yield
                for d in range(2):
                    taken(pe, ("vnew", q, d))
                    taken(pe, ("intraT", q, d))
                    by_head(("intraV", q, d), of("intraT", d), of("vn", d))
                for d in range(2):
                    pe.wait_ge(kd_ready.sem, kd_ready.count((q, d)))
                    by_head(("dS", q, d), of("kdK", d), of("vn", d))
                yield
            yield
            for i, t in enumerate(tiles):
                pe.wait_ge(yb_ready.sem, yb_ready.count(t))
                by_head(("ybT", t), lambda h: m["oacc"][:, i, h * P:(h + 1) * P], ident, TR)
            yield
            pe.wait_ge(ya_ready, 4)
            for i, t in enumerate(tiles):
                taken(pe, ("ybT", t))
                for c in range(2):
                    w = weights(pe, ("w_out0", s, c)).rearrange("p (k n) -> p k n", k=KT)
                    bank = out_bank(pe, ("out0", t, c))
                    for k in range(KT):
                        y = m["ya"][:, k, tok(i)] if k < 4 else m["yb"][:, k - 4, tok(i)]
                        last = M(bank, y, w[:, k, :], start=(k == 0), stop=(k == KT - 1))
                    product.mark(last, ("out0", t, c))
                    yield
            yield
            for i, t in enumerate(tiles):
                norm_pe(pe, "p0", t, m["hx2"][:, i, :])
            yield
            for t in tiles:
                for half in range(2):
                    taken(pe, ("ht", "p0", t, half))
            for j in range(5):
                if j < 4:
                    w = weights(pe, ("w_q0", s, j // 2)).rearrange("p (k n) -> p k n", k=KT)
                    for h in (2 * j, 2 * j + 1):
                        bank = out_bank(pe, ("q0", s, h))
                        for k in range(KT):
                            last = M(bank[:, 0:256], w[:, k, (h % 4) * P:(h % 4 + 1) * P], m["hT"][:, k, :],
                                     start=(k == 0), stop=(k == KT - 1))
                        product.mark(last, ("q0", s, h))
                if j:
                    pe.wait_ge(bc_landed["keys0", s], 16)
                    for i, t in enumerate(tiles):
                        bank = out_bank(pe, ("s0", t, j - 1))
                        for k in range(2):
                            h = 2 * j - 2 + k
                            taken(pe, ("q0", s, h))
                            last = M(bank[:, 256 * k:256 * k + 256], m["qT"][:, h, tok(i)], m["keys"][:, h, :],
                                     start=True, stop=True)
                        product.mark(last, ("s0", t, j - 1))
                yield

        def of_state(d):
            return lambda h: S[:, d, h * P:(h + 1) * P]

        def whole(stages):
            for _ in stages:
                pass

        def is_gain(n):
            return (MODS[n][1] // 2) % 3 == 1

        def quarters(row):
            return row.rearrange("(g n) -> g n", g=4)

        def load_mod_rows(pool, n):
            i, c = MODS[n]
            cols = slice((c % 2) * 512, (c % 2) * 512 + 512)
            for s in range(2):
                pool.dma_start(mod_row[n % 4][s:P:32], quarters(T["b_mod"][i, c // 2, cols])).then_inc(
                    row_landed[n % 4], 16)
                if is_gain(n):
                    pool.dma_start(norm_row[n % 4][s:P:32], quarters(T["norms"][i, c // 6, cols])).then_inc(
                        row_landed[n % 4], 16)

        def mod_pe(pe, n):
            w = weights(pe, ("mod",) + MODS[n]).rearrange("p (k g n) -> p k g n", k=KT, g=4)
            if n >= 2:
                pe.wait_ge(mod_taken, n - 1)
            for k in range(KT):
                for g in range(4):
                    last = nc.tensor.matmul(ps[32 * g:32 * g + 2, 6 + n % 2, 0:P], sT[:, 2 * k:2 * k + 2],
                                            w[:, k, g, :], start=(k == 0), stop=(k == KT - 1))
            last.then_inc(mod_done, 1)

        def mod_dve(dve, n):
            V = nc.vector
            dve.wait_ge(row_landed[n % 4], 32 * sum(1 + is_gain(m) for m in range(n % 4, n + 1, 4)))
            dve.wait_ge(mod_done, n + 1)
            rows = [(mod_row[n % 4][32 * g:32 * g + 2], 32 * g) for g in range(4)]
            last = [V.tensor_tensor(row, ps[at:at + 2, 6 + n % 2, 0:P], row, ALU.add) for row, at in rows][-1]
            last.then_inc(mod_taken, 1)
            dve.wait_ge(mod_taken, n + 1)
            if is_gain(n):
                dve_step(*[V.scalar_tensor_tensor(out=row, in0=row, scalar=1.0, in1=norm_row[n % 4][at:at + 2],
                                                  op0=ALU.add, op1=ALU.mult) for row, at in rows])
            dve.sem_inc(rows_ready, 1)

        def store_mod_rows(pool, n):
            i, c = MODS[n]
            for s in range(2):
                pool.dma_start(quarters(mods[i, s, c // 2, (c % 2) * 512:(c % 2) * 512 + 512]),
                               mod_row[n % 4][s:P:32]).then_inc(rows_stored[n % 2], 16)

        def with_mods(stages, part):
            rest = iter(range(MODS_FIRST + MODS_SECOND, len(MODS)))
            for i, _ in enumerate(stages):
                if i % 2 == 0:
                    for n in [n for n in [next(rest, None)] if n is not None]:
                        part(n)

        def first_block(block):
            @block.sync
            def _(sp):
                def load_mod(n):
                    i, c = MODS[n]
                    load_weight(sp, ("mod", i, c), ktiles(T["w_mod"][i], c * 512, (c + 1) * 512))

                sp.dma_start(sTin, T["c_cols"]).then_inc(c_landed, 16)
                load_mod(0)
                load_mod(1)
                sp.dma_start(x[:, 0:2, :], T["ctx"].rearrange("(t p) d -> p t d", p=P)).then_inc(x_landed, 16)
                load_mod(2)
                load_mod(3)
                sp.wait_ge(x_landed, 16)
                sp.dma_start(x[:, 2:4, :], T["x"].rearrange("(t p) d -> p t d", p=P)).then_inc(x_landed, 16)
                for n in range(4, MODS_FIRST):
                    load_mod(n)
                for c in range(7):
                    load_weight(sp, ("w_in", c), ktiles(T["ev_w_in"], c * 512, (c + 1) * 512))
                load_weight(sp, ("w_ab",), ktiles(T["ev_w_in"], 3584, 3600))
                for n in range(MODS_FIRST, len(MODS)):
                    load_mod(n)
                mixer_dma(sp, 0)

            @block.gpsimd
            def _(pool):
                nc.gpsimd.memset(eps_col, EPS).then_inc(eps_ready, 1)
                for n in range(4):
                    load_mod_rows(pool, n)
                pool.dma_start(consts[:, :], T["consts"]).then_inc(consts_landed, 16)
                pool.dma_start(iota16[:, :], T["iota16"]).then_inc(consts_landed, 16)
                pool.dma_start(conv_w[:, :, :], T["conv_w"]).then_inc(consts_landed, 16)
                pool.dma_start(alog, T["a_log"].partition_broadcast(P)).then_inc(consts_landed, 16)
                pool.dma_start(dtb, T["dt_bias"].partition_broadcast(P)).then_inc(consts_landed, 16)
                pool.dma_start(ogain, T["o_norm"].partition_broadcast(P)).then_inc(consts_landed, 16)
                for n in range(len(MODS)):
                    pool.wait_ge(rows_ready, n + 1)
                    store_mod_rows(pool, n)
                    if n:
                        wait_stored(pool, n - 1) if n > 1 else pool.wait_ge(rows_stored[0], 32)
                    if n and n + 3 < len(MODS):
                        load_mod_rows(pool, n + 3)
                wait_stored(pool, len(MODS) - 1)

            @block.scalar
            def _(act):
                A_, copy = nc.scalar.activation, nc.scalar.copy
                halves = lambda bank: bank.rearrange("p (s t) -> p s t", s=2)
                act.wait_ge(c_landed, 16)
                A_(sT, sTin, ACT.Silu).then_inc(silu_c, 1)
                act.wait_ge(eps_ready, 1)
                for t in range(NTOK):
                    if t == 2:
                        act.wait_ge(x_landed, 32)
                    first = (x_landed, 16) if t < 2 else (product.sem, product.count(("ht", "m0", t - 2, 1)))
                    norm_act(act, "m0", t, hbuf0[:, t % 2, :], first)
                    for row in range(2) if t == 1 else ():
                        wait_stored(act, 2 * row + 1)
                        for s in range(2):
                            act.dma_start(modbc0[s][:, row, :], mods[0, s, row].partition_broadcast(P)).then_inc(
                                bc_landed["m0", s], 16)
                    if t:
                        norm_take(act, copy, "m0", t - 1, 0, t - 1)
                norm_take(act, copy, "m0", 3, 0, 3)
                act.wait_ge(consts_landed, 6 * 16)
                for b in range(8):
                    free_bank(copy(bgcg[:, b, :], in_bank(act, ("proj", b))), ("proj", b))
                for b in range(4):
                    act.wait_ge(u_ready.sem, u_ready.count(("u", b)))
                    xa_conv.mark(A_(ya_block(b), halves(conv_in[:, b, :]), ACT.Copy, scale=conv_w[:, b, 1:2]),
                                 ("xa", b))
                for b in range(12):
                    bank = in_bank(act, ("proj", 12 + b))
                    centre_ready.mark(A_(qkv_block(b), halves(bank), ACT.Copy, scale=conv_w[:, 4 + b, 1:2]), b)
                    act.wait_ge(conv_ready.sem, conv_ready.count(("conv", b)))
                    silu_ready.mark(A_(qkv_block(b), qkv_block(b), ACT.Silu), ("silu", b))
                    if b == 0:
                        act.wait_ge(ya_ready, 4)
                    if b < 8:
                        act.wait_ge(silu_ready.sem, silu_ready.count(("silu", b)))
                        square_ready.mark(A_(halves(bgcg[:, b, :]), qkv_block(b), ACT.Square), ("sq", b))
                    if 3 <= b < 11:
                        free_bank(A_(bgcg[:, b - 3, :], in_bank(act, ("sumsq", b - 3)), ACT.Sqrt, bias=eps_col),
                                  ("sumsq", b - 3))
                for t in range(NTOK):
                    free_bank(A_(MEM[t // 2]["z"][:, t % 2, :], in_bank(act, ("z", t)), ACT.Silu), ("z", t))
                act.wait_ge(sp_dve, 1)
                A_(beta, ab[:, :, 8:16], ACT.Sigmoid).then_inc(sp_act, 1)
                A_(g2, g2, ACT.Exp).then_inc(sp_act, 1)
                A_(nexpa, alog, ACT.Exp).then_inc(sp_act, 1)
                act.wait_ge(sp_act, 3)
                A_(g2, g2, ACT.Ln, bias=1.0).then_inc(sp_act, 1)
                free_bank(A_(expo, in_bank(act, ("cum",))[:, 0:96], ACT.Exp), ("cum",))
                taken(act, ("cum",))
                act.sem_inc(sp_act, 1)
                whole(mixer_act(act, 0))

            @block.vector
            def _(dve):
                V, step = nc.vector, dve_step
                halves = lambda bank: bank.rearrange("p (s t) -> p s t", s=2)
                for n in range(MODS_FIRST):
                    mod_dve(dve, n)
                for t in range(NTOK):
                    if t % 2 == 0:
                        dve.wait_ge(bc_landed["m0", t // 2], 32)
                    bc = modbc0[t // 2]
                    norm_dve(dve, step, "m0", t, hbuf0[:, t % 2, :], bc[:, 1, :], bc[:, 0, :])
                    if t:
                        norm_take(dve, V.tensor_copy, "m0", t - 1, 1, t - 1)
                norm_take(dve, V.tensor_copy, "m0", 3, 1, 3)

                def other_taps(a3, u3, w):
                    step(V.scalar_tensor_tensor(out=a3[:, :, 1:256], in0=u3[:, :, 0:255], scalar=w[:, 0:1],
                                                in1=a3[:, :, 1:256], op0=ALU.mult, op1=ALU.add))
                    return V.scalar_tensor_tensor(out=a3[:, :, 0:255], in0=u3[:, :, 1:256], scalar=w[:, 2:3],
                                                  in1=a3[:, :, 0:255], op0=ALU.mult, op1=ALU.add)

                dve.wait_ge(consts_landed, 6 * 16)
                for b in range(4):
                    bank = in_bank(dve, ("proj", 8 + b))
                    taken(dve, ("proj", 4 + b))
                    free_bank(V.tensor_tensor(conv_in[:, b, :], bank, bgcg[:, 4 + b, :], ALU.mult), ("proj", 8 + b))
                    taken(dve, ("proj", 8 + b))
                    dve.sem_inc(u_ready.sem, 1)
                    u_ready.done += 1
                    dve.wait_ge(xa_conv.sem, xa_conv.count(("xa", b)))
                    step(other_taps(ya_block(b), halves(conv_in[:, b, :]), conv_w[:, b, :]))
                    taken(dve, ("proj", b))
                    last = V.tensor_tensor(ya_block(b), ya_block(b), halves(bgcg[:, b, :]), ALU.mult)
                    last.then_inc(ya_ready, 1)

                def over_length(b):
                    r = bgcg[:, b, :]
                    taken(dve, ("sumsq", b))
                    step(V.reciprocal(r, r))
                    step(V.scalar_tensor_tensor(out=qkv_block(b), in0=qkv_block(b),
                                                scalar=float(DK) ** -0.5 if b < 4 else 1.0, in1=halves(r),
                                                op0=ALU.mult, op1=ALU.mult))
                    dve.sem_inc(qk_ready, 1)

                for b in range(12):
                    bank = in_bank(dve, ("proj", 12 + b))
                    dve.wait_ge(centre_ready.sem, centre_ready.count(b))
                    free_bank(other_taps(qkv_block(b), halves(bank), conv_w[:, 4 + b, :]), ("proj", 12 + b))
                    taken(dve, ("proj", 12 + b))
                    dve.sem_inc(conv_ready.sem, 1)
                    conv_ready.done += 1
                    if b >= 4:
                        over_length(b - 4)
                free_bank(V.tensor_copy(small[:, 16:80], in_bank(dve, ("ab",))[:, 0:64]), ("ab",))
                taken(dve, ("ab",))
                step(V.tensor_tensor(g1, ab[:, :, 0:8], dtb.unsqueeze(1).broadcast_to((P, NTOK, 8)), ALU.add))
                step(V.scalar_tensor_tensor(out=g2, in0=g1, scalar=-1.0, in1=g1, op0=ALU.mult, op1=ALU.min))
                dve.sem_inc(sp_dve, 1)
                step(V.tensor_scalar(g1, g1, 0.0, None, ALU.max))
                dve.wait_ge(sp_act, 4)
                step(V.tensor_tensor(g1, g1, g2, ALU.add))
                step(V.scalar_tensor_tensor(out=gdec, in0=g1, scalar=-1.0,
                                            in1=nexpa.unsqueeze(1).broadcast_to((P, NTOK, 8)),
                                            op0=ALU.mult, op1=ALU.mult))
                dve.sem_inc(sp_dve, 1)
                for n in range(MODS_FIRST, MODS_FIRST + MODS_SECOND):
                    mod_dve(dve, n)
                dve.sem_inc(slot_free, RING)
                dve.sem_inc(peer_taken, 1)
                dve.wait_ge(sp_act, 5)
                step(V.memset(S[:, :, :], 0.0))
                dve.sem_inc(s_ready.sem, 1)
                s_ready.done += 1
                with_mods(mixer_dve(dve, 0), lambda n: mod_dve(dve, n))

            @block.tensor
            def _(pe):
                M = nc.tensor.matmul

                def accumulate(dst, pairs):
                    for i, (l, r) in enumerate(pairs):
                        last = M(dst, l, r, start=(i == 0), stop=(i == len(pairs) - 1))
                    return last

                pe.wait_ge(silu_c, 1)
                for n in range(MODS_FIRST):
                    mod_pe(pe, n)
                pe.wait_ge(consts_landed, 6 * 16)
                for t in range(NTOK):
                    norm_pe(pe, "m0", t, hbuf0[:, t % 2, :])
                for t in range(NTOK):
                    for half in range(2):
                        taken(pe, ("ht", "m0", t, half))
                for b in range(24):
                    w = weights(pe, ("w_in", b // 4)).rearrange("p (k n) -> p k n", k=KT)
                    c = (b % 4) * P
                    bank = out_bank(pe, ("proj", b))
                    product.mark(accumulate(bank, [(w[:, k, c:c + P], hT[:, k, :]) for k in range(KT)]), ("proj", b))
                    if 14 <= b < 22:
                        pe.wait_ge(square_ready.sem, square_ready.count(("sq", b - 14)))
                        bank = out_bank(pe, ("sumsq", b - 14))
                        product.mark(M(bank, const(ONES), bgcg[:, b - 14, :], start=True, stop=True),
                                     ("sumsq", b - 14))
                w = weights(pe, ("w_in", 6)).rearrange("p (k n) -> p k n", k=KT)
                for t in range(NTOK):
                    bank = out_bank(pe, ("z", t))
                    product.mark(accumulate(bank, [(hT[:, k, tok(t)], w[:, k, :]) for k in range(KT)]), ("z", t))
                w = weights(pe, ("w_ab",))[:, 0:16 * KT].rearrange("p (k n) -> p k n", k=KT)
                bank = out_bank(pe, ("ab",))
                for t in range(NTOK):
                    last = accumulate(bank[:, 16 * t:16 * t + 16], [(hT[:, k, tok(t)], w[:, k, :]) for k in range(KT)])
                product.mark(last, ("ab",))
                for n in range(MODS_FIRST, MODS_FIRST + MODS_SECOND):
                    mod_pe(pe, n)
                pe.wait_ge(sp_dve, 2)
                bank = out_bank(pe, ("cum",))
                for j, masks in enumerate((SUM_TO, SUM_REST)):
                    for d in range(2):
                        at = 32 * j + 16 * d
                        M(bank[:, at:at + 16].rearrange("p (t h) -> p t h", t=NTOK), const(masks[d]),
                          gdec[:, :, 4 * d:4 * d + 4], start=True, stop=True)
                product.mark(M(bank[:, 64:96], const(ONES), small[:, 152:184], start=True, stop=True), ("cum",))
                pe.wait_ge(qk_ready, 8)
                pe.wait_ge(silu_ready.sem, 12)
                with_mods(mixer_pe(pe, 0), lambda n: mod_pe(pe, n))

        GROUPS_OF_HEAD = TOPK // GRP

        def sums_pool(pool, G, par, k, table):
            pool.wait_ge(slot_free, G * TOPK + k + 1)
            pool_step.wait_apart()
            nc.gpsimd.indirect_dma_start(
                ring[:, k % RING, :], None, table,
                bass.IndirectOffsetOnAxis(ap=expert_cur[:, par, k:k + 1], axis=0),
            ).then_inc(slot_landed[k % RING], 16)

        def sums_act(act, G, par, j):
            g = slice(j * GRP, (j + 1) * GRP)
            act.wait_ge(dots_ready, G * GROUPS_OF_HEAD + j + 1)
            act_step(nc.scalar.activation(acts[:, par, g], dots[:, par, g], ACT.Gelu))
            act_step(*[nc.scalar.activation(coef[:, par, k:k + 1], acts[:, par, k:k + 1], ACT.Copy,
                                            scale=gate_cur[:, par, k:k + 1])
                       for k in range(j * GRP, (j + 1) * GRP)])
            for k in range(j * GRP, (j + 1) * GRP):
                nc.scalar.activation(diag[:, k % RING, :], const(IDENT), ACT.Copy,
                                     scale=coef[:, par, k:k + 1]).then_inc(diag_ready, 1)

        def gate_exp_act(act, G):
            act.wait_ge(gmax_ready, G + 1)
            nc.scalar.activation(gate_exp[:, :], best[:, :], ACT.Exp, bias=gate_stat[:, 0:1],
                                 accum_out=gate_stat[:, 1:2]).then_inc(gexp_ready, 1)

        def head_act(act, G, par, rank_next, between=lambda: None):
            act.wait_ge(ranked, G + 1)
            for j in range(GROUPS_OF_HEAD):
                if j in STAGE_AT:
                    between()
                sums_act(act, G, par, j)
                if j == 2 and rank_next:
                    gate_exp_act(act, G + 1)

        def tile_sum_act(act, T_, place):
            act.wait_ge(slot_free, (T_ + 1) * SLOTS + RING)
            nc.scalar.copy(arena[:, place].rearrange("p (a b) -> p a b", a=2), ps[:, 6:8, :]).then_inc(peer_taken, 1)

        def tile_open_pe(pe, T_):
            pe.wait_ge(peer_taken, T_ + 1)
            for c in range(2):
                nc.tensor.matmul(ps[:, 6 + c, :], const(ZERO), consts[:, 0:512], start=True, stop=True)

        def head_pe(pe, G, between=lambda: None):
            for k in range(TOPK):
                if k % GRP == 0 and k // GRP in STAGE_AT:
                    between()
                pe.wait_ge(diag_ready, G * TOPK + k + 1)
                for c in range(2):
                    last = nc.tensor.matmul(ps[:, 6 + c, :], diag[:, k % RING, :],
                                            ring[:, k % RING, D + 512 * c:D + 512 * c + 512],
                                            start=False, stop=True, skip_group_check=True)
                last.then_inc(slot_free, 1)

        def square(mat):
            return mat[:, :].rearrange("p (a b) -> p a b", a=TOPK)

        def rank_dve(G, n, par):
            V, step = nc.vector, dve_step
            step(V.tensor_copy(score_cur[:, :], arena[:, bass.ds(n * 256 + 16384, 256)]), apart=True)
            yield
            both = [(p, score_cur[:, p * NKEY:(p + 1) * NKEY], score_left[:, p * NKEY:(p + 1) * NKEY])
                    for p in range(2)]
            step(*[V.max(top_val[:, p, 0:8], cur) for p, cur, _ in both], apart=True)
            yield
            step(*[V.max_index(top_idx[:, p, 0:8], top_val[:, p, 0:8], cur) for p, cur, _ in both],
                 *[V.match_replace(left, top_val[:, p, 0:8], cur, -3e38) for p, cur, left in both], apart=True)
            yield
            step(*[V.max(top_val[:, p, 8:16], left) for p, _, left in both], apart=True)
            yield
            step(*[V.max_index(top_idx[:, p, 8:16], top_val[:, p, 8:16], left) for p, _, left in both],
                 V.tensor_tensor(square(cand), top_val[:, 0, :].unsqueeze(2).broadcast_to((P, TOPK, TOPK)),
                                 top_val[:, 1, :].unsqueeze(1).broadcast_to((P, TOPK, TOPK)), ALU.add))
            yield
            step(V.tensor_copy(top_idx_f[:, :, :], top_idx[:, :, :]), V.max(best[:, 0:8], cand[:, :]), apart=True)
            yield
            step(V.max_index(best_pos[:, 0:8], best[:, 0:8], cand[:, :]),
                 V.match_replace(cand_left[:, :], best[:, 0:8], cand[:, :], -3e38),
                 V.tensor_scalar(gate_stat[:, 0:1], best[:, 0:1], -1.0, None, ALU.mult), apart=True)
            yield
            step(V.max(best[:, 8:16], cand_left[:, :]), apart=True)
            dve_step.eng.sem_inc(gmax_ready, 1)
            yield
            step(V.max_index(best_pos[:, 8:16], best[:, 8:16], cand_left[:, :]))
            yield
            step(V.tensor_scalar(pos_ab[:, 0, :], best_pos[:, :], 4, None, ALU.logical_shift_right),
                 V.tensor_scalar(pos_ab[:, 1, :], best_pos[:, :], 15, None, ALU.bitwise_and))
            yield
            step(V.tensor_copy(pos_ab_f[:, :, :], pos_ab[:, :, :]))
            yield
            hot = (onehot, cand)
            step(*[V.tensor_tensor(square(hot[i]), iota16[:, :].unsqueeze(1).broadcast_to((P, TOPK, TOPK)),
                                   pos_ab_f[:, i, :].unsqueeze(2).broadcast_to((P, TOPK, TOPK)), ALU.is_equal)
                   for i in range(2)])
            yield
            step(*[V.tensor_tensor(square(hot[i]), square(hot[i]),
                                   top_idx_f[:, i, :].unsqueeze(1).broadcast_to((P, TOPK, TOPK)), ALU.mult)
                   for i in range(2)])
            yield
            step(*[V.tensor_reduce(sel_ab[:, i, :], square(hot[i]), AX, ALU.add) for i in range(2)])
            yield
            dve_step.eng.wait_ge(gexp_ready, G + 1)
            step(V.scalar_tensor_tensor(out=expert_cur[:, par, :], in0=sel_ab[:, 0, :],
                                        scalar=float(NKEY), in1=sel_ab[:, 1, :], op0=ALU.mult, op1=ALU.add),
                 V.reciprocal(gate_stat[:, 2:3], gate_stat[:, 1:2]))
            yield
            step(V.tensor_scalar(gate_cur[:, par, :], gate_exp[:, :], gate_stat[:, 2:3], None, ALU.mult))
            dve_step.eng.sem_inc(ranked, 1)
            yield

        RANK = 31
        RANK_SLOTS = range(1, 9)
        STAGE_AT = (0, 4, 6)

        def tile_start_dve(T_, place):
            if not (isinstance(T_, int) and T_ == 0):
                dve_step.eng.wait_ge(dots_ready, T_ * (PH * GROUPS_OF_HEAD))
            dve_step(nc.vector.tensor_copy(hx_cur[:, :], arena[:, place]))

        def head_dve(dve, G, n, par, rank_next, between=lambda: None):
            rank = rank_dve(G + 1, n + 1, 1 - par)
            for k in range(TOPK):
                slot = k % RING
                dve.wait_ge(slot_landed[slot], (G * (TOPK // RING) + k // RING + 1) * 16)
                ins = nc.vector.tensor_tensor_reduce(
                    out=ring[:, slot, 0:D], in0=ring[:, slot, 0:D], in1=hx_cur[:, :], scale=1.0, scalar=0.0,
                    op0=ALU.mult, op1=ALU.add, accum_out=dots[:, par, k:k + 1])
                if k % GRP == GRP - 1:
                    ins.then_inc(dots_ready, 1)
                    if k // GRP in STAGE_AT:
                        between()
                if rank_next and k in RANK_SLOTS:
                    next(rank)
                    next(rank)

        def tile_place(i):
            return bass.ds(i * D + 24576, D)

        def loop_act(act, tiles, T0, G0, last):
            n = len(tiles)
            start = act_step.base + act_step.n
            per_pair = 2 * GROUPS_OF_HEAD * (1 + GRP)

            def pair(i, hp, follows):
                act_step.start(start + (i * 4 + hp) * per_pair)
                for par in range(2):
                    head_act(act, G0 + i * PH + hp * 2 + par, par, follows or par == 0)
                assert act_step.n == per_pair

            with act.Fori(0, n - 1) as i:
                with act.Fori(0, 4) as hp:
                    pair(i, hp, True)
                tile_sum_act(act, i + T0, tile_place(i + tiles[0]))
            with act.Fori(0, 3) as hp:
                pair(n - 1, hp, True)
            pair(n - 1, 3, not last)
            tile_sum_act(act, n - 1 + T0, tile_place(n - 1 + tiles[0]))

        def loop_pe(pe, tiles, T0, G0):
            with pe.Fori(0, len(tiles)) as i:
                tile_open_pe(pe, i + T0)
                with pe.Fori(0, PH) as h:
                    head_pe(pe, G0 + i * PH + h)

        def loop_pool(pool, tiles, G0, table):
            with pool.Fori(0, len(tiles)) as i:
                with pool.Fori(0, 4) as hp:
                    for par in range(2):
                        G = G0 + i * PH + hp * 2 + par
                        pool.wait_ge(ranked, G + 1)
                        for k in range(TOPK):
                            sums_pool(pool, G, par, k, table)

        def loop_dve(dve, tiles, G0, n0, before_last_tile, before_last_pair):
            n = len(tiles)
            T0 = G0 // PH
            start = dve_step.base + dve_step.n
            per_tile = 1 + PH * RANK

            def pair(i, hp, follows):
                dve_step.start(start + i * per_tile + 1 + hp * (2 * RANK))
                for par in range(2):
                    h = i * PH + hp * 2 + par
                    head_dve(dve, G0 + h, n0 + h, par, follows or par == 0)
                assert dve_step.n == (2 * RANK if follows else RANK), dve_step.n

            with dve.Fori(0, n - 1) as i:
                dve_step.start(start + i * per_tile)
                tile_start_dve(i + T0, tile_place(i + tiles[0]))
                with dve.Fori(0, 4) as hp:
                    pair(i, hp, True)
            before_last_tile()
            dve_step.start(start + (n - 1) * per_tile)
            tile_start_dve(n - 1 + T0, tile_place(n - 1 + tiles[0]))
            with dve.Fori(0, 3) as hp:
                pair(n - 1, hp, True)
            before_last_pair()
            pair(n - 1, 3, False)

        def first_rank_dve(G, n):
            for _ in rank_dve(G, n, 0):
                pass

        def peer_gate_dma(sp, layer):
            for s in range(2):
                sp.dma_start(peer_gate[:, s, :], mods[layer, s, 5].partition_broadcast(P)).then_inc(
                    bc_landed[f"pg{layer}",], 16)

        def peer_residual_dve(dve, layer, t):
            i = t if layer == 0 else t - 2
            dve.wait_ge(bc_landed[f"pg{layer}",], 32)
            dve.wait_ge(peer_taken, NTOK * layer + i + 2)
            gated.mark(nc.vector.tensor_tensor(hx2[:, i, :], hx2[:, i, :], peer_gate[:, t // 2, :], ALU.mult),
                       (layer, t))
            dve.wait_ge(gated.sem, gated.count((layer, t)))
            x_ready.mark(nc.vector.tensor_tensor(x[:, t, :], x[:, t, :], hx2[:, i, :], ALU.add), (f"p{layer}", t))

        def sums_and_mixer(block):
            table = T["experts0"]
            HEADS = 2 * PH

            def weave(stages):
                return lambda: next(stages, None)

            @block.sync
            def _(sp):
                mixer_dma(sp, 1)
                sp.wait_ge(product.sem, product.count(("s0", 3, 3)))
                peer_gate_dma(sp, 0)
                load_weight(sp, ("w_kv1",), ktiles(T["od_w_in"], QL, QL + KVL + ROPE))
                load_weight(sp, ("w_q_1",), ktiles(T["od_w_in"], 0, QL))
                sp.wait_ge(ranked, 2 * PH)
                for s in range(2):
                    sp.dma_start(modbc1[s], mods[1, s, 0:2].partition_broadcast(P)).then_inc(bc_landed["m1", s], 16)

            @block.gpsimd
            def _(pool):
                for G in range(HEADS):
                    pool.wait_ge(ranked, G + 1)
                    for k in range(TOPK):
                        sums_pool(pool, G, G % 2, k, table)
                loop_pool(pool, (2, 3), HEADS, table)

            @block.scalar
            def _(act):
                between = weave(mixer_act(act, 1))
                for G in range(HEADS):
                    head_act(act, G, G % 2, True, between)
                    if G % PH == PH - 1:
                        tile_sum_act(act, G // PH, tile_place(G // PH))
                loop_act(act, (2, 3), 2, HEADS, True)

            @block.tensor
            def _(pe):
                between = weave(mixer_pe(pe, 1))
                for G in range(HEADS):
                    if G % PH == 0:
                        tile_open_pe(pe, G // PH)
                    head_pe(pe, G, between)
                loop_pe(pe, (2, 3), 2, HEADS)

            @block.vector
            def _(dve):
                between = weave(mixer_dve(dve, 1))
                for G in range(HEADS):
                    if G % PH == 0:
                        tile_start_dve(G // PH, tile_place(G // PH))
                    head_dve(dve, G, G, G % 2, True, between)
                loop_dve(dve, (2, 3), HEADS, HEADS, lambda: [peer_residual_dve(dve, 0, t) for t in (0, 1)],
                         lambda: peer_residual_dve(dve, 0, 2))
                peer_residual_dve(dve, 0, 3)

        def last_sums(block):
            tiles, G0, T0 = (2, 3), 4 * PH, 4

            @block.gpsimd
            def _(pool):
                loop_pool(pool, (0, 1), G0, T["experts1"])

            @block.scalar
            def _(act):
                loop_act(act, (0, 1), T0, G0, True)
                for i, t in enumerate(tiles):
                    norm_act(act, "f", t, hfin[:, i, :], (x_ready.sem, x_ready.count(("p1", t))))

            @block.tensor
            def _(pe):
                loop_pe(pe, (0, 1), T0, G0)

            @block.vector
            def _(dve):
                loop_dve(dve, (0, 1), G0, 0, lambda: None, lambda: peer_residual_dve(dve, 1, 2))
                peer_residual_dve(dve, 1, 3)
                dve.wait_ge(bc_landed["nf",], 16)
                for i, t in enumerate(tiles):
                    norm_dve(dve, dve_step, "f", t, hfin[:, i, :], gain_f, None)

            @block.sync
            def _(sp):
                peer_gate_dma(sp, 1)
                sp.dma_start(gain_f, T["norm_f"].partition_broadcast(P)).then_inc(bc_landed["nf",], 16)
                for i, t in enumerate(tiles):
                    sp.wait_ge(h_ready.sem, h_ready.count(("f", t)))
                    sp.dma_start(out[tok(i), :], hfin[:, i, :]).then_inc(stored, 16)
                sp.wait_ge(stored, 32)

        def second_block(block):
            SC = float(NOPE + ROPE) ** -0.5

            @block.sync
            def _(sp):
                load_weight(sp, ("w_uq_n",), ktiles(T["uq_nope"], 0, HC * NOPE))
                load_weight(sp, ("w_uq_r",), ktiles(T["uq_rope"], 0, HC * ROPE))
                load_weight(sp, ("w_ukv",), ktiles(T["ukv"], 0, HC * (NOPE + VD)))
                for c in range(2):
                    load_weight(sp, ("w_out1", c), ktiles(T["od_w_out"], c * 512, (c + 1) * 512))
                for c in range(2):
                    load_weight(sp, ("w_q1", c), ktiles(T["p_w_q"][1], c * 512, (c + 1) * 512))

            @block.gpsimd
            def _(pool):
                pool.dma_start(lat_gain[:, 0:QL], T["q_norm"].partition_broadcast(P)).then_inc(bc_landed["lat",], 16)
                pool.dma_start(lat_gain[:, QL:QL + KVL], T["kv_norm"].partition_broadcast(P)).then_inc(bc_landed["lat",], 16)
                pool.dma_start(rope_cs, T["rope"]).then_inc(bc_landed["lat",], 16)
                pool.wait_ge(h_ready.sem, h_ready.count(("m1", 3)))
                pool.dma_start(gate1, mods[1, 1, 2].partition_broadcast(P)).then_inc(bc_landed["g1",], 16)
                pool.dma_start(keysB[:, :, :], T["keys"][1]).then_inc(bc_landed["keys1",], 16)
                pool.wait_ge(product.sem, product.count(("cqT", 3)))
                pool.dma_start(modbcp, mods[1, 1, 3:5].partition_broadcast(P)).then_inc(bc_landed["p1",], 16)

            @block.scalar
            def _(act):
                A_ = nc.scalar.activation
                for t in range(NTOK):
                    first = ((x_ready.sem, x_ready.count(("p0", 3))) if t < 2
                             else (product.sem, product.count(("ht", "m1", t - 2, 1))))
                    norm_act(act, "m1", t, hbuf1[:, t % 2, :], first)
                    if t:
                        norm_take(act, nc.scalar.copy, "m1", t - 1, 0, t - 1)
                norm_take(act, nc.scalar.copy, "m1", 3, 0, 3)
                junk = area(20480, QL)
                for t in range(NTOK):
                    for name, lo, n, i in (("lkv", QL, KVL, 0), ("lq", 0, QL, 1)):
                        if name == "lq" and t < 2:
                            continue
                        bank = in_bank(act, (name, t))
                        col = slice(2 * t + i, 2 * t + i + 1)
                        act_step(A_(junk[:, 0:n], bank[:, 0:n], ACT.Square, accum_out=lssq[:, col]))
                        act_step(A_(lrst[:, col], lssq[:, col], ACT.Sqrt, bias=eps_col, scale=1.0 / n))
                        width = KVL + ROPE if name == "lkv" else QL
                        free_bank(nc.scalar.copy(lat[:, t, lo:lo + width], bank[:, 0:width]), (name, t))
                        taken(act, (name, t))
                    act.sem_inc(lsq_ready, 1)
                for t in range(NTOK):
                    bank = in_bank(act, ("ckvT", t))
                    act_step(nc.scalar.copy(krT[0:ROPE, tok(t)], bank[0:ROPE, 256:384]))
                    free_bank(nc.scalar.copy(ckvT[:, :, tok(t)], bank[:, 0:256].rearrange("p (k t) -> p k t", k=2)),
                              ("ckvT", t))
                    if t >= 2:
                        bank = in_bank(act, ("cqT", t))
                        free_bank(nc.scalar.copy(cqT[:, :, tok(t - 2)], bank[:, 0:384].rearrange("p (k t) -> p k t", k=3)),
                                  ("cqT", t))
                for h in range(HC):
                    free_bank(nc.scalar.copy(qnT[:, h, :], in_bank(act, ("qn", h))[:, 0:256]), ("qn", h))
                for t in (2, 3):
                    for g in range(2):
                        bank = in_bank(act, ("qrT", t, g))
                        free_bank(nc.scalar.copy(qrT[0:ROPE, 4 * g:4 * g + 4, tok(t - 2)],
                                                 bank[0:ROPE, :].rearrange("p (h t) -> p h t", h=4)), ("qrT", t, g))
                for h in range(HC):
                    if h % 2 == 0:
                        free_bank(nc.scalar.copy(knT[:, h, :], in_bank(act, ("kn", h))), ("kn", h))
                for t in range(NTOK):
                    free_bank(nc.scalar.copy(vatt[:, t, 0:512], in_bank(act, ("v", t, 0))), ("v", t, 0))

                def turn_probs(u):
                    free_bank(nc.scalar.copy(probT[:, u % 2, :], in_bank(act, ("pT", u))), ("pT", u))

                for u in range(UNITS):
                    bank = in_bank(act, ("sc", u))
                    act.wait_ge(nmax_ready.sem, nmax_ready.count(u))
                    if u >= 3:
                        act.wait_ge(product.sem, product.count(("pT", u - 3)))
                    free_bank(A_(prob[:, u % 3, :], bank, ACT.Exp, bias=nsmax[:, u:u + 1], scale=SC,
                                 accum_out=ssum[:, u:u + 1]), ("sc", u))
                    if u >= 2:
                        turn_probs(u - 2)
                turn_probs(UNITS - 2)
                turn_probs(UNITS - 1)
                for i, t in enumerate((2, 3)):
                    norm_act(act, "p1", t, hx2[:, i, :], (x_ready.sem, x_ready.count(("m1", t))))
                    if i:
                        norm_take(act, nc.scalar.copy, "p1", t - 1, 0, i - 1)
                norm_take(act, nc.scalar.copy, "p1", 3, 0, 1)
                for h in range(PH):
                    free_bank(nc.scalar.copy(qT[:, h, 0:256], in_bank(act, ("q1", h))[:, 0:256]), ("q1", h))
                gate_exp_act(act, 4 * PH)

            @block.vector
            def _(dve):
                V = nc.vector
                step = dve_step

                def rope(dst, src, t, nh, last_read):
                    s4, d4 = (v.rearrange("p (h a b n) -> p h a b n", h=nh, a=2, b=2) for v in (src, dst))
                    cs = [rope_cs[:, t, i].unsqueeze(1).broadcast_to((P, nh, 2, 16)) for i in range(2)]
                    tmps = [rtmp[:, i, 0:nh * 32].rearrange("p (h a n) -> p h a n", h=nh, a=2) for i in range(4)]
                    parts = [(0, 0), (1, 1), (1, 0), (0, 1)]
                    ins = [V.tensor_tensor(tmps[i], s4[:, :, :, b, :], cs[c], ALU.mult)
                           for i, (b, c) in enumerate(parts)]
                    if last_read is None:
                        step(*ins)
                    else:
                        free_bank(ins[-1], last_read)
                        step(*ins[:-1])
                        taken(dve, last_read)
                    return (V.tensor_tensor(d4[:, :, :, 0, :], tmps[0], tmps[1], ALU.subtract),
                            V.tensor_tensor(d4[:, :, :, 1, :], tmps[2], tmps[3], ALU.add))

                for t in range(NTOK):
                    if t % 2 == 0:
                        dve.wait_ge(bc_landed["m1", t // 2], 16)
                    bc = modbc1[t // 2]
                    norm_dve(dve, step, "m1", t, hbuf1[:, t % 2, :], bc[:, 1, :], bc[:, 0, :])
                    if t:
                        norm_take(dve, V.tensor_copy, "m1", t - 1, 1, t - 1)
                norm_take(dve, V.tensor_copy, "m1", 3, 1, 3)
                dve.wait_ge(bc_landed["lat",], 48)
                for t in range(NTOK):
                    dve.wait_ge(lsq_ready, t + 1)
                    for i, lo, n in ((0, QL, KVL), (1, 0, QL)):
                        if i and t < 2:
                            continue
                        r = lrst[:, 2 * t + i:2 * t + i + 1]
                        step(V.reciprocal(r, r))
                        step(V.scalar_tensor_tensor(out=lat[:, t, lo:lo + n], in0=lat[:, t, lo:lo + n], scalar=r,
                                                    in1=lat_gain[:, lo:lo + n], op0=ALU.mult, op1=ALU.mult))
                    if t >= 2:
                        kr = lat[:, t, QL + KVL:QL + KVL + ROPE]
                        step(*rope(kr, kr, t - 2, 1, None))
                    dve.sem_inc(lat_ready.sem, 1)
                for t in (2, 3):
                    step(*rope(qrope[:, t - 2, :], in_bank(dve, ("qr", t)), t - 2, HC, ("qr", t)))
                    dve.sem_inc(qr_ready.sem, 1)
                for h in range(HC):
                    if h % 2:
                        free_bank(V.tensor_copy(knT[:, h, :], in_bank(dve, ("kn", h))), ("kn", h))
                for t in range(NTOK):
                    free_bank(V.tensor_copy(vatt[:, t, 512:1024], in_bank(dve, ("v", t, 1))), ("v", t, 1))

                def take_o(u):
                    free_bank(V.tensor_copy(oT[:, u // 2, tok(u % 2)], in_bank(dve, ("oT", u))[:, 0:P]), ("oT", u))

                for u in range(UNITS + 3):
                    if u < UNITS:
                        c = slice(u, u + 1)
                        step(V.tensor_reduce(smax[:, c], in_bank(dve, ("sc", u)), AX, ALU.max))
                        nmax_ready.mark(V.tensor_scalar(nsmax[:, c], smax[:, c], -SC, None, ALU.mult), u)
                    if 1 <= u <= UNITS:
                        v = u - 1
                        c = slice(v, v + 1)
                        taken(dve, ("sc", v))
                        step(V.reciprocal(srec[:, c], ssum[:, c]))
                        prob_ready.mark(V.tensor_scalar(prob[:, v % 3, :], prob[:, v % 3, :], srec[:, c], None,
                                                        ALU.mult), v)
                    if u >= 3:
                        take_o(u - 3)
                dve.wait_ge(bc_landed["g1",], 16)
                for t in (2, 3):
                    for c in range(2):
                        residual_half(dve, "out1", "m1", t, c, gate1, rtmp.rearrange("p (a b) n -> p a (b n)", a=2))
                dve.wait_ge(bc_landed["p1",], 16)
                for i, t in enumerate((2, 3)):
                    norm_dve(dve, step, "p1", t, hx2[:, i, :], modbcp[:, 1, :], modbcp[:, 0, :])
                    if i:
                        norm_take(dve, V.tensor_copy, "p1", t - 1, 1, i - 1)
                norm_take(dve, V.tensor_copy, "p1", 3, 1, 1)
                for j in range(4):
                    for i, t in enumerate((2, 3)):
                        bank = in_bank(dve, ("s1", t, j))
                        free_bank(V.tensor_copy(score[:, i, 2 * j:2 * j + 2, :],
                                                bank.rearrange("p (h n) -> p h n", h=2)), ("s1", t, j))
                    if j == 1:
                        taken(dve, ("s1", 2, 0))
                        first_rank_dve(4 * PH, 0)

            @block.tensor
            def _(pe):
                M, TR = nc.tensor.matmul, nc.tensor.transpose

                def accumulate(dst, pairs):
                    for i, (l, r) in enumerate(pairs):
                        last = M(dst, l, r, start=(i == 0), stop=(i == len(pairs) - 1))
                    return last

                for t in range(NTOK):
                    norm_pe(pe, "m1", t, hbuf1[:, t % 2, :])
                for t in range(NTOK):
                    for half in range(2):
                        taken(pe, ("ht", "m1", t, half))
                for t in range(NTOK):
                    for name, key, n in (("lkv", "w_kv1", KVL + ROPE), ("lq", "w_q_1", QL)):
                        if name == "lq" and t < 2:
                            continue
                        w = weights(pe, (key,))[:, 0:KT * n].rearrange("p (k n) -> p k n", k=KT)
                        bank = out_bank(pe, (name, t))
                        product.mark(accumulate(bank[:, 0:n], [(hT[:, k, tok(t)], w[:, k, :]) for k in range(KT)]),
                                     (name, t))
                for t in range(NTOK):
                    pe.wait_ge(lat_ready.sem, t + 1)
                    bank = out_bank(pe, ("ckvT", t))
                    for k in range(2):
                        TR(bank[:, k * P:(k + 1) * P], lat[:, t, QL + k * P:QL + (k + 1) * P], const(IDENT))
                    product.mark(TR(bank[0:ROPE, 256:384], lat[:, t, QL + KVL:QL + KVL + ROPE], const(IDENT)),
                                 ("ckvT", t))
                    if t >= 2:
                        bank = out_bank(pe, ("cqT", t))
                        for k in range(3):
                            last = TR(bank[:, k * P:(k + 1) * P], lat[:, t, k * P:(k + 1) * P], const(IDENT))
                        product.mark(last, ("cqT", t))
                for t in range(NTOK):
                    taken(pe, ("ckvT", t))
                for t in (2, 3):
                    taken(pe, ("cqT", t))
                w = weights(pe, ("w_uq_n",))[:, 0:3 * D].rearrange("p (k n) -> p k n", k=3)
                for h in range(HC):
                    bank = out_bank(pe, ("qn", h))
                    product.mark(accumulate(bank[:, 0:256], [(w[:, k, h * P:(h + 1) * P], cqT[:, k, :])
                                                             for k in range(3)]), ("qn", h))
                w = weights(pe, ("w_uq_r",))[:, 0:3 * 512].rearrange("p (k n) -> p k n", k=3)
                for t in (2, 3):
                    bank = out_bank(pe, ("qr", t))
                    product.mark(accumulate(bank, [(cqT[:, k, tok(t - 2)], w[:, k, :]) for k in range(3)]), ("qr", t))
                for t in (2, 3):
                    pe.wait_ge(qr_ready.sem, t - 1)
                    for g in range(2):
                        bank = out_bank(pe, ("qrT", t, g))
                        for j in range(4):
                            h = 4 * g + j
                            last = TR(bank[0:ROPE, j * P:(j + 1) * P], qrope[:, t - 2, h * ROPE:(h + 1) * ROPE],
                                      const(IDENT))
                        product.mark(last, ("qrT", t, g))
                w = weights(pe, ("w_ukv",)).rearrange("p (k n) -> p k n", k=2)
                for h in range(HC):
                    bank = out_bank(pe, ("kn", h))
                    product.mark(accumulate(bank, [(w[:, k, h * P:(h + 1) * P], ckvT[:, k, :]) for k in range(2)]),
                                 ("kn", h))
                for t in range(NTOK):
                    for c in range(2):
                        bank = out_bank(pe, ("v", t, c))
                        product.mark(accumulate(bank, [(ckvT[:, k, tok(t)], w[:, k, D + 512 * c:D + 512 * c + 512])
                                                       for k in range(2)]), ("v", t, c))
                for h in range(HC):
                    taken(pe, ("kn", h))
                    taken(pe, ("qn", h))
                for t in (2, 3):
                    for g in range(2):
                        taken(pe, ("qrT", t, g))
                for t in range(NTOK):
                    for c in range(2):
                        taken(pe, ("v", t, c))

                for u in range(UNITS + 3):
                    if u < UNITS:
                        h = u // 2
                        bank = out_bank(pe, ("sc", u))
                        product.mark(accumulate(bank, [(qnT[:, h, tok(u % 2)], knT[:, h, :]),
                                                       (qrT[0:ROPE, h, tok(u % 2)], krT[0:ROPE, :])]), ("sc", u))
                    if 0 <= u - 2 < UNITS:
                        v = u - 2
                        pe.wait_ge(prob_ready.sem, prob_ready.count(v))
                        bank = out_bank(pe, ("pT", v))
                        for k in range(4):
                            last = TR(bank[:, k * P:(k + 1) * P], prob[:, v % 3, k * P:(k + 1) * P], const(IDENT))
                        product.mark(last, ("pT", v))
                    if 0 <= u - 3 < UNITS:
                        v = u - 3
                        taken(pe, ("pT", v))
                        bank = out_bank(pe, ("oT", v))
                        product.mark(accumulate(bank[:, 0:P], [(vatt[:, k, (v // 2) * P:(v // 2 + 1) * P],
                                                                probT[:, v % 2, k * P:(k + 1) * P])
                                                               for k in range(4)]), ("oT", v))
                for u in range(UNITS):
                    taken(pe, ("oT", u))
                for i, t in enumerate((2, 3)):
                    for c in range(2):
                        w = weights(pe, ("w_out1", c)).rearrange("p (k n) -> p k n", k=KT)
                        bank = out_bank(pe, ("out1", t, c))
                        product.mark(accumulate(bank, [(oT[:, k, tok(i)], w[:, k, :]) for k in range(KT)]),
                                     ("out1", t, c))
                for i, t in enumerate((2, 3)):
                    norm_pe(pe, "p1", t, hx2[:, i, :])
                peer_scores_pe(pe, "1", (2, 3), bc_landed["keys1",])

        for part in (first_block, sums_and_mixer, second_block, last_sums):
            with nc.Block() as block:
                part(block)


def constants():
    r, c = np.mgrid[0:P, 0:P]
    mats = [r == c, r >= 0, r <= c, r > c, r >= c, r < c, r < 0]
    lower = [(r // s == c // s + 1) & (c // s % 2 == 0) for s in LEVELS]
    mats += lower + [m.T for m in lower]
    consts = np.concatenate([m.astype(np.float32) for m in mats], axis=1)
    iota = np.tile(np.arange(TOPK, dtype=np.float32), (P, 1))
    n = ROPE // 4
    freqs = (np.float32(10000.0) ** (-np.arange(n, dtype=np.float32) / np.float32(n))).astype(np.float32)
    t = np.arange(2 * P)
    ang = np.stack([(t // GRID_W).astype(np.float32)[:, None] * freqs, (t % GRID_W).astype(np.float32)[:, None] * freqs], 1)
    rope = np.stack([np.cos(ang), np.sin(ang)], 1).astype(np.float32)
    rope = rope.reshape(2, P, 2, 2, n).transpose(1, 0, 2, 3, 4)
    return consts, iota, np.ascontiguousarray(rope)


def kernel(**inputs):
    import concourse.bacc as bacc
    from concourse.bass_utils import run_bass_kernel_spmd

    a = {k: np.asarray(v) for k, v in inputs.items()}
    consts, iota, rope = constants()
    uq = a["od_w_uq"][0].reshape(QL, HC, NOPE + ROPE)
    ukv = a["od_w_ukv"][0].reshape(KVL, HC, NOPE + VD)
    keys = np.zeros((2, P, PH, 2, NKEY), np.float32)
    for p in range(2):
        keys[:, 64 * p:64 * p + 64, :, p, :] = a["p_keys"][:, :, p].transpose(0, 3, 1, 2)
    arrays = {
        "x": a["x"][0], "ctx": a["ctx"][0],
        "c_cols": np.stack([a["c_ctx"].reshape(KT, P), a["c"][0].reshape(KT, P)], 2).transpose(1, 0, 2).reshape(P, 2 * KT),
        "w_mod": a["w_mod"], "b_mod": a["b_mod"].reshape(2, 6, D),
        "norms": np.stack([a["norm1"], a["norm2"]], 1),
        "ev_w_in": a["ev_w_in"][0],
        "conv_w": np.concatenate([a["ev_a_conv"][0], a["ev_qkv_conv"][0]], 1).reshape(3, 16, P).transpose(2, 1, 0),
        "a_log": a["ev_a_log"].reshape(8), "dt_bias": a["ev_dt_bias"].reshape(8),
        "o_norm": a["ev_o_norm"][0], "ev_w_out": a["ev_w_out"][0],
        "od_w_in": a["od_w_in"][0], "q_norm": a["od_q_norm"][0], "kv_norm": a["od_kv_norm"][0],
        "uq_nope": uq[:, :, :NOPE].reshape(QL, -1), "uq_rope": uq[:, :, NOPE:].reshape(QL, -1),
        "ukv": np.concatenate([ukv[:, :, :NOPE].reshape(KVL, -1), ukv[:, :, NOPE:].reshape(KVL, -1)], 1),
        "od_w_out": a["od_w_out"][0], "p_w_q": a["p_w_q"], "keys": keys.reshape(2, P, PH, 2 * NKEY),
        "experts0": np.concatenate([a["p_u"][0], a["p_v"][0]], 1),
        "experts1": np.concatenate([a["p_u"][1], a["p_v"][1]], 1),
        "norm_f": a["norm_f"], "consts": consts, "iota16": iota, "rope": rope,
    }
    nc = bacc.Bacc("TRN2", target_bir_lowering=False, num_devices=1)
    feed, T = {}, {}
    for name, v in arrays.items():
        feed[f"in_{name}"] = np.ascontiguousarray(v)
        T[name] = nc.dram_tensor(f"in_{name}", v.shape, F32, kind="ExternalInput").ap()
    out = nc.dram_tensor("out", (2 * P, D), F32, kind="ExternalOutput").ap()
    build(nc, T, out)
    r = run_bass_kernel_spmd(nc, [feed], core_ids=[0])
    return r.results[0]["out"].reshape(1, 2 * P, D)
```
